# Optimizing a Trainium2 kernel written in Bass

```python
import jax, jax.numpy as jnp
from jax import lax
import numpy as np

D_MODEL = 1024
BATCH = 1
SEQ = 512
DEPTH = 4

N_MIXERS = 4
EPS = 1e-6

D_FF = 2816
FFN_CONV = 3

D_RNN = 1280
LRU_BLOCKS = 10
LRU_BLK = D_RNN // LRU_BLOCKS
LRU_CONV = 4
LRU_C = 8.0

D_INNER = 2 * D_MODEL
SSD_HEAD_DIM = 64
SSD_HEADS = D_INNER // SSD_HEAD_DIM
SSD_GROUPS = 4
SSD_HPG = SSD_HEADS // SSD_GROUPS
SSD_STATE = 128
SSD_CONV = 4
SSD_CHUNK = 128
SSD_GN = SSD_GROUPS * SSD_STATE
SSD_CONV_DIM = D_INNER + 2 * SSD_GN
SSD_IN = D_INNER + SSD_CONV_DIM + SSD_HEADS

SWA_HEAD_DIM = 64
SWA_Q_HEADS = D_MODEL // SWA_HEAD_DIM
SWA_KV_HEADS = 4
SWA_GQA = SWA_Q_HEADS // SWA_KV_HEADS
SWA_IN = (SWA_Q_HEADS + 2 * SWA_KV_HEADS) * SWA_HEAD_DIM
WINDOW = 128
SWA_BLOCK = 128
ROPE_THETA = 500000.0
ROT_DIM = SWA_HEAD_DIM // 4

HGRN_EXPAND = 128
HGRN_HEADS = D_MODEL // HGRN_EXPAND
HGRN_DK = HGRN_EXPAND
HGRN_DV = D_MODEL // HGRN_HEADS
HGRN_FD = HGRN_HEADS * HGRN_DK
HGRN_IN = 2 * HGRN_FD + 2 * D_MODEL
HGRN_CHUNK = 64

N_LRU = (DEPTH + 3) // 4
N_SSD = (DEPTH + 2) // 4
N_SWA = (DEPTH + 1) // 4
N_HGRN = DEPTH // 4

kernel_name = "hybrid_interleaved_rglru_ssd_swa_hgrn2"

def _rmsnorm(x, g):
    xf = x.astype(jnp.float32)
    y = xf * lax.rsqrt(jnp.mean(xf * xf, axis=-1, keepdims=True) + EPS)
    return (y * g.astype(jnp.float32)).astype(x.dtype)

def _causal_dwconv(x, w, b):
    k_w, ch = w.shape
    y = lax.conv_general_dilated(x, w.reshape(k_w, 1, ch).astype(x.dtype), window_strides=(1,),
                                 padding=[(k_w - 1, 0)], dimension_numbers=('NWC', 'WIO', 'NWC'),
                                 feature_group_count=ch)
    return y + b.astype(x.dtype)

def _linear_combine(left, right):
    a1, b1 = left
    a2, b2 = right
    return a1 * a2, a2 * b1 + b2

def _rg_lru_mixer(h, w_in, conv_w, conv_b, w_gate, b_gate, lam, w_out):
    bsz, s, _ = h.shape
    proj = h @ w_in
    gate_branch, xr = proj[..., :D_RNN], proj[..., D_RNN:]
    xc = _causal_dwconv(xr, conv_w, conv_b)
    xb = xc.reshape(bsz, s, LRU_BLOCKS, LRU_BLK)
    gates = (jnp.einsum('bsnc,nce->bsne', xb, w_gate) + b_gate).astype(jnp.float32)
    r = jax.nn.sigmoid(gates[..., :LRU_BLK]).reshape(bsz, s, D_RNN)
    i = jax.nn.sigmoid(gates[..., LRU_BLK:]).reshape(bsz, s, D_RNN)
    log_a = -LRU_C * r * jax.nn.softplus(-lam.astype(jnp.float32))
    a = jnp.exp(log_a)
    u = jnp.sqrt(-jnp.expm1(2.0 * log_a)) * (i * xc.astype(jnp.float32))
    _, hs = lax.associative_scan(_linear_combine, (a, u), axis=1)
    y = jax.nn.gelu(gate_branch.astype(jnp.float32)) * hs
    return y.astype(h.dtype) @ w_out

def _ssd_mixer(h, w_in, conv_w, conv_b, dt_bias, a_log, d_skip, norm_w, w_out):
    bsz, s, _ = h.shape
    nc, L, G, R, P, N = s // SSD_CHUNK, SSD_CHUNK, SSD_GROUPS, SSD_HPG, SSD_HEAD_DIM, SSD_STATE
    proj = h @ w_in
    z = proj[..., :D_INNER]
    xbc = proj[..., D_INNER:D_INNER + SSD_CONV_DIM]
    dt_raw = proj[..., D_INNER + SSD_CONV_DIM:]
    xbc = jax.nn.silu(_causal_dwconv(xbc, conv_w, conv_b)).astype(jnp.float32)
    xs = xbc[..., :D_INNER]
    bm = xbc[..., D_INNER:D_INNER + SSD_GN]
    cm = xbc[..., D_INNER + SSD_GN:]
    dt = jax.nn.softplus(dt_raw.astype(jnp.float32) + dt_bias.astype(jnp.float32))
    a = -jnp.exp(a_log.astype(jnp.float32)).reshape(G, R)
    x_c = xs.reshape(bsz, nc, L, G, R, P)
    dt_c = dt.reshape(bsz, nc, L, G, R)
    b_c = bm.reshape(bsz, nc, L, G, N)
    c_c = cm.reshape(bsz, nc, L, G, N)
    x_dt = x_c * dt_c[..., None]
    cs = jnp.cumsum(dt_c * a, axis=2)
    causal = jnp.tril(jnp.ones((L, L), dtype=bool))[None, None, :, :, None, None]
    seg = cs[:, :, :, None] - cs[:, :, None, :]
    decay = jnp.exp(jnp.where(causal, seg, -jnp.inf))
    cb = jnp.einsum('bclgn,bcsgn->bclsg', c_c, b_c)
    y_diag = jnp.einsum('bclsgr,bcsgrp->bclgrp', cb[..., None] * decay, x_dt)
    decay_to_end = jnp.exp(cs[:, :, -1:] - cs)
    states = jnp.einsum('bclgn,bclgr,bclgrp->bcgrpn', b_c, decay_to_end, x_dt)
    chunk_decay = jnp.exp(cs[:, :, -1])

    def step(carry, inp):
        st, dec = inp
        return carry * dec[..., None, None] + st, carry

    init = jnp.zeros((bsz, G, R, P, N), jnp.float32)
    _, prev = lax.scan(step, init, (jnp.moveaxis(states, 1, 0), jnp.moveaxis(chunk_decay, 1, 0)))
    prev = jnp.moveaxis(prev, 0, 1)
    y_off = jnp.einsum('bclgn,bcgrpn,bclgr->bclgrp', c_c, prev, jnp.exp(cs))
    y = (y_diag + y_off).reshape(bsz, s, SSD_HEADS, P) + xs.reshape(bsz, s, SSD_HEADS, P) * d_skip.astype(jnp.float32)[:, None]
    y = y.reshape(bsz, s, D_INNER) * jax.nn.silu(z.astype(jnp.float32))
    y = _rmsnorm(y.reshape(bsz, s, G, D_INNER // G), jnp.ones((), jnp.float32)).reshape(bsz, s, D_INNER) * norm_w.astype(jnp.float32)
    return y.astype(h.dtype) @ w_out

def _partial_rope(x, cos, sin):
    xf = x.astype(jnp.float32)
    half = ROT_DIM // 2
    x1, x2, rest = xf[..., :half], xf[..., half:ROT_DIM], xf[..., ROT_DIM:]
    c, s = cos[None, :, None, :], sin[None, :, None, :]
    return jnp.concatenate([x1 * c - x2 * s, x2 * c + x1 * s, rest], axis=-1)

def _swa_mixer(h, w_in, q_norm, k_norm, sinks, w_out, cos, sin):
    bsz, s, _ = h.shape
    nb, blk, hd = s // SWA_BLOCK, SWA_BLOCK, SWA_HEAD_DIM
    proj = h @ w_in
    nq, nkv = SWA_Q_HEADS * hd, SWA_KV_HEADS * hd
    q = proj[..., :nq].reshape(bsz, s, SWA_Q_HEADS, hd)
    k = proj[..., nq:nq + nkv].reshape(bsz, s, SWA_KV_HEADS, hd)
    v = proj[..., nq + nkv:].reshape(bsz, s, SWA_KV_HEADS, hd).astype(jnp.float32)
    q = _partial_rope(_rmsnorm(q, q_norm), cos, sin)
    k = _partial_rope(_rmsnorm(k, k_norm), cos, sin)
    qb = q.reshape(bsz, nb, blk, SWA_KV_HEADS, SWA_GQA, hd)
    pad = ((0, 0), (blk, 0), (0, 0), (0, 0))
    kp = jnp.pad(k, pad).reshape(bsz, nb + 1, blk, SWA_KV_HEADS, hd)
    vp = jnp.pad(v, pad).reshape(bsz, nb + 1, blk, SWA_KV_HEADS, hd)
    kw = jnp.concatenate([kp[:, :-1], kp[:, 1:]], axis=2)
    vw = jnp.concatenate([vp[:, :-1], vp[:, 1:]], axis=2)
    scores = jnp.einsum('bnqhgd,bnkhd->bnhgqk', qb, kw) * (hd ** -0.5)
    blk_idx = jnp.arange(nb)[:, None]
    qpos = blk_idx * blk + jnp.arange(blk)[None]
    kpos = blk_idx * blk - blk + jnp.arange(2 * blk)[None]
    diff = qpos[:, :, None] - kpos[:, None, :]
    mask = (diff >= 0) & (diff < WINDOW) & (kpos[:, None, :] >= 0)
    scores = jnp.where(mask[None, :, None, None], scores, -jnp.inf)
    sink = sinks.astype(jnp.float32).reshape(SWA_KV_HEADS, SWA_GQA)[None, None, :, :, None, None]
    m = jnp.maximum(jnp.max(scores, axis=-1, keepdims=True), sink)
    p = jnp.exp(scores - m)
    denom = jnp.sum(p, axis=-1, keepdims=True) + jnp.exp(sink - m)
    o = jnp.einsum('bnhgqk,bnkhd->bnqhgd', p / denom, vw).reshape(bsz, s, nq)
    return o.astype(h.dtype) @ w_out

def _hgrn2_mixer(h, w_in, norm_w, w_out, lb):
    bsz, s, _ = h.shape
    nc, L, H, DK, DV = s // HGRN_CHUNK, HGRN_CHUNK, HGRN_HEADS, HGRN_DK, HGRN_DV
    proj = h @ w_in
    q = proj[..., :HGRN_FD].astype(jnp.float32).reshape(bsz, s, H, DK) * (DK ** -0.5)
    f = lb.astype(jnp.float32) + (1.0 - lb.astype(jnp.float32)) * jax.nn.sigmoid(proj[..., HGRN_FD:2 * HGRN_FD].astype(jnp.float32))
    i = proj[..., 2 * HGRN_FD:2 * HGRN_FD + D_MODEL].astype(jnp.float32).reshape(bsz, s, H, DV)
    g_out = proj[..., 2 * HGRN_FD + D_MODEL:]
    log_f = jnp.log(f).reshape(bsz, s, H, DK)
    kk = (1.0 - f).reshape(bsz, s, H, DK)

    def chunks(t):
        return jnp.moveaxis(t.reshape(bsz, nc, L, H, t.shape[-1]), 1, 0)

    causal = jnp.tril(jnp.ones((L, L), dtype=bool))[None, :, :, None, None]

    def step(state, inp):
        qc, kc, vc, gc = inp
        cum = jnp.cumsum(gc, axis=1)
        decay = jnp.exp(jnp.where(causal, cum[:, :, None] - cum[:, None, :], -jnp.inf))
        attn = jnp.einsum('blhk,blshk,bshk->blsh', qc, decay, kc)
        o = jnp.einsum('blsh,bshv->blhv', attn, vc) + jnp.einsum('blhk,bhkv->blhv', qc * jnp.exp(cum), state)
        total = cum[:, -1]
        k_end = kc * jnp.exp(total[:, None] - cum)
        new_state = jnp.exp(total)[..., None] * state + jnp.einsum('bshk,bshv->bhkv', k_end, vc)
        return new_state, o

    state0 = jnp.zeros((bsz, H, DK, DV), jnp.float32)
    _, o = lax.scan(step, state0, (chunks(q), chunks(kk), chunks(i), chunks(log_f)))
    o = jnp.moveaxis(o, 0, 1).reshape(bsz, s, H, DV)
    o = _rmsnorm(o, norm_w).reshape(bsz, s, D_MODEL) * jax.nn.silu(g_out.astype(jnp.float32))
    return o.astype(h.dtype) @ w_out

def _conv_ffn(h, w_up, conv_w, conv_b, w_down):
    u = _causal_dwconv(h @ w_up, conv_w, conv_b)
    return (jax.nn.silu(u[..., D_FF:]) * u[..., :D_FF]) @ w_down

def setup_inputs(seed: int = 0) -> dict:
    key = jax.random.key(seed)
    ks = iter(jax.random.split(key, 64))
    f32 = jnp.float32
    out_scale = (2.0 * DEPTH) ** -0.5

    def nrm(shape, scale):
        return scale * jax.random.normal(next(ks), shape, f32)

    def gain(shape):
        return 1.0 + nrm(shape, 0.02)

    a_lru = jax.random.uniform(next(ks), (N_LRU, D_RNN), f32, 0.9, 0.999)
    dt0 = jnp.exp(jax.random.uniform(next(ks), (N_SSD, SSD_HEADS), f32, np.log(1e-3), np.log(1e-1)))
    return {
        "x": nrm((BATCH, SEQ, D_MODEL), 1.0),
        "mix_norm": gain((DEPTH, D_MODEL)),
        "ffn_norm": gain((DEPTH, D_MODEL)),
        "ffn_w_up": nrm((DEPTH, D_MODEL, 2 * D_FF), D_MODEL ** -0.5),
        "ffn_conv_w": nrm((DEPTH, FFN_CONV, 2 * D_FF), FFN_CONV ** -0.5),
        "ffn_conv_b": nrm((DEPTH, 2 * D_FF), 0.02),
        "ffn_w_down": nrm((DEPTH, D_FF, D_MODEL), D_FF ** -0.5 * out_scale),
        "lru_w_in": nrm((N_LRU, D_MODEL, 2 * D_RNN), D_MODEL ** -0.5),
        "lru_conv_w": nrm((N_LRU, LRU_CONV, D_RNN), LRU_CONV ** -0.5),
        "lru_conv_b": nrm((N_LRU, D_RNN), 0.02),
        "lru_w_gate": nrm((N_LRU, LRU_BLOCKS, LRU_BLK, 2 * LRU_BLK), LRU_BLK ** -0.5),
        "lru_b_gate": nrm((N_LRU, LRU_BLOCKS, 2 * LRU_BLK), 0.02),
        "lru_lambda": jnp.log(a_lru) - jnp.log1p(-a_lru),
        "lru_w_out": nrm((N_LRU, D_RNN, D_MODEL), D_RNN ** -0.5 * out_scale),
        "ssd_w_in": nrm((N_SSD, D_MODEL, SSD_IN), D_MODEL ** -0.5),
        "ssd_conv_w": nrm((N_SSD, SSD_CONV, SSD_CONV_DIM), SSD_CONV ** -0.5),
        "ssd_conv_b": nrm((N_SSD, SSD_CONV_DIM), 0.02),
        "ssd_dt_bias": dt0 + jnp.log(-jnp.expm1(-dt0)),
        "ssd_a_log": jnp.log(jax.random.uniform(next(ks), (N_SSD, SSD_HEADS), f32, 1.0, 16.0)),
        "ssd_d": gain((N_SSD, SSD_HEADS)),
        "ssd_norm": gain((N_SSD, D_INNER)),
        "ssd_w_out": nrm((N_SSD, D_INNER, D_MODEL), D_INNER ** -0.5 * out_scale),
        "swa_w_in": nrm((N_SWA, D_MODEL, SWA_IN), D_MODEL ** -0.5),
        "swa_q_norm": gain((N_SWA, SWA_HEAD_DIM)),
        "swa_k_norm": gain((N_SWA, SWA_HEAD_DIM)),
        "swa_sinks": nrm((N_SWA, SWA_Q_HEADS), 0.5),
        "swa_w_out": nrm((N_SWA, SWA_Q_HEADS * SWA_HEAD_DIM, D_MODEL), (SWA_Q_HEADS * SWA_HEAD_DIM) ** -0.5 * out_scale),
        "hgrn_w_in": nrm((N_HGRN, D_MODEL, HGRN_IN), D_MODEL ** -0.5),
        "hgrn_norm": gain((N_HGRN, HGRN_DV)),
        "hgrn_w_out": nrm((N_HGRN, D_MODEL, D_MODEL), D_MODEL ** -0.5 * out_scale),
        "hgrn_lower_bounds": nrm((DEPTH, HGRN_FD), 0.5),
    }

def reference(x, mix_norm, ffn_norm, ffn_w_up, ffn_conv_w, ffn_conv_b, ffn_w_down,
              lru_w_in, lru_conv_w, lru_conv_b, lru_w_gate, lru_b_gate, lru_lambda, lru_w_out,
              ssd_w_in, ssd_conv_w, ssd_conv_b, ssd_dt_bias, ssd_a_log, ssd_d, ssd_norm, ssd_w_out,
              swa_w_in, swa_q_norm, swa_k_norm, swa_sinks, swa_w_out,
              hgrn_w_in, hgrn_norm, hgrn_w_out, hgrn_lower_bounds):
    s = x.shape[1]
    inv_freq = ROPE_THETA ** (-jnp.arange(0, ROT_DIM, 2, dtype=jnp.float32) / ROT_DIM)
    ang = jnp.arange(s, dtype=jnp.float32)[:, None] * inv_freq[None]
    cos, sin = jnp.cos(ang), jnp.sin(ang)
    lbs = jnp.cumsum(jax.nn.softmax(hgrn_lower_bounds.astype(jnp.float32), axis=0), axis=0)
    lbs = lbs - lbs[0]
    for i in range(DEPTH):
        kind, j = i % N_MIXERS, i // N_MIXERS
        hn = _rmsnorm(x, mix_norm[i])
        if kind == 0:
            mix = _rg_lru_mixer(hn, lru_w_in[j], lru_conv_w[j], lru_conv_b[j], lru_w_gate[j],
                                lru_b_gate[j], lru_lambda[j], lru_w_out[j])
        elif kind == 1:
            mix = _ssd_mixer(hn, ssd_w_in[j], ssd_conv_w[j], ssd_conv_b[j], ssd_dt_bias[j],
                             ssd_a_log[j], ssd_d[j], ssd_norm[j], ssd_w_out[j])
        elif kind == 2:
            mix = _swa_mixer(hn, swa_w_in[j], swa_q_norm[j], swa_k_norm[j], swa_sinks[j],
                             swa_w_out[j], cos, sin)
        else:
            mix = _hgrn2_mixer(hn, hgrn_w_in[j], hgrn_norm[j], hgrn_w_out[j], lbs[i])
        x = x + mix.astype(x.dtype)
        x = x + _conv_ffn(_rmsnorm(x, ffn_norm[i]), ffn_w_up[i], ffn_conv_w[i], ffn_conv_b[i],
                          ffn_w_down[i]).astype(x.dtype)
    return x


_drawn_inputs = setup_inputs


def setup_inputs(seed=0):
    import zlib

    import numpy as np

    out = dict(_drawn_inputs(seed))
    spreads = {}
    factors = {'mix_norm': 3.966,
     'ffn_norm': 4.608,
     'ffn_conv_b': 4.69,
     'lru_conv_b': 4.953,
     'lru_b_gate': 8.0,
     'ssd_conv_b': 5.895,
     'ssd_d': 200.0,
     'ssd_norm': 7.842,
     'swa_q_norm': 8.0,
     'swa_k_norm': 8.0,
     'swa_sinks': 64.0,
     'hgrn_norm': 103.49}
    for name, (base, spread) in spreads.items():
        noise = np.random.default_rng([zlib.crc32(name.encode()), seed]).standard_normal(out[name].shape)
        drawn = base * np.exp(spread * noise) if base else spread * noise
        out[name] = __import__('jax').numpy.asarray(drawn.astype(out[name].dtype))
    for name, factor in factors.items():
        out[name] = (out[name] * factor).astype(out[name].dtype)
    return out
```

```python
from contextlib import ExitStack

import numpy as np

import concourse.bass as bass
from concourse import mybir

ALU = mybir.AluOpType
ACT = mybir.ActivationFunctionType
AX = mybir.AxisListType
F32 = mybir.dt.float32
BF16 = mybir.dt.bfloat16
I32 = mybir.dt.int32

P = 128
S = 512
D = 1024
DT = D // P
DEPTH = 4
EPS = 1e-6

FF_T = 2816 // P
LRU_T = 1280 // P
LRU_C = 8.0
SSD_T = 2048 // P
SSD_G = 4
SSD_TG = SSD_T // SSD_G
SSD_R = 8
NC = S // P
SWA_Q = 16
HG_H = 8

RING = 4
PANEL = 2304

JOBS = [("lru_in", LRU_T, 8 * 256 + 256), ("lru_out", DT, LRU_T * P)]
JOBS += [("up0", FF_T, 8 * 256), ("down0", 2 * DT, FF_T // 2 * P)]
JOBS += [("ssd_in", 1 + 5 * SSD_G, 8 * 256), ("ssd_out", DT, SSD_T * P)]
JOBS += [("up1", FF_T, 8 * 256), ("down1", 2 * DT, FF_T // 2 * P)]
JOBS += [("swa_in", 6, 8 * 256), ("swa_out", DT, 8 * P)]
JOBS += [("up2", FF_T, 8 * 256), ("down2", 2 * DT, FF_T // 2 * P)]
JOBS += [("hgrn_in", 2 * HG_H, 8 * 256), ("hgrn_out", DT, 8 * P)]
JOBS += [("up3", FF_T, 8 * 256), ("down3", 2 * DT, FF_T // 2 * P)]

PARAMS = {}


def _columns():
    at = 0
    for name, n in [("eps", 1), ("mix_norm", DEPTH * DT), ("ffn_norm", DEPTH * DT),
                    ("ffn_conv_w", DEPTH * 3 * 2 * FF_T), ("ffn_conv_b", DEPTH * 2 * FF_T),
                    ("lru_conv_w", 4 * LRU_T), ("lru_conv_b", LRU_T), ("lru_b_gate", 2 * LRU_T),
                    ("lru_lambda", LRU_T),
                    ("ssd_conv_w", 4 * 24), ("ssd_conv_b", 24), ("ssd_dt_bias", 1), ("ssd_a_log", 1),
                    ("ssd_d", SSD_T), ("ssd_norm", SSD_T),
                    ("swa_q_norm", 1), ("swa_k_norm", 1), ("swa_sinks", SWA_Q),
                    ("hgrn_norm", 1), ("hgrn_lower_bounds", DEPTH * HG_H)]:
        PARAMS[name] = (at, n)
        at += n
    return at


NPARAM = _columns()

CONSTS = {}


def _constants():
    at = 0
    for name, n in [("ones", P), ("ident", P)]:
        CONSTS[name] = (at, n)
        at += n
    return at


NCONST = _constants()
LEVELS = [1, 2, 4, 8, 16, 32, 64]


def steps(eng, lo, hi, unroll):
    full = (hi - lo) // unroll
    if full > 1:
        with eng.Fori(0, full) as i:
            for u in range(unroll):
                yield i * unroll + (lo + u), (lo + u) % unroll
    else:
        full = 0
    for j in range(lo + full * unroll, hi):
        yield j, j % unroll


class Core:

    def __init__(self, nc, ctx, dram, layers):
        self.nc, self.dram = nc, dram
        self._ctx = ctx
        sb = self.sb
        self.x = sb("x_resid", [P, DT, S])
        self.xh = sb("x_hi", [P, DT, S], BF16)
        self.xl = sb("x_lo", [P, DT, S], BF16)
        self.gh = sb("g_hi", [P, FF_T, S], BF16)
        self.gl = sb("g_lo", [P, FF_T, S], BF16)
        self.w = sb("w_panel", [P, RING, PANEL])
        self.wl = sb("w_lo", [P, RING, PANEL], BF16)
        self.rstd = sb("rstd", [P, S])
        self.rms = sb("rms", [P, S])
        self.sq = sb("x_sq", [P, 2, S])
        self.sqsum = sb("x_sqsum", [P, S])
        self.par = sb("params", [P, NPARAM])
        self.con = sb("consts", [P, NCONST])
        self.arena = sb("arena", [P, 15850])
        self.ps = ctx.enter_context(nc.psum_tensor("psum", [P, 8, S], F32))
        self._sems = {}
        self.panel0, self.pair0, self.count, p, n = {}, {}, {}, 0, 0
        for name, count, _ in JOBS:
            if name not in layers:
                continue
            self.panel0[name], self.pair0[name] = p, n
            self.count[name] = count
            p += count
            n += count if not name.startswith("down") else count // 2

    def sb(self, name, shape, dt=F32):
        return self._ctx.enter_context(self.nc.sbuf_tensor(name, shape, dt))

    def s(self, name):
        if name not in self._sems:
            self._sems[name] = self._ctx.enter_context(self.nc.semaphore(name))
        return self._sems[name]

    def p(self, name, i=0):
        a, n = PARAMS[name]
        assert i < n if isinstance(i, int) else True
        return self.par[:, bass.ds(i + a, 1)]

    def c(self, name, lo=0, hi=None):
        a, n = CONSTS[name]
        return self.con[:, a + lo:a + (n if hi is None else hi)]

    def whi(self, slot, words=PANEL):
        v = self.w[:, slot, 0:words].bitcast(BF16)
        return v.rearrange("p (n two) -> p n two", two=2)[:, :, 1]

    def slot(self, job, u):
        return (self.panel0[job] + u) % RING

    def bank(self, job, u):
        return 2 * ((self.pair0[job] + u) % 2)



def weights_sync(sp, k, job, words):
    p0, n = k.panel0[job], k.count[job]
    lo = 0
    if p0 == 0:
        for j in range(RING):
            sp.dma_start(k.w[:, j, 0:words], k.dram[job][j]).then_inc(k.s(f"panel_landed{j}"), 16)
        lo = RING
    for j, u in steps(sp, lo, n, RING):
        slot = k.slot(job, u)
        sp.wait_ge(k.s("panel_used"), j + (p0 - RING + 1))
        sp.dma_start(k.w[:, slot, 0:words],
                     k.dram[job][bass.ds(j, 1), :, :].rearrange("a p w -> p (a w)")
                     ).then_inc(k.s(f"panel_landed{slot}"), 16)


def weights_gpsimd(pool, k, job, words):
    p0, n = k.panel0[job], k.count[job]
    for j, u in steps(pool, 0, n, RING):
        slot = k.slot(job, u)
        pool.wait_ge(k.s(f"panel_landed{slot}"), (j + (p0 - slot)) * (16 // RING) + 16)
        pool.tensor_tensor(k.wl[:, slot, 0:words], k.w[:, slot, 0:words], k.whi(slot, words),
                           ALU.subtract).then_inc(k.s("panel_split"), 1)


def product(pe, out, wh, wl, ah, al, start, stop):
    pe.matmul(out, wh, ah, start=start, stop=False)
    pe.matmul(out, wh, al, start=False, stop=False)
    return pe.matmul(out, wl, ah, start=False, stop=stop)


def gemm_tile(pe, k, bank, slot, kt, nb, col, hi, lo, k0=0, start=True, stop=True, m=P):
    wh, wl = k.whi(slot), k.wl[:, slot, :]
    for q in range(kt):
        a = q * nb + col
        last = product(pe, k.ps[0:m, bank, :], wh[:, a:a + m], wl[:, a:a + m],
                       hi[:, k0 + q, :], lo[:, k0 + q, :], start and q == 0, stop and q == kt - 1)
    return last



def gain(k, c, o):
    return k.p("ffn_norm" if c % 2 else "mix_norm", o + DT * (c // 2))


def out_tensor(pe, k, job, kt, parts, ready, count):
    pe.wait_ge(k.s(ready), count)
    p0, n0 = k.panel0[job], k.pair0[job]
    unroll = RING // parts
    for o, u in steps(pe, 0, DT, unroll):
        bank = k.bank(job, u)
        pe.wait_ge(k.s("banks_free"), o * 2 + (2 * n0 + 2))
        for h in range(parts):
            slot = k.slot(job, u * parts + h)
            pe.wait_ge(k.s("panel_split"), o * parts + (p0 + h + 1))
            gemm_tile(pe, k, bank, slot, kt, P, 0, k.gh, k.gl, h * kt, h == 0, h == parts - 1
                      ).then_inc(k.s("panel_used"), 1)


def residual_scalar(act, k, c, job):
    for o, u in steps(act, 0, DT, 2) if job is not None else ((o, o % 2) for o in range(DT)):
        if job is not None:
            act.wait_ge(k.s("banks_free"), o * 2 + (4 + 2 * k.pair0[job] + 2))
        elif o >= 2:
            act.wait_ge(k.s("sq_summed"), o)
        act.activation(k.sq[:, u % 2, :], tile(k.x, o), ACT.Square).then_inc(k.s("x_squared"), 1)
        act.activation(tile(k.xh, o), tile(k.x, o), ACT.Identity, scale=gain(k, c, o)
                       ).then_inc(k.s("x_hi"), 1)


def norm_scalar(act, k, c):
    act.wait_ge(k.s("norm_summed"), c + 1)
    act.activation(k.rms[:, :], k.ps[:, 4, :], ACT.Sqrt, bias=k.p("eps"), scale=1.0 / D
                   ).then_inc(k.s("rms_ready"), 1)


def residual_vector(dve, k, c, job, parts=1):
    if c is not None:
        dve.memset(k.sqsum[:, :], 0.0).then_inc(k.s("sq_summed"), 1)
    for o, u in steps(dve, 0, DT, 2):
        if job is not None:
            bank = k.bank(job, u)
            dve.wait_ge(k.s("panel_used"), o * parts + (k.panel0[job] + parts))
            dve.tensor_tensor(tile(k.x, o), tile(k.x, o), k.ps[:, bank, :], ALU.add
                              ).then_inc(k.s("banks_free"), 2)
        if c is None:
            continue
        dve.wait_ge(k.s("x_squared"), o + (DT * c + 1))
        dve.wait_ge(k.s("sq_summed"), o + ((DT + 1) * c + 1))
        dve.tensor_tensor(k.sqsum[:, :], k.sqsum[:, :], k.sq[:, u % 2, :], ALU.add
                          ).then_inc(k.s("sq_summed"), 1)
        dve.wait_ge(k.s("x_hi"), o + (DT * c + 1))
        if job is not None:
            dve.wait_ge(k.s("banks_free"), o * 2 + (4 + 2 * k.pair0[job] + 2))
        dve.scalar_tensor_tensor(tile(k.xl, o), tile(k.x, o), gain(k, c, o), tile(k.xh, o),
                                 ALU.mult, ALU.subtract).then_inc(k.s("x_split"), 1)


def norm_vector(dve, k, c):
    dve.wait_ge(k.s("rms_ready"), c + 1)
    dve.reciprocal(k.rstd[:, :], k.rms[:, :]).then_inc(k.s("rstd_ready"), 1)
    dve.wait_ge(k.s("rstd_ready"), c + 1)


def norm_tensor(pe, k, c):
    pe.wait_ge(k.s("sq_summed"), (DT + 1) * (c + 1))
    pe.matmul(k.ps[:, 4, :], k.c("ones"), k.sqsum[:, :], start=True, stop=True
              ).then_inc(k.s("norm_summed"), 1)
    pe.wait_ge(k.s("x_split"), DT * (c + 1))


def tile(t, o):
    return t[:, bass.ds(o, 1), :].rearrange("p a s -> p (a s)")



class FfnBuffers:
    def __init__(self, k):
        a = Arena(k)
        self.raw = a.take(2, 2, S + 2)
        self.conv = a.take(2, 2, S)


class Chain:

    def __init__(self, eng, k, name):
        self.eng, self.k, self.name, self.n = eng, k, name, 0

    def __call__(self, ins):
        self.n += 1
        ins.then_inc(self.k.s(self.name), 1)
        self.eng.wait_ge(self.k.s(self.name), self.n)


class Arena:
    def __init__(self, k, at=0):
        self.k, self.at = k, at

    def take(self, *shape, dt=F32):
        n = int(np.prod(shape))
        words = n if dt != BF16 else (n + 1) // 2
        v = self.k.arena[:, self.at:self.at + words]
        self.at += words
        assert self.at <= self.k.arena.shape[1], self.at
        if dt != F32:
            v = v.bitcast(dt)
        if len(shape) == 1:
            return v
        names = "abcd"[:len(shape)]
        return v.rearrange("p (%s) -> p %s" % (" ".join(names), " ".join(names)),
                           **{n: s for n, s in zip(names, shape)})


def up_tensor(pe, k, l):
    job = f"up{l}"
    p0, n0 = k.panel0[job], k.pair0[job]
    for j, u in steps(pe, 0, FF_T, RING):
        slot, bank = k.slot(job, u), k.bank(job, u)
        pe.wait_ge(k.s("panel_split"), j + (p0 + 1))
        pe.wait_ge(k.s("banks_free"), j * 2 + (2 * n0 + 2))
        gemm_tile(pe, k, bank, slot, DT, 256, 0, k.xh, k.xl)
        gemm_tile(pe, k, bank + 1, slot, DT, 256, P, k.xh, k.xl).then_inc(k.s("panel_used"), 1)


def up_scalar(act, k, l):
    b = FfnBuffers(k)
    n0 = k.pair0[f"up{l}"]
    for j, u in steps(act, 0, FF_T, 2):
        for half in (1, 0):
            act.wait_ge(k.s("banks_free"), j * 2 + (4 + 2 * n0 + 2 - half))
            act.activation(b.conv[:, u, half, :], b.raw[:, u, half, 2:], ACT.Identity,
                           bias=k.p("ffn_conv_b", j + (l * 2 * FF_T + half * FF_T)),
                           scale=k.p("ffn_conv_w", j + ((l * 3 + 2) * 2 * FF_T + half * FF_T))
                           ).then_inc(k.s("ffn_biased"), 1)
        act.wait_ge(k.s("ffn_tapped"), j * 4 + (4 * FF_T * l + 3))
        act.activation(b.conv[:, u, 1, :], b.conv[:, u, 1, :], ACT.Silu).then_inc(k.s("ffn_silu"), 1)
        act.wait_ge(k.s("ffn_gated"), j + (FF_T * l + 1))
        act.activation(tile(k.gh, j), b.conv[:, u, 0, :], ACT.Copy).then_inc(k.s("ffn_hi"), 1)


def up_vector(dve, k, l):
    b = FfnBuffers(k)
    job = f"up{l}"
    p0 = k.panel0[job]
    dve.memset(b.raw[:, :, :, 0:2], 0.0).then_inc(k.s("ffn_padded"), 1)
    dve.wait_ge(k.s("ffn_padded"), l + 1)
    norm_vector(dve, k, 2 * l + 1)
    for j, u in steps(dve, 0, FF_T, 2):
        bank = k.bank(job, u)
        dve.wait_ge(k.s("panel_used"), j + (p0 + 1))
        for half in (1, 0):
            dve.tensor_tensor(b.raw[:, u, half, 2:], k.ps[:, bank + half, :], k.rstd[:, :], ALU.mult
                              ).then_inc(k.s("banks_free"), 1)
        for tap in (1, 0):
            for half in (1, 0):
                if tap == 1:
                    dve.wait_ge(k.s("ffn_biased"), j * 2 + (2 * FF_T * l + 2 - half))
                else:
                    dve.wait_ge(k.s("ffn_tapped"), j * 4 + (4 * FF_T * l + 2 - half))
                dve.scalar_tensor_tensor(
                    b.conv[:, u, half, :], b.raw[:, u, half, tap:tap + S],
                    k.p("ffn_conv_w", j + ((l * 3 + tap) * 2 * FF_T + half * FF_T)),
                    b.conv[:, u, half, :], ALU.mult, ALU.add).then_inc(k.s("ffn_tapped"), 1)
        dve.wait_ge(k.s("ffn_tapped"), j * 4 + (4 * FF_T * l + 4))
        dve.wait_ge(k.s("ffn_silu"), j + (FF_T * l + 1))
        dve.tensor_tensor(b.conv[:, u, 0, :], b.conv[:, u, 0, :], b.conv[:, u, 1, :], ALU.mult
                          ).then_inc(k.s("ffn_gated"), 1)
        dve.wait_ge(k.s("ffn_hi"), j + (FF_T * l + 1))
        dve.tensor_tensor(tile(k.gl, j), b.conv[:, u, 0, :], tile(k.gh, j), ALU.subtract
                          ).then_inc(k.s("g_split"), 1)



def softplus_scalar(act, k, name, n_abs, e):
    act.wait_ge(k.s(name), 2)
    act.activation(e, n_abs, ACT.Exp, scale=-1.0).then_inc(k.s(name + "_exp"), 1)


def softplus_vector(dve, k, name, x, size, e, z, out):
    chained = Chain(dve, k, name)
    chained(dve.tensor_scalar(out, x, 0.0, None, ALU.max))
    chained(dve.scalar_tensor_tensor(size, x, -1.0, x, ALU.mult, ALU.max))
    dve.wait_ge(k.s(name + "_exp"), 1)
    chained(dve.tensor_scalar(z, e, 2.0, None, ALU.add))
    chained(dve.reciprocal(z, z))
    chained(dve.tensor_tensor(z, e, z, ALU.mult))
    chained(dve.tensor_tensor(e, z, z, ALU.mult))
    chained(dve.tensor_scalar(size, e, 1.0 / 17, None, ALU.mult))
    for odd in (15, 13, 11, 9, 7, 5, 3):
        chained(dve.scalar_tensor_tensor(size, size, 1.0 / odd, e, ALU.add, ALU.mult))
    chained(dve.scalar_tensor_tensor(size, size, 1.0, z, ALU.add, ALU.mult))
    chained(dve.scalar_tensor_tensor(out, size, 2.0, out, ALU.mult, ALU.add))



class LruBuffers:
    def __init__(self, k):
        a = Arena(k)
        self.gate = a.take(2, S)
        self.inner = a.take(2, S)
        self.raw = a.take(2, S + 3)
        self.conv = a.take(2, S)
        self.conv_hi = a.take(2, S, dt=BF16)
        self.conv_lo = a.take(2, S, dt=BF16)
        self.tanh_r, self.tanh_i, self.a, self.th, self.s, self.wu, self.h = (a.take(S) for _ in range(7))
        self.half_rate = a.take(LRU_T)
        self.neg_half_rate = a.take(LRU_T)
        self.half_bias = a.take(2 * LRU_T)
        self.nlam, self.t0, self.t1, self.t2, self.t3 = (a.take(LRU_T) for _ in range(5))


GELU_A = float(np.sqrt(2.0 / np.pi))
GELU_B = GELU_A * 0.044715


def lru_tensor(pe, k):
    b = LruBuffers(k)
    job, T = "lru_in", LRU_T
    p0, n0 = k.panel0[job], k.pair0[job]

    def project(j, u):
        slot, bank = k.slot(job, u), k.bank(job, u)
        pe.wait_ge(k.s("panel_split"), j + (p0 + 1))
        pe.wait_ge(k.s("banks_free"), j * 2 + (2 * n0 + 2))
        gemm_tile(pe, k, bank, slot, DT, 256, 0, k.xh, k.xl)
        gemm_tile(pe, k, bank + 1, slot, DT, 256, P, k.xh, k.xl).then_inc(k.s("lru_projected"), 1)

    def gates(j, u, first):
        slot = k.slot(job, u)
        pe.wait_ge(k.s("lru_conv_split"), j + 1)
        if not first:
            pe.wait_ge(k.s("lru_gates_read"), j * 2)
        for half in range(2):
            a = DT * 256 + half * P
            product(pe, k.ps[:, 5 + half, :], k.whi(slot)[:, a:a + P], k.wl[:, slot, a:a + P],
                    b.conv_hi[:, u % 2, :], b.conv_lo[:, u % 2, :], True, True
                    ).then_inc(k.s("panel_used" if half else "lru_r_done"), 1)

    project(0, 0)
    project(1, 1)
    gates(0, 0, True)
    for j, u in steps(pe, 2, T, RING):
        project(j, u)
        gates(j - 1, (u - 1) % RING, False)
    gates(T - 1, (T - 1) % RING, False)


def lru_scalar(act, k):
    b = LruBuffers(k)
    n0, p0 = k.pair0["lru_in"], k.panel0["lru_in"]
    softplus_scalar(act, k, "lru_softplus", b.t0, b.t1)

    def conv_and_gelu(j, u):
        act.wait_ge(k.s("banks_free"), j * 2 + (4 + 2 * n0 + 1))
        act.activation(b.inner[:, u, :], b.gate[:, u, :], ACT.Square).then_inc(k.s("lru_gate_sq"), 1)
        act.wait_ge(k.s("banks_free"), j * 2 + (4 + 2 * n0 + 2))
        act.activation(b.conv[:, u, :], b.raw[:, u, 3:], ACT.Identity, bias=k.p("lru_conv_b", j),
                       scale=k.p("lru_conv_w", j + 3 * LRU_T)).then_inc(k.s("lru_biased"), 1)
        act.wait_ge(k.s("lru_inner"), j * 2 + 2)
        act.activation(b.inner[:, u, :], b.inner[:, u, :], ACT.Tanh).then_inc(k.s("lru_gate_tanh"), 1)
        act.wait_ge(k.s("lru_tapped"), j * 3 + 3)
        act.activation(b.conv_hi[:, u, :], b.conv[:, u, :], ACT.Copy).then_inc(k.s("lru_conv_hi"), 1)

    def recurrence(j, u):
        act.wait_ge(k.s("lru_r_done"), j + 1)
        act.activation(b.tanh_r, k.ps[:, 5, :], ACT.Tanh, bias=b.half_bias[:, bass.ds(j, 1)], scale=0.5
                       ).then_inc(k.s("lru_gates_read"), 1)
        act.wait_ge(k.s("panel_used"), j + (p0 + 1))
        act.activation(b.tanh_i, k.ps[:, 6, :], ACT.Tanh, bias=b.half_bias[:, bass.ds(j + LRU_T, 1)],
                       scale=0.5).then_inc(k.s("lru_gates_read"), 1)
        act.wait_ge(k.s("lru_gates_read"), j * 2 + 1)
        rate, neg = b.half_rate[:, bass.ds(j, 1)], b.neg_half_rate[:, bass.ds(j, 1)]
        act.activation(b.a, b.tanh_r, ACT.Exp, bias=rate, scale=rate).then_inc(k.s("lru_decay"), 1)
        act.activation(b.th, b.tanh_r, ACT.Tanh, bias=neg, scale=neg).then_inc(k.s("lru_decay"), 1)
        act.wait_ge(k.s("lru_s"), j * 2 + 2)
        act.activation(b.s, b.s, ACT.Sqrt).then_inc(k.s("lru_root"), 1)
        act.wait_ge(k.s("lru_y"), j * 3 + 3)
        act.activation(tile(k.gh, j), b.h, ACT.Copy).then_inc(k.s("lru_y_hi"), 1)

    act.wait_ge(k.s("lru_constants"), 3)
    conv_and_gelu(0, 0)
    for j, u in steps(act, 1, LRU_T, 2):
        conv_and_gelu(j, u)
        recurrence(j - 1, 1 - u)
    recurrence(LRU_T - 1, (LRU_T - 1) % 2)


def lru_vector(dve, k):
    b = LruBuffers(k)
    job = "lru_in"
    dve.tensor_scalar(b.nlam, k.par[:, PARAMS["lru_lambda"][0]:PARAMS["lru_lambda"][0] + LRU_T], -1.0, None,
                      ALU.mult).then_inc(k.s("lru_nlam"), 1)
    dve.wait_ge(k.s("lru_nlam"), 1)
    softplus_vector(dve, k, "lru_softplus", b.nlam, b.t0, b.t1, b.t2, b.t3)
    dve.tensor_scalar(b.half_rate, b.t3, -LRU_C / 2, None, ALU.mult).then_inc(k.s("lru_constants"), 1)
    dve.tensor_scalar(b.neg_half_rate, b.t3, LRU_C / 2, None, ALU.mult).then_inc(k.s("lru_constants"), 1)
    bias0 = PARAMS["lru_b_gate"][0]
    dve.tensor_scalar(b.half_bias, k.par[:, bias0:bias0 + 2 * LRU_T], 0.5, None, ALU.mult
                      ).then_inc(k.s("lru_constants"), 1)
    dve.memset(b.raw[:, :, 0:3], 0.0).then_inc(k.s("lru_padded"), 1)
    dve.wait_ge(k.s("lru_padded"), 1)
    norm_vector(dve, k, 0)

    def conv_and_gelu(j, u):
        bank = k.bank(job, u)
        dve.wait_ge(k.s("lru_projected"), j + 1)
        dve.tensor_tensor(b.gate[:, u, :], k.ps[:, bank, :], k.rstd[:, :], ALU.mult
                          ).then_inc(k.s("banks_free"), 1)
        dve.tensor_tensor(b.raw[:, u, 3:], k.ps[:, bank + 1, :], k.rstd[:, :], ALU.mult
                          ).then_inc(k.s("banks_free"), 1)
        dve.wait_ge(k.s("lru_gate_sq"), j + 1)
        dve.tensor_scalar(b.inner[:, u, :], b.inner[:, u, :], GELU_B, GELU_A, ALU.mult, ALU.add
                          ).then_inc(k.s("lru_inner"), 1)
        dve.wait_ge(k.s("lru_inner"), j * 2 + 1)
        dve.tensor_tensor(b.inner[:, u, :], b.inner[:, u, :], b.gate[:, u, :], ALU.mult
                          ).then_inc(k.s("lru_inner"), 1)
        dve.wait_ge(k.s("lru_biased"), j + 1)
        for n, tap in enumerate((2, 1, 0)):
            if n:
                dve.wait_ge(k.s("lru_tapped"), j * 3 + n)
            dve.scalar_tensor_tensor(b.conv[:, u, :], b.raw[:, u, tap:tap + S],
                                     k.p("lru_conv_w", j + tap * LRU_T), b.conv[:, u, :],
                                     ALU.mult, ALU.add).then_inc(k.s("lru_tapped"), 1)
        dve.wait_ge(k.s("lru_gate_tanh"), j + 1)
        dve.scalar_tensor_tensor(b.gate[:, u, :], b.inner[:, u, :], 1.0, b.gate[:, u, :], ALU.add, ALU.mult
                                 ).then_inc(k.s("lru_gelu"), 1)
        dve.wait_ge(k.s("lru_tapped"), j * 3 + 3)
        dve.wait_ge(k.s("lru_conv_hi"), j + 1)
        dve.tensor_tensor(b.conv_lo[:, u, :], b.conv[:, u, :], b.conv_hi[:, u, :], ALU.subtract
                          ).then_inc(k.s("lru_conv_split"), 1)

    def recurrence(j, u):
        dve.wait_ge(k.s("lru_decay"), j * 2 + 1)
        dve.tensor_tensor(b.s, b.a, b.a, ALU.mult).then_inc(k.s("lru_s"), 1)
        dve.wait_ge(k.s("lru_decay"), j * 2 + 2)
        dve.wait_ge(k.s("lru_s"), j * 2 + 1)
        dve.scalar_tensor_tensor(b.s, b.s, 1.0, b.th, ALU.add, ALU.mult).then_inc(k.s("lru_s"), 1)
        dve.scalar_tensor_tensor(b.wu, b.tanh_i, 1.0, b.conv[:, u, :], ALU.add, ALU.mult
                                 ).then_inc(k.s("lru_gated"), 1)
        dve.wait_ge(k.s("lru_gated"), j + 1)
        dve.wait_ge(k.s("lru_root"), j + 1)
        dve.scalar_tensor_tensor(b.wu, b.wu, 0.5, b.s, ALU.mult, ALU.mult).then_inc(k.s("lru_y"), 1)
        dve.wait_ge(k.s("lru_y"), j * 3 + 1)
        dve.tensor_tensor_scan(b.h, b.a, b.wu, 0.0, ALU.mult, ALU.add).then_inc(k.s("lru_y"), 1)
        dve.wait_ge(k.s("lru_y"), j * 3 + 2)
        dve.wait_ge(k.s("lru_gelu"), j + 1)
        dve.scalar_tensor_tensor(b.h, b.gate[:, u, :], 0.5, b.h, ALU.mult, ALU.mult
                                 ).then_inc(k.s("lru_y"), 1)
        dve.wait_ge(k.s("lru_y"), j * 3 + 3)
        dve.wait_ge(k.s("lru_y_hi"), j + 1)
        dve.tensor_tensor(tile(k.gl, j), b.h, tile(k.gh, j), ALU.subtract
                          ).then_inc(k.s("lru_y_split"), 1)

    conv_and_gelu(0, 0)
    for j, u in steps(dve, 1, LRU_T, 2):
        conv_and_gelu(j, u)
        recurrence(j - 1, 1 - u)
    recurrence(LRU_T - 1, (LRU_T - 1) % 2)



SSD_DT = 32
SSD_ROWS = 3 * SSD_DT


class SsdBuffers:
    def __init__(self, k):
        a = Arena(k)
        self.x = a.take(2, SSD_TG, S)
        self.bc = a.take(2, 2, S)
        self.z = a.take(SSD_TG, S)
        self.xdt = a.take(NC, S)
        self.xw = a.take(2, S)
        self.raw = a.take(2, S + 3)
        self.prev = a.take(NC - 1, S)
        self.cs_t, self.dt_t, self.end_w, self.dec = (a.take(NC, SSD_DT) for _ in range(4))
        self.pick = a.take(SSD_R, P, dt=BF16)
        self.cs3 = a.take(S, dt=BF16)
        self.ident, self.mask = a.take(P, dt=BF16), a.take(P, dt=BF16)
        self.table = a.take(P + P + SSD_DT)
        self.last_row, self.mask32 = self.table[:, 0:P], self.table[:, P:2 * P]
        self.pick32 = self.table[:, 2 * P:2 * P + SSD_DT]
        t = Arena(k, SSD_TG * S)
        self.dtx, self.size, self.e, self.q = (t.take(S) for _ in range(4))
        t = Arena(k, 2 * SSD_TG * S + 2 * S)
        self.dt, self.start = t.take(S), t.take(S)
        gh = k.gh[:, SSD_T:, :].bitcast(F32).rearrange("p a s -> p (a s)")
        gl = k.gl[:, SSD_T:, :].bitcast(F32).rearrange("p a s -> p (a s)")
        self.m = gh[:, 0:2 * S].rearrange("p (a s) -> p a s", a=2)
        self.cb = gh[:, 2 * S:3 * S]
        self.ecs = gl[:, 0:384]
        self.cdec = gl[:, 384:384 * 3].rearrange("p (a s) -> p a s", a=2)
        self.ncs3 = gl[:, 1152:1408].bitcast(BF16)
        self.pick3 = gl[:, 1408:1408 + SSD_DT // 2].bitcast(BF16)
        self.ea = gl[0:SSD_ROWS, 1424:1425]


def heads_of(t, c, g):
    return t[:, c, SSD_R * g:SSD_R * (g + 1)].unsqueeze(2).to_broadcast([P, SSD_R, 64])


def by_head(t):
    return t.rearrange("p (h d) -> p h d", d=64)


def ssd_events():
    ev = [("dt", 0, 0)]
    for g in range(SSD_G):
        for i in range(5):
            for half in range(2):
                two = (2 * i + half) * 2
                work = g > 0 and two < SSD_R
                if work:
                    ev += [("seg", g - 1, two), ("seg", g - 1, two + 1)]
                ev.append(("tile", g, 2 * i + half))
                if work:
                    ev += [("out", g - 1, two), ("out", g - 1, two + 1)]
            if i == 2 and g > 0:
                ev.append(("norm", g - 1, 0))
            if i == 3:
                ev.append(("turn", g, 0))
        ev.append(("states", g, 0))
    g = SSD_G - 1
    ev += [("seg", g, 0)]
    for r in range(SSD_R):
        if r + 1 < SSD_R:
            ev.append(("seg", g, r + 1))
        ev.append(("out", g, r))
    return ev + [("norm", g, 0)]


def ssd_tensor(pe, k):
    b = SsdBuffers(k)
    job = "ssd_in"
    p0, n0 = k.panel0[job], k.pair0[job]
    chunk = [slice(c * P, (c + 1) * P) for c in range(NC)]

    def dt(g, i):
        pe.wait_ge(k.s("panel_split"), p0 + 1)
        pe.wait_ge(k.s("banks_free"), 2 * n0 + 2)
        gemm_tile(pe, k, k.bank(job, 0), k.slot(job, 0), DT, SSD_ROWS, 0, k.xh, k.xl, m=SSD_ROWS
                  ).then_inc(k.s("panel_used"), 1)

    def tile_(g, i):
        n = 1 + 5 * g + i // 2
        if i % 2 == 0:
            pe.wait_ge(k.s("panel_split"), p0 + n + 1)
            pe.wait_ge(k.s("banks_free"), 2 * (n0 + n) + (4 if i == 0 else 2))
        mm = gemm_tile(pe, k, 2 * (i // 2 % 2) + i % 2, k.slot(job, n), DT, 256, P * (i % 2), k.xh, k.xl)
        if i % 2:
            mm.then_inc(k.s("panel_used"), 1)
        if i == 5 and g == 0:
            decays()

    def decays():
        pe.wait_ge(k.s("ssd_cs"), 1)
        for c in range(NC):
            pe.transpose(k.ps[:, 5, c * SSD_DT:(c + 1) * SSD_DT], b.dtx[0:SSD_DT, chunk[c]],
                         k.c("ident")[0:SSD_DT, 0:SSD_DT])
            mm = pe.transpose(k.ps[:, 5, (NC + c) * SSD_DT:(NC + c + 1) * SSD_DT], b.dt[0:SSD_DT, chunk[c]],
                              k.c("ident")[0:SSD_DT, 0:SSD_DT])
        mm.then_inc(k.s("ssd_turned_dt"), 1)
        pe.wait_ge(k.s("ssd_dt_t"), 2)
        pe.matmul(k.ps[:, 6, 0:P], b.last_row, b.cs_t.rearrange("p c h -> p (c h)"), start=True, stop=True
                  ).then_inc(k.s("ssd_ends"), 1)

    def turn(g, _):
        if g == 0:
            pe.wait_ge(k.s("rms_ready"), 3)
            pe.wait_ge(k.s("ssd_decays"), 2)
        pe.wait_ge(k.s("ssd_silu"), 6 * g + 6)
        for c in range(NC):
            if c >= 2:
                pe.wait_ge(k.s("ssd_xdt"), NC * g + c - 1)
            for t in range(SSD_TG):
                mm = pe.transpose(k.ps[:, 5 + c % 2, t * P:(t + 1) * P], b.x[:, g % 2, t, chunk[c]],
                                  k.c("ident"))
            mm.then_inc(k.s("ssd_turned_x"), 1)
        if g:
            pe.wait_ge(k.s("ssd_rms"), g)
            pe.wait_ge(k.s("ssd_y"), SSD_TG * g)
        for c in range(NC - 1):
            mm = pe.transpose(k.ps[:, 7, chunk[c]], b.bc[:, g % 2, 0, chunk[c]], k.c("ident"))
        mm.then_inc(k.s("ssd_turned_b"), 1)
        for c in range(NC):
            mm = pe.matmul(k.ps[:, 4, chunk[c]], b.bc[:, g % 2, 0, chunk[c]], b.bc[:, g % 2, 1, chunk[c]],
                           start=True, stop=True)
        mm.then_inc(k.s("ssd_cb_done"), 1)

    def states(g, _):
        for c in range(NC - 1):
            pe.wait_ge(k.s("ssd_xw"), 3 * g + c + 1)
            if c == 0:
                pe.wait_ge(k.s("ssd_b_t"), g + 1)
                pe.wait_ge(k.s("ssd_xdt"), NC * (g + 1))
            if c == 2:
                pe.wait_ge(k.s("ssd_prev"), 5 * g + 1)
            pe.matmul(k.ps[:, 5 + c % 2, :], b_tok(b, c), b.xw[:, c % 2, :],
                      start=True, stop=True).then_inc(k.s("ssd_state"), 1)

    def seg(g, r):
        h = SSD_R * g + r
        if r < 2:
            pe.wait_ge(k.s("ssd_prev"), 5 * (g + 1))
            pe.wait_ge(k.s("ssd_pick"), g + 1)
            pe.wait_ge(k.s("ssd_cb"), g + 1)
            pe.wait_ge(k.s("ssd_b_t"), g + 1)
        if h:
            pe.wait_ge(k.s("ssd_ecs"), h)
        if h >= 2:
            pe.wait_ge(k.s("ssd_seg_exp"), h - 1)
        pick = b.pick[0:SSD_ROWS, r, :]
        pe.matmul(k.ps[:, 7, 0:384], pick, b.cs3[0:SSD_ROWS, P:], start=True, stop=True
                  ).then_inc(k.s("ssd_cs_spread"), 1)
        bank = 5 + r % 2
        pe.matmul(k.ps[:, bank, :], pick, b.cs3[0:SSD_ROWS, :], start=True, stop=False)
        for c in range(NC):
            pe.matmul(k.ps[:, bank, chunk[c]], b.ncs3[0:SSD_ROWS, chunk[c]], b.pick[0:SSD_ROWS, r, :],
                      start=False, stop=False)
        for c in range(NC):
            mm = pe.matmul(k.ps[:, bank, chunk[c]], b.ident, b.mask, start=False, stop=c == NC - 1)
        mm.then_inc(k.s("ssd_seg"), 1)

    def out(g, r):
        h, rows = SSD_R * g + r, slice(64 * (r % 2), 64 * (r % 2) + 64)
        if r % 2 == 0 and h >= 2:
            pe.wait_ge(k.s("ssd_y"), h // 2)
        pe.wait_ge(k.s("ssd_m"), h + 1)
        pe.wait_ge(k.s("ssd_cdec"), h + 1)
        if r == 0:
            pe.wait_ge(k.s("ssd_cb"), g + 1)
        cols = slice(64 * r, 64 * r + 64)
        for c in range(NC):
            mm = pe.matmul(k.ps[rows, 4, chunk[c]], b.xdt[:, c, cols], b.m[:, r % 2, chunk[c]],
                           start=True, stop=c == 0)
            if c:
                mm = pe.matmul(k.ps[rows, 4, chunk[c]], b.prev[:, c - 1, cols],
                               b.cdec[:, r % 2, chunk[c - 1]], start=False, stop=True)
        mm.then_inc(k.s("ssd_out"), 1)

    def norm(g, _):
        pe.wait_ge(k.s("ssd_sqsum"), SSD_TG * (g + 1))
        pe.wait_ge(k.s("ssd_ecs"), SSD_R * (g + 1))
        pe.matmul(k.ps[:, 7, :], k.c("ones"), k.sqsum[:, :], start=True, stop=True
                  ).then_inc(k.s("ssd_norm_sum"), 1)

    do = {"dt": dt, "tile": tile_, "turn": turn, "states": states, "seg": seg, "out": out, "norm": norm}
    for what, g, i in ssd_events():
        do[what](g, i)


def b_tok(b, c):
    return b.cdec.rearrange("p a s -> p (a s)")[:, c * P:(c + 1) * P]


def ssd_channel(g, i):
    return (SSD_T + g, SSD_T + SSD_G + g)[i] if i < 2 else SSD_TG * g + i - 2


def ssd_place(b, g, i):
    return b.bc[:, g % 2, i, :] if i < 2 else b.x[:, g % 2, i - 2, :]


def ssd_scalar(act, k):
    b = SsdBuffers(k)
    n0 = k.pair0["ssd_in"]
    act.dma_start(b.table, k.dram["ssd_table"][:, 0:2 * P + SSD_DT]).then_inc(k.s("ssd_table"), 16)
    act.dma_start(b.start, k.dram["ssd_table"][:, 2 * P + SSD_DT:]).then_inc(k.s("ssd_table"), 16)

    def dt(g, i):
        act.activation(b.ea, k.p("ssd_a_log")[0:SSD_ROWS], ACT.Exp).then_inc(k.s("ssd_ea"), 1)
        softplus_scalar(act, k, "ssd_softplus", b.size[0:SSD_ROWS], b.e[0:SSD_ROWS])

    def decays():
        act.wait_ge(k.s("ssd_end_diff"), 1)
        ends = k.ps[:, 6, 0:P].rearrange("p (c h) -> p c h", h=SSD_DT)
        act.activation(b.dec, ends, ACT.Exp).then_inc(k.s("ssd_decays"), 1)
        act.activation(b.end_w, b.end_w, ACT.Exp).then_inc(k.s("ssd_decays"), 1)

    def tile_(g, i):
        if i % 2:
            pair_tile(g, i - 1)
            pair_tile(g, i)
        if i == 5 and g == 0:
            decays()

    def pair_tile(g, i):
        n = n0 + 1 + 5 * g + i // 2
        act.wait_ge(k.s("banks_free"), 4 + 2 * n + i % 2 + 1)
        if i < 6:
            ci = 6 * g + i
            ch = ssd_channel(g, i)
            place = ssd_place(b, g, i)
            act.activation(place, b.raw[:, i % 2, 3:], ACT.Identity, bias=k.p("ssd_conv_b", ch),
                           scale=k.p("ssd_conv_w", 3 * 24 + ch)).then_inc(k.s("ssd_biased"), 1)
            act.wait_ge(k.s("ssd_tapped"), 3 * ci + 3)
            act.activation(place, place, ACT.Silu).then_inc(k.s("ssd_silu"), 1)
        else:
            act.activation(b.z[:, i - 6, :], b.z[:, i - 6, :], ACT.Silu).then_inc(k.s("ssd_z"), 1)

    def turn(g, _):
        act.wait_ge(k.s("ssd_turned_b"), g + 1)
        act.activation(b.cdec.rearrange("p a s -> p (a s)")[:, 0:384], k.ps[:, 7, 0:384], ACT.Copy
                       ).then_inc(k.s("ssd_b_t"), 1)
        act.wait_ge(k.s("ssd_cb_done"), g + 1)
        act.activation(b.cb, k.ps[:, 4, :], ACT.Copy).then_inc(k.s("ssd_cb"), 1)

    def seg(g, r):
        h = SSD_R * g + r
        act.wait_ge(k.s("ssd_cs_spread"), h + 1)
        if h:
            act.wait_ge(k.s("ssd_cdec"), h)
        act.activation(b.ecs, k.ps[:, 7, 0:384], ACT.Exp).then_inc(k.s("ssd_ecs"), 1)
        act.wait_ge(k.s("ssd_seg"), h + 1)
        if h >= 2:
            act.wait_ge(k.s("ssd_out"), h - 1)
        act.activation(b.m[:, r % 2, :], k.ps[:, 5 + r % 2, :], ACT.Exp).then_inc(k.s("ssd_seg_exp"), 1)

    def out(g, r):
        if r % 2:
            t = SSD_TG * g + r // 2
            act.wait_ge(k.s("ssd_gated"), t + 1)
            if t >= 2:
                act.wait_ge(k.s("ssd_sqsum"), t - 1)
            act.activation(k.sq[:, t % 2, :], b.x[:, g % 2, r // 2, :], ACT.Square).then_inc(k.s("ssd_sq"), 1)

    def norm(g, _):
        act.wait_ge(k.s("ssd_norm_sum"), g + 1)
        act.activation(k.rms[:, :], k.ps[:, 7, :], ACT.Sqrt, bias=k.p("eps"), scale=1.0 / (SSD_TG * P)
                       ).then_inc(k.s("ssd_rms"), 1)
        for t in range(SSD_TG):
            act.wait_ge(k.s("ssd_normed"), SSD_TG * g + t + 1)
            act.activation(k.gh[:, SSD_TG * g + t, :], b.x[:, g % 2, t, :], ACT.Copy
                           ).then_inc(k.s("ssd_y_hi"), 1)

    do = {"dt": dt, "tile": tile_, "turn": turn, "seg": seg, "out": out, "norm": norm}
    for what, g, i in ssd_events():
        if what in do:
            do[what](g, i)


def ssd_vector(dve, k):
    b = SsdBuffers(k)
    job = "ssd_in"
    p0 = k.panel0[job]
    R = slice(0, SSD_ROWS)
    dve.memset(b.raw[:, :, 0:3], 0.0).then_inc(k.s("ssd_padded"), 1)
    dve.wait_ge(k.s("ssd_padded"), 1)
    norm_vector(dve, k, 2)

    def dt(g, i):
        dve.wait_ge(k.s("ssd_table"), 32)
        dve.tensor_copy(b.ident, k.c("ident")).then_inc(k.s("ssd_tables"), 1)
        dve.tensor_copy(b.mask, b.mask32).then_inc(k.s("ssd_tables"), 1)
        dve.tensor_copy(b.pick3, b.pick32).then_inc(k.s("ssd_tables"), 1)
        dve.wait_ge(k.s("panel_used"), p0 + 1)
        dve.tensor_tensor(b.dtx[R], k.ps[R, k.bank(job, 0), :], k.rstd[R], ALU.mult
                          ).then_inc(k.s("banks_free"), 2)
        dve.wait_ge(k.s("banks_free"), 4 + 2 * k.pair0[job] + 2)
        dve.tensor_scalar(b.dtx[R], b.dtx[R], k.p("ssd_dt_bias")[R], None, ALU.add
                          ).then_inc(k.s("ssd_dt_raw"), 1)
        dve.wait_ge(k.s("ssd_dt_raw"), 1)
        softplus_vector(dve, k, "ssd_softplus", b.dtx[R], b.size[R], b.e[R], b.q[R], b.dt[R])
        dve.wait_ge(k.s("ssd_ea"), 1)
        chain = Chain(dve, k, "ssd_chain")
        chain(dve.tensor_scalar(b.size[R], b.dt[R], b.ea, -1.0, ALU.mult, ALU.mult))
        chain(dve.tensor_tensor_scan(b.dtx[R], b.start[R], b.size[R], 0.0, ALU.mult, ALU.add))
        hi, mid = b.e[R].bitcast(BF16)[:, 0:S], b.e[R].bitcast(BF16)[:, S:2 * S]
        chain(dve.tensor_copy(hi, b.dtx[R]))
        chain(dve.tensor_tensor(b.q[R], b.dtx[R], hi, ALU.subtract))
        chain(dve.tensor_copy(mid, b.q[R]))
        chain(dve.tensor_copy(b.cs3[0:32], hi[0:32]))
        chain(dve.tensor_copy(b.cs3[32:64], mid[32:64]))
        chain(dve.tensor_tensor(b.cs3[64:96], b.q[64:96], mid[64:96], ALU.subtract))
        dve.tensor_scalar(b.ncs3[R], b.cs3[R], -1.0, None, ALU.mult).then_inc(k.s("ssd_cs"), 1)

    def decays():
        dve.wait_ge(k.s("ssd_turned_dt"), 1)
        dve.tensor_copy(b.cs_t.rearrange("p c h -> p (c h)"), k.ps[:, 5, 0:P]).then_inc(k.s("ssd_dt_t"), 1)
        dve.tensor_copy(b.dt_t.rearrange("p c h -> p (c h)"), k.ps[:, 5, P:2 * P]).then_inc(k.s("ssd_dt_t"), 1)
        dve.wait_ge(k.s("ssd_dt_t"), 2)
        dve.wait_ge(k.s("ssd_ends"), 1)
        dve.tensor_tensor(b.end_w.rearrange("p c h -> p (c h)"), k.ps[:, 6, 0:P],
                          b.cs_t.rearrange("p c h -> p (c h)"), ALU.subtract).then_inc(k.s("ssd_end_diff"), 1)
        dve.wait_ge(k.s("ssd_decays"), 2)

    def tile_(g, i):
        if i % 2:
            n = 1 + 5 * g + i // 2
            dve.wait_ge(k.s("panel_used"), p0 + n + 1)
            for j in (i - 1, i):
                evac(g, j)
            if i < 6:
                for j in (i - 1, i):
                    taps(g, j)
        if i == 5 and g == 0:
            decays()

    def evac(g, i):
        place = b.raw[:, i % 2, 3:] if i < 6 else b.z[:, i - 6, :]
        if i < 6 and 6 * g + i >= 2:
            dve.wait_ge(k.s("ssd_tapped"), 3 * (6 * g + i - 1))
        if i >= 6 and g:
            dve.wait_ge(k.s("ssd_gated"), SSD_TG * g)
        dve.tensor_tensor(place, k.ps[:, 2 * (i // 2 % 2) + i % 2, :], k.rstd[:, :], ALU.mult
                          ).then_inc(k.s("banks_free"), 1)

    def taps(g, i):
        ci, ch, place = 6 * g + i, ssd_channel(g, i), ssd_place(b, g, i)
        dve.wait_ge(k.s("ssd_biased"), ci + 1)
        for n, tap in enumerate((2, 1, 0)):
            if n:
                dve.wait_ge(k.s("ssd_tapped"), 3 * ci + n)
            dve.scalar_tensor_tensor(place, b.raw[:, i % 2, tap:tap + S], k.p("ssd_conv_w", tap * 24 + ch),
                                     place, ALU.mult, ALU.add).then_inc(k.s("ssd_tapped"), 1)

    def turn(g, _):
        if g:
            dve.wait_ge(k.s("ssd_xw"), 3 * g)
        for c in range(NC):
            dve.wait_ge(k.s("ssd_turned_x"), NC * g + c + 1)
            dve.tensor_tensor(by_head(b.xdt[:, c, :]), by_head(k.ps[:, 5 + c % 2, :]), heads_of(b.dt_t, c, g),
                              ALU.mult).then_inc(k.s("ssd_xdt"), 1)

    def states(g, _):
        def weigh(c):
            dve.wait_ge(k.s("ssd_xdt"), NC * g + c + 1)
            dve.tensor_tensor(by_head(b.xw[:, c % 2, :]), by_head(b.xdt[:, c, :]), heads_of(b.end_w, c, g),
                              ALU.mult).then_inc(k.s("ssd_xw"), 1)

        def carry(c):
            dve.wait_ge(k.s("ssd_prev"), 5 * g + 2 * c - 1)
            dve.tensor_tensor(by_head(b.prev[:, c, :]), by_head(b.prev[:, c - 1, :]), heads_of(b.dec, c, g),
                              ALU.mult).then_inc(k.s("ssd_prev"), 1)
            dve.wait_ge(k.s("ssd_prev"), 5 * g + 2 * c)
            dve.wait_ge(k.s("ssd_state"), 3 * g + c + 1)
            dve.tensor_tensor(b.prev[:, c, :], b.prev[:, c, :], k.ps[:, 5 + c % 2, :], ALU.add
                              ).then_inc(k.s("ssd_prev"), 1)

        weigh(0)
        weigh(1)
        dve.wait_ge(k.s("ssd_state"), 3 * g + 1)
        if g:
            dve.wait_ge(k.s("ssd_prev"), 5 * g)
        dve.tensor_copy(b.prev[:, 0, :], k.ps[:, 5, :]).then_inc(k.s("ssd_prev"), 1)
        weigh(2)
        carry(1)
        carry(2)
        dve.wait_ge(k.s("ssd_tables"), 3)
        dve.tensor_copy(b.pick[R], b.pick3[R, SSD_R * g:SSD_R * (g + 1)].unsqueeze(2)
                        .to_broadcast([SSD_ROWS, SSD_R, P])).then_inc(k.s("ssd_pick"), 1)

    def seg(g, r):
        h = SSD_R * g + r
        dve.wait_ge(k.s("ssd_ecs"), h + 1)
        if r < 2:
            dve.wait_ge(k.s("ssd_state"), 3 * (g + 1))
        if h >= 2:
            dve.wait_ge(k.s("ssd_out"), h - 1)
        dve.tensor_tensor(b.cdec[:, r % 2, :], b.bc[:, g % 2, 1, P:], b.ecs, ALU.mult
                          ).then_inc(k.s("ssd_cdec"), 1)
        dve.wait_ge(k.s("ssd_seg_exp"), h + 1)
        if r == 0:
            dve.wait_ge(k.s("ssd_cb"), g + 1)
        dve.tensor_tensor(b.m[:, r % 2, :], b.m[:, r % 2, :], b.cb, ALU.mult).then_inc(k.s("ssd_m"), 1)

    def out(g, r):
        if r % 2 == 0:
            return
        t = r // 2
        n = SSD_TG * g + t
        place = b.x[:, g % 2, t, :]
        dve.wait_ge(k.s("ssd_out"), SSD_R * g + r + 1)
        dve.scalar_tensor_tensor(place, place, k.p("ssd_d", n), k.ps[:, 4, :], ALU.mult, ALU.add
                                 ).then_inc(k.s("ssd_y"), 1)
        dve.wait_ge(k.s("ssd_y"), n + 1)
        dve.wait_ge(k.s("ssd_z"), SSD_TG * (g + 1))
        dve.tensor_tensor(place, place, b.z[:, t, :], ALU.mult).then_inc(k.s("ssd_gated"), 1)
        dve.wait_ge(k.s("ssd_sq"), n + 1)
        if t == 0:
            if n:
                dve.wait_ge(k.s("ssd_sqsum"), n)
            dve.tensor_copy(k.sqsum[:, :], k.sq[:, n % 2, :]).then_inc(k.s("ssd_sqsum"), 1)
        else:
            dve.wait_ge(k.s("ssd_sqsum"), n)
            dve.tensor_tensor(k.sqsum[:, :], k.sqsum[:, :], k.sq[:, n % 2, :], ALU.add
                              ).then_inc(k.s("ssd_sqsum"), 1)

    def norm(g, _):
        dve.wait_ge(k.s("ssd_rms"), g + 1)
        dve.reciprocal(k.rms[:, :], k.rms[:, :]).then_inc(k.s("ssd_rstd"), 1)
        dve.wait_ge(k.s("ssd_rstd"), g + 1)
        dve.wait_ge(k.s("ssd_gated"), SSD_TG * (g + 1))
        for t in range(SSD_TG):
            n = SSD_TG * g + t
            place = b.x[:, g % 2, t, :]
            dve.scalar_tensor_tensor(place, place, k.p("ssd_norm", n), k.rms[:, :], ALU.mult, ALU.mult
                                     ).then_inc(k.s("ssd_normed"), 1)
        for t in range(SSD_TG):
            n = SSD_TG * g + t
            dve.wait_ge(k.s("ssd_normed"), n + 1)
            dve.wait_ge(k.s("ssd_y_hi"), n + 1)
            dve.tensor_tensor(k.gl[:, n, :], b.x[:, g % 2, t, :], k.gh[:, n, :], ALU.subtract
                              ).then_inc(k.s("ssd_y_split"), 1)

    do = {"dt": dt, "tile": tile_, "turn": turn, "states": states, "seg": seg, "out": out, "norm": norm}
    for what, g, i in ssd_events():
        do[what](g, i)



HG_HALVES = 8
HG_LEVEL_AT = 5
HG_TAIL_AT = HG_LEVEL_AT + 8


class HgrnBuffers:
    def __init__(self, k):
        a = Arena(k)
        self.q, self.ks, self.qp = a.take(2, S), a.take(2, S), a.take(2, S)
        self.f = a.take(S)
        self.pd = [self.f] + [a.take(S >> n) for n in range(1, 8)]
        self.attn, self.i, self.g = a.take(2, S), a.take(2, S), a.take(2, S)
        self.i_t = a.take(NC, P)
        self.k_end = a.take(NC - 1, P)
        self.state = a.take(NC - 1, P)
        self.y = a.take(S)
        self.masks = a.take(len(LEVELS), P, dt=I32)
        self.lb, self.one_lb, self.top = (a.take(HG_H) for _ in range(3))
        self.e = a.take(DEPTH, HG_H)


def hgrn_events():
    ev = []
    for slot in range((HG_H - 1) * HG_HALVES + HG_TAIL_AT + 6):
        h, t = divmod(slot - HG_TAIL_AT, HG_HALVES)
        if 0 <= h < HG_H and t < 6:
            ev.append(("tail", h, t))
        h, half = divmod(slot, HG_HALVES)
        if h < HG_H:
            ev.append(("half", h, half))
        h, level = divmod(slot - HG_LEVEL_AT, HG_HALVES)
        if 0 <= h < HG_H:
            ev.append(("level", h, level))
    return ev


def hgrn_tensor(pe, k):
    b = HgrnBuffers(k)
    job = "hgrn_in"
    p0, n0 = k.panel0[job], k.pair0[job]
    chunk = [slice(c * P, (c + 1) * P) for c in range(NC)]

    def half(h, i):
        n, second, part = 2 * h + i // 4, i // 2 % 2, i % 2
        if i % 4 == 0:
            pe.wait_ge(k.s("panel_split"), p0 + n + 1)
            pe.wait_ge(k.s("banks_free"), 2 * (n0 + n) + 2)
        slot = k.slot(job, n)
        wh, wl = k.whi(slot), k.wl[:, slot, :]
        for q in range(4 * part, 4 * part + 4):
            a = q * 256 + P * second
            mm = product(pe, k.ps[:, k.bank(job, n) + second, :], wh[:, a:a + P], wl[:, a:a + P],
                         k.xh[:, q, :], k.xl[:, q, :], q == 0, q == DT - 1)
        if part:
            mm.then_inc(k.s("panel_used" if second else "hgrn_tile"), 1)

    def level(h, n):
        if n == 0:
            pe.wait_ge(k.s("hgrn_gates"), 3 * h + 3)
        elif n >= 2:
            pe.wait_ge(k.s("hgrn_update"), 21 * h + 3 * (n - 1))
        done = 8 * h + n
        if done >= 2:
            pe.wait_ge(k.s("hgrn_attn"), done - 1)
        rhs = b.qp if n else b.q
        for c in range(NC):
            mm = pe.matmul(k.ps[:, 5 + n % 2, chunk[c]], b.ks[:, h % 2, chunk[c]], rhs[:, h % 2, chunk[c]],
                           start=True, stop=True)
        mm.then_inc(k.s("hgrn_level"), 1)

    def tail(h, t):
        if t == 0:
            pe.wait_ge(k.s("banks_free"), 4 + 2 * (n0 + 2 * h + 1) + 1)
            if h:
                pe.wait_ge(k.s("hgrn_rms"), h)
            else:
                pe.wait_ge(k.s("rms_ready"), 7)
            for c in range(NC):
                mm = pe.transpose(k.ps[:, 4, chunk[c]], b.i[:, h % 2, chunk[c]], k.c("ident"))
            mm.then_inc(k.s("hgrn_turned_i"), 1)
        elif t == 1:
            pe.wait_ge(k.s("hgrn_i_t"), h + 1)
            pe.wait_ge(k.s("hgrn_update"), 21 * (h + 1))
            for c in range(NC - 1):
                mm = pe.transpose(k.ps[:, 4, chunk[c]], b.ks[:, h % 2, chunk[c]], k.c("ident"))
            mm.then_inc(k.s("hgrn_turned_k"), 1)
        elif t == 2:
            pe.wait_ge(k.s("hgrn_k_end"), h + 1)
            for c in range(NC - 1):
                mm = pe.matmul(k.ps[:, 4, chunk[c]], b.k_end[:, c, :], b.i_t[:, c, :], start=True, stop=True)
            mm.then_inc(k.s("hgrn_kv"), 1)
        elif t == 3:
            pe.wait_ge(k.s("hgrn_state"), 3 * (h + 1))
            pe.wait_ge(k.s("hgrn_attn"), 8 * (h + 1))
            if h:
                pe.wait_ge(k.s("hgrn_y"), 2 * h)
            for c in range(NC):
                mm = pe.matmul(k.ps[:, 7, chunk[c]], b.i_t[:, c, :], b.attn[:, h % 2, chunk[c]],
                               start=True, stop=c == 0)
                if c:
                    mm = pe.matmul(k.ps[:, 7, chunk[c]], b.state[:, c - 1, :], b.qp[:, h % 2, chunk[c]],
                                   start=False, stop=True)
            mm.then_inc(k.s("hgrn_o"), 1)
        elif t == 4:
            pe.wait_ge(k.s("hgrn_sq"), h + 1)
            pe.matmul(k.ps[:, 4, :], k.c("ones"), k.sq[:, h % 2, :], start=True, stop=True
                      ).then_inc(k.s("hgrn_sum"), 1)

    do = {"half": half, "level": level, "tail": tail}
    for what, h, i in hgrn_events():
        do[what](h, i)


def hgrn_scalar(act, k):
    b = HgrnBuffers(k)
    n0 = k.pair0["hgrn_in"]
    act.dma_start(b.masks, k.dram["hgrn_masks"]).then_inc(k.s("hgrn_masks"), 16)
    act.wait_ge(k.s("hgrn_lb"), 4)
    act.activation(b.e, b.e, ACT.Exp).then_inc(k.s("hgrn_lb_exp"), 1)

    def half(h, i):
        freed = 4 + 2 * (n0 + 2 * h)
        if i == 3:
            act.wait_ge(k.s("banks_free"), freed + 2)
            act.activation(b.f, b.f, ACT.Sigmoid).then_inc(k.s("hgrn_sigmoid"), 1)
        elif i == 7:
            act.wait_ge(k.s("banks_free"), freed + 4)
            act.activation(b.g[:, h % 2, :], b.g[:, h % 2, :], ACT.Silu).then_inc(k.s("hgrn_silu"), 1)

    def tail(h, t):
        if t == 0:
            act.wait_ge(k.s("hgrn_turned_i"), h + 1)
            act.activation(b.i_t.rearrange("p c v -> p (c v)"), k.ps[:, 4, :], ACT.Copy
                           ).then_inc(k.s("hgrn_i_t"), 1)
        elif t == 1:
            act.wait_ge(k.s("hgrn_turned_k"), h + 1)
            act.activation(b.k_end.rearrange("p c v -> p (c v)"), k.ps[:, 4, 0:384], ACT.Copy
                           ).then_inc(k.s("hgrn_k_end"), 1)
        elif t == 3:
            act.wait_ge(k.s("hgrn_o"), h + 1)
            act.activation(k.sq[:, h % 2, :], k.ps[:, 7, :], ACT.Square).then_inc(k.s("hgrn_sq"), 1)
        elif t == 4:
            act.wait_ge(k.s("hgrn_sum"), h + 1)
            if h:
                act.wait_ge(k.s("hgrn_y"), 2 * h)
            act.activation(k.rms[:, :], k.ps[:, 4, :], ACT.Sqrt, bias=k.p("eps"), scale=1.0 / P
                           ).then_inc(k.s("hgrn_rms"), 1)
        elif t == 5:
            act.wait_ge(k.s("hgrn_y"), 2 * h + 2)
            act.activation(k.gh[:, h, :], b.y, ACT.Copy).then_inc(k.s("hgrn_y_hi"), 1)

    do = {"half": half, "tail": tail}
    for what, h, i in hgrn_events():
        if what in do:
            do[what](h, i)


def hgrn_vector(dve, k):
    b = HgrnBuffers(k)
    job = "hgrn_in"
    p0 = k.panel0[job]
    low0, n = PARAMS["hgrn_lower_bounds"]
    low = k.par[:, low0:low0 + n].rearrange("p (l h) -> p l h", l=DEPTH)
    chain = Chain(dve, k, "hgrn_lb")
    chain(dve.tensor_tensor(b.top, low[:, 0], low[:, 1], ALU.max))
    chain(dve.tensor_tensor(b.top, b.top, low[:, 2], ALU.max))
    chain(dve.tensor_tensor(b.top, b.top, low[:, 3], ALU.max))
    chain(dve.tensor_tensor(b.e, low, b.top.unsqueeze(1).to_broadcast([P, DEPTH, HG_H]), ALU.subtract))
    dve.wait_ge(k.s("hgrn_lb_exp"), 1)
    chain(dve.tensor_tensor(b.lb, b.e[:, 1], b.e[:, 2], ALU.add))
    chain(dve.tensor_tensor(b.lb, b.lb, b.e[:, 3], ALU.add))
    chain(dve.tensor_tensor(b.top, b.lb, b.e[:, 0], ALU.add))
    chain(dve.reciprocal(b.top, b.top))
    chain(dve.tensor_tensor(b.lb, b.lb, b.top, ALU.mult))
    chain(dve.tensor_scalar(b.one_lb, b.lb, -1.0, 1.0, ALU.mult, ALU.add))
    norm_vector(dve, k, 6)
    dve.wait_ge(k.s("hgrn_masks"), 16)

    def half(h, i):
        if i % 2 == 0:
            return
        n, which = 2 * h + i // 4, i // 2
        bank = k.bank(job, n) + which % 2
        dve.wait_ge(k.s("panel_used" if which % 2 else "hgrn_tile"), (p0 if which % 2 else 0) + n + 1)
        if which == 0:
            dve.scalar_tensor_tensor(b.q[:, h % 2, :], k.ps[:, bank, :], float(P) ** -0.5, k.rstd[:, :],
                                     ALU.mult, ALU.mult).then_inc(k.s("banks_free"), 1)
            return
        if which == 1 and h:
            dve.wait_ge(k.s("hgrn_update"), 21 * (h - 1) + 3)
        place = (b.q[:, 0, :], b.f, b.i[:, h % 2, :], b.g[:, h % 2, :])[which]
        dve.tensor_tensor(place, k.ps[:, bank, :], k.rstd[:, :], ALU.mult).then_inc(k.s("banks_free"), 1)
        if which == 1:
            dve.wait_ge(k.s("hgrn_sigmoid"), h + 1)
            dve.tensor_scalar(b.f, b.f, b.one_lb[:, h:h + 1], b.lb[:, h:h + 1], ALU.mult, ALU.add
                              ).then_inc(k.s("hgrn_gates"), 1)
            dve.wait_ge(k.s("hgrn_gates"), 3 * h + 1)
            dve.tensor_scalar(b.ks[:, h % 2, :], b.f, -1.0, 1.0, ALU.mult, ALU.add
                              ).then_inc(k.s("hgrn_gates"), 1)
            dve.tensor_tensor(b.qp[:, h % 2, :], b.q[:, h % 2, :], b.f, ALU.mult
                              ).then_inc(k.s("hgrn_gates"), 1)

    def level(h, n):
        if n:
            B = LEVELS[n - 1]
            blocks = S // (2 * B)
            pd = b.pd[n - 1].rearrange("p (n two) -> p n two", two=2)
            first, second = pd[:, :, 0], pd[:, :, 1]
            wide = [P, blocks, B]
            qp = b.qp[:, h % 2, :].rearrange("p (n two b) -> p n two b", two=2, b=B)[:, :, 1, :]
            ks = b.ks[:, h % 2, :].rearrange("p (n two b) -> p n two b", two=2, b=B)[:, :, 0, :]
            dve.wait_ge(k.s("hgrn_level"), 8 * h + n + 1)
            if n > 1:
                dve.wait_ge(k.s("hgrn_update"), 21 * h + 3 * (n - 1))
            else:
                dve.wait_ge(k.s("hgrn_gates"), 3 * h + 3)
            dve.tensor_tensor(b.pd[n], first, second, ALU.mult).then_inc(k.s("hgrn_update"), 1)
            dve.tensor_tensor(qp, qp, first.unsqueeze(2).to_broadcast(wide), ALU.mult
                              ).then_inc(k.s("hgrn_update"), 1)
            dve.tensor_tensor(ks, ks, second.unsqueeze(2).to_broadcast(wide), ALU.mult
                              ).then_inc(k.s("hgrn_update"), 1)
            dve.wait_ge(k.s("hgrn_attn"), 8 * h + n)
        else:
            dve.wait_ge(k.s("hgrn_level"), 8 * h + 1)
        attn = b.attn[:, h % 2, :].rearrange("p (c l) -> p c l", c=NC)
        ps = k.ps[:, 5 + n % 2, :].rearrange("p (c l) -> p c l", c=NC)
        if n:
            mask = b.masks[:, n - 1, :].unsqueeze(1).to_broadcast([P, NC, P])
            dve.copy_predicated(attn, mask, ps).then_inc(k.s("hgrn_attn"), 1)
        else:
            ident = k.c("ident").unsqueeze(1).to_broadcast([P, NC, P])
            dve.tensor_tensor(attn, ps, ident, ALU.mult).then_inc(k.s("hgrn_attn"), 1)

    def tail(h, t):
        if t == 2:
            dve.wait_ge(k.s("hgrn_kv"), h + 1)
            if h:
                dve.wait_ge(k.s("hgrn_state"), 3 * h)
            dve.tensor_copy(b.state[:, 0, :], k.ps[:, 4, 0:P]).then_inc(k.s("hgrn_state"), 1)
            for c in (1, 2):
                dve.wait_ge(k.s("hgrn_state"), 3 * h + c)
                dve.scalar_tensor_tensor(b.state[:, c, :], b.state[:, c - 1, :], b.pd[7][:, c:c + 1],
                                         k.ps[:, 4, c * P:(c + 1) * P], ALU.mult, ALU.add
                                         ).then_inc(k.s("hgrn_state"), 1)
        elif t == 5:
            dve.wait_ge(k.s("hgrn_rms"), h + 1)
            dve.reciprocal(k.rms[:, :], k.rms[:, :]).then_inc(k.s("hgrn_rstd"), 1)
            dve.wait_ge(k.s("hgrn_rstd"), h + 1)
            if h:
                dve.wait_ge(k.s("hgrn_y_split"), h)
            dve.scalar_tensor_tensor(b.y, k.ps[:, 7, :], k.p("hgrn_norm"), k.rms[:, :], ALU.mult, ALU.mult
                                     ).then_inc(k.s("hgrn_y"), 1)
            dve.wait_ge(k.s("hgrn_y"), 2 * h + 1)
            dve.wait_ge(k.s("hgrn_silu"), h + 1)
            dve.tensor_tensor(b.y, b.y, b.g[:, h % 2, :], ALU.mult).then_inc(k.s("hgrn_y"), 1)
            dve.wait_ge(k.s("hgrn_y_hi"), h + 1)
            dve.tensor_tensor(k.gl[:, h, :], b.y, k.gh[:, h, :], ALU.subtract
                              ).then_inc(k.s("hgrn_y_split"), 1)

    do = {"half": half, "level": level, "tail": tail}
    for what, h, i in hgrn_events():
        do[what](h, i)



SWA_TILES = 12
ROT = 16
ROPE_THETA = 500000.0
SWA_TABLE = P + P + 3 * 256 + 2 * S


class SwaBuffers:
    def __init__(self, k):
        a = Arena(k)
        self.table = a.take(SWA_TABLE)
        t, at = self.table, 0
        self.half_ones, self.perm = t[:, 0:P], t[:, P:2 * P]
        self.mask = t[:, 2 * P:2 * P + 768]
        self.cos, self.sin = t[:, 1024:1024 + S], t[:, 1024 + S:1024 + 2 * S]
        self.raw = a.take(2, S)
        self.kt = a.take(2, S)
        self.vt = a.take(NC, 256)
        self.q = a.take(2, S)
        self.s = a.take(2, 2, 2, 256)
        self.pt = a.take(2, 2, 4 * P)
        self.xc, self.xs = a.take(S), a.take(S)
        self.mx, self.neg, self.sum, self.esink, self.inv = (a.take(2, 2, 2) for _ in range(5))


def swa_events():
    ev = []
    for i in range(SWA_TILES + 3):
        t = i - 6
        prev = i - 1
        normed = prev in (0, 1) or 4 <= prev < SWA_TILES
        if normed:
            ev.append(("sum", prev, 0))
        if 0 <= t - 1 < 8:
            ev.append(("turn", t - 1, 1))
        if 0 <= t < 8:
            ev.append(("score", t, 0))
        if 0 <= t - 1 < 8:
            ev.append(("pv", t - 1, 1))
        if i < SWA_TILES:
            ev.append(("tile", i, 0))
        if 0 <= t < 8:
            ev += [("turn", t, 0), ("score", t, 1), ("pv", t, 0)]
        if normed:
            ev.append(("rope", prev, 0))
        elif prev in (2, 3):
            ev.append(("turn_v", prev, 0))
    return ev


def normed_index(i):
    return i if i < 2 else i - 2


def swa_tensor(pe, k):
    b = SwaBuffers(k)
    job = "swa_in"
    p0, n0 = k.panel0[job], k.pair0[job]

    def tile_(i, _):
        n = i // 2
        if i % 2 == 0:
            pe.wait_ge(k.s("panel_split"), p0 + n + 1)
        pe.wait_ge(k.s("banks_free"), 2 * n0 + max(i, 1) + 3)
        gemm_tile(pe, k, i % 2, k.slot(job, n), DT, 256, P * (i % 2), k.xh, k.xl
                  ).then_inc(k.s("panel_used" if i % 2 else "swa_tile"), 1)

    def sum_(i, _):
        m = normed_index(i)
        pe.wait_ge(k.s("swa_sq"), m + 1)
        if m == 0:
            pe.wait_ge(k.s("swa_table"), 16)
        else:
            pe.wait_ge(k.s("swa_rotated"), 3 * m)
        pe.matmul(k.ps[:, 3, :], b.half_ones, k.sq[:, i % 2, :], start=True, stop=True
                  ).then_inc(k.s("swa_half_sum"), 1)

    def rope(i, _):
        m = normed_index(i)
        pe.wait_ge(k.s("swa_normed"), m + 1)
        pe.matmul(k.ps[:, 3, :], b.perm, b.raw[:, i % 2, :], start=True, stop=True
                  ).then_inc(k.s("swa_partner"), 1)

    def turn_v(i, _):
        pe.wait_ge(k.s("banks_free"), 4 + 2 * n0 + i + 1)
        if i == 3:
            pe.wait_ge(k.s("swa_v"), 1)
        for c in range(NC):
            mm = pe.transpose(k.ps[:, 7, c * P:(c + 1) * P], b.raw[:, i % 2, c * P:(c + 1) * P], k.c("ident"))
        mm.then_inc(k.s("swa_turned_v"), 1)

    def score(t, m):
        un = 2 * t + m
        pe.wait_ge(k.s("swa_rotated"), 3 * (2 + t) + 3)
        if un:
            pe.wait_ge(k.s("swa_masked"), 2 * un)
        for a in range(2):
            rows = slice(64 * a, 64 * a + 64)
            for blk in range(2):
                n = 2 * m + blk
                key = max(n - 1, 0) * P
                mm = pe.matmul(k.ps[:, 5 + a, blk * 256:(blk + 1) * 256], b.q[rows, t % 2, n * P:(n + 1) * P],
                               b.kt[rows, t // 4, key:key + 256], start=True, stop=True)
        mm.then_inc(k.s("swa_scored"), 1)

    def turn(t, m):
        un = 2 * t + m
        pe.wait_ge(k.s("swa_p"), 4 * (un + 1))
        if un:
            pe.wait_ge(k.s("swa_pt0"), un)
            pe.wait_ge(k.s("swa_pt1"), un)
        else:
            pe.wait_ge(k.s("swa_v"), 2)
            pe.wait_ge(k.s("rms_ready"), 5)
        for a in range(2):
            for blk in range(2):
                for kh in range(2):
                    at = (2 * blk + kh) * P
                    mm = pe.transpose(k.ps[:, (7, 4)[a], at:at + P], b.s[:, m, a, blk, kh * P:(kh + 1) * P],
                                      k.c("ident"))
            mm.then_inc(k.s(f"swa_turned{a}"), 1)

    def pv(t, m):
        un = 2 * t + m
        if m == 0 and t:
            pe.wait_ge(k.s("swa_y_split"), t)
        for a in range(2):
            pe.wait_ge(k.s(f"swa_pt{a}"), un + 1)
            head = 2 * (t // 4) + a
            for blk in range(2):
                n = 2 * m + blk
                for kh in range(2):
                    chunk = max(n - 1, 0) + kh
                    at = (2 * blk + kh) * P
                    mm = pe.matmul(k.ps[64 * a:64 * a + 64, 2, n * P:(n + 1) * P],
                                   b.vt[:, chunk, 64 * head:64 * head + 64], b.pt[:, m, a, at:at + P],
                                   start=kh == 0, stop=kh == 1)
        mm.then_inc(k.s("swa_pv"), 1)

    do = {"tile": tile_, "sum": sum_, "rope": rope, "turn_v": turn_v, "score": score, "turn": turn, "pv": pv}
    for what, i, m in swa_events():
        do[what](i, m)


def swa_scalar(act, k):
    b = SwaBuffers(k)
    n0 = k.pair0["swa_in"]
    act.dma_start(b.table, k.dram["swa_table"]).then_inc(k.s("swa_table"), 16)

    def tile_(i, _):
        if i in (2, 3):
            return
        act.wait_ge(k.s("banks_free"), 4 + 2 * n0 + i + 1)
        act.activation(k.sq[:, i % 2, :], b.raw[:, i % 2, :], ACT.Square).then_inc(k.s("swa_sq"), 1)

    def sum_(i, _):
        m = normed_index(i)
        act.wait_ge(k.s("swa_half_sum"), m + 1)
        if m:
            act.wait_ge(k.s("swa_normed"), m)
        act.activation(k.rms[:, :], k.ps[:, 3, :], ACT.Sqrt, bias=k.p("eps"), scale=1.0 / 64
                       ).then_inc(k.s("swa_rms"), 1)

    def turn_v(i, _):
        act.wait_ge(k.s("swa_turned_v"), i - 1)
        v = b.vt[:, :, P * (i - 2):P * (i - 1)]
        act.activation(v, k.ps[:, 7, :].rearrange("p (c d) -> p c d", c=NC), ACT.Copy
                       ).then_inc(k.s("swa_v"), 1)

    def score(t, m):
        un = 2 * t + m
        act.wait_ge(k.s("swa_max"), 4 * (un + 1))
        for a in range(2):
            for blk in range(2):
                row = b.s[:, m, a, blk, :]
                act.activation(row, row, ACT.Exp, bias=b.neg[:, m, a, blk:blk + 1],
                               accum_out=b.sum[:, m, a, blk:blk + 1]).then_inc(k.s("swa_exp"), 1)
        act.activation(b.esink[:, m], b.esink[:, m], ACT.Exp).then_inc(k.s("swa_exp"), 1)

    def turn(t, m):
        un = 2 * t + m
        act.wait_ge(k.s("swa_inv"), 2 * (un + 1))
        for a in range(2):
            for blk in range(2):
                row = b.s[:, m, a, blk, :]
                act.activation(row, row, ACT.Copy, scale=b.inv[:, m, a, blk:blk + 1]
                               ).then_inc(k.s("swa_p"), 1)
        act.wait_ge(k.s("swa_turned0"), un + 1)
        act.activation(b.pt[:, m, 0, :], k.ps[:, 7, :], ACT.Copy).then_inc(k.s("swa_pt0"), 1)

    def pv(t, m):
        if m:
            act.wait_ge(k.s("swa_pv"), 2 * t + 2)
            act.activation(k.gh[:, t, :], k.ps[:, 2, :], ACT.Copy).then_inc(k.s("swa_y_hi"), 1)

    do = {"tile": tile_, "sum": sum_, "turn_v": turn_v, "score": score, "turn": turn, "pv": pv}
    for what, i, m in swa_events():
        if what in do:
            do[what](i, m)


def swa_vector(dve, k):
    b = SwaBuffers(k)
    job = "swa_in"
    p0, n0 = k.panel0[job], k.pair0[job]
    sink0 = PARAMS["swa_sinks"][0]
    norm_vector(dve, k, 4)
    dve.wait_ge(k.s("swa_table"), 16)

    def tile_(i, _):
        dve.wait_ge(k.s("panel_used" if i % 2 else "swa_tile"), (p0 if i % 2 else 0) + i // 2 + 1)
        if i in (4, 5):
            dve.wait_ge(k.s("swa_turned_v"), i - 3)
        elif i >= 2:
            dve.wait_ge(k.s("swa_rotated"), 3 * normed_index(i - 2) + 3)
        dve.tensor_tensor(b.raw[:, i % 2, :], k.ps[:, i % 2, :], k.rstd[:, :], ALU.mult
                          ).then_inc(k.s("banks_free"), 1)

    def sum_(i, _):
        m = normed_index(i)
        dve.wait_ge(k.s("swa_rms"), m + 1)
        dve.reciprocal(k.rms[:, :], k.rms[:, :]).then_inc(k.s("swa_rstd"), 1)
        dve.wait_ge(k.s("swa_rstd"), m + 1)
        x = b.raw[:, i % 2, :]
        dve.scalar_tensor_tensor(x, x, k.p("swa_k_norm" if i < 2 else "swa_q_norm"), k.rms[:, :],
                                 ALU.mult, ALU.mult).then_inc(k.s("swa_normed"), 1)

    def rope(i, _):
        m = normed_index(i)
        dve.wait_ge(k.s("swa_normed"), m + 1)
        if m:
            dve.wait_ge(k.s("swa_rotated"), 3 * m)
        dve.tensor_tensor(b.xc, b.raw[:, i % 2, :], b.cos, ALU.mult).then_inc(k.s("swa_rotated"), 1)
        dve.wait_ge(k.s("swa_partner"), m + 1)
        dve.tensor_tensor(b.xs, k.ps[:, 3, :], b.sin, ALU.mult).then_inc(k.s("swa_rotated"), 1)
        dve.wait_ge(k.s("swa_rotated"), 3 * m + 2)
        place = b.kt[:, i, :] if i < 2 else b.q[:, i % 2, :]
        dve.tensor_tensor(place, b.xc, b.xs, ALU.add).then_inc(k.s("swa_rotated"), 1)

    def score(t, m):
        un = 2 * t + m
        dve.wait_ge(k.s("swa_scored"), un + 1)
        if un >= 2:
            dve.wait_ge(k.s("swa_turned1"), un - 1)
        for a in range(2):
            dve.scalar_tensor_tensor(b.s[:, m, a].rearrange("p b k -> p (b k)"), k.ps[:, 5 + a, :], 0.125,
                                     b.mask[:, 256 * m:256 * m + 512], ALU.mult, ALU.add
                                     ).then_inc(k.s("swa_masked"), 1)
        chain = 4 * un
        dve.wait_ge(k.s("swa_masked"), 2 * un + 2)
        dve.tensor_reduce(b.mx[:, m], b.s[:, m], AX.X, ALU.max).then_inc(k.s("swa_max"), 1)
        at = sink0 + 8 * (t // 4) + t % 4
        sinks = k.par[:, at:at + 5:4].unsqueeze(2).to_broadcast([P, 2, 2])
        dve.wait_ge(k.s("swa_max"), chain + 1)
        dve.tensor_tensor(b.mx[:, m], b.mx[:, m], sinks, ALU.max).then_inc(k.s("swa_max"), 1)
        dve.wait_ge(k.s("swa_max"), chain + 2)
        dve.tensor_scalar(b.neg[:, m], b.mx[:, m], -1.0, None, ALU.mult).then_inc(k.s("swa_max"), 1)
        dve.tensor_tensor(b.esink[:, m], sinks, b.mx[:, m], ALU.subtract).then_inc(k.s("swa_max"), 1)

    def turn(t, m):
        un = 2 * t + m
        dve.wait_ge(k.s("swa_exp"), 5 * (un + 1))
        dve.tensor_tensor(b.sum[:, m], b.sum[:, m], b.esink[:, m], ALU.add).then_inc(k.s("swa_inv"), 1)
        dve.wait_ge(k.s("swa_inv"), 2 * un + 1)
        dve.reciprocal(b.inv[:, m], b.sum[:, m]).then_inc(k.s("swa_inv"), 1)
        dve.wait_ge(k.s("swa_turned1"), un + 1)
        dve.tensor_copy(b.pt[:, m, 1, :], k.ps[:, 4, :]).then_inc(k.s("swa_pt1"), 1)

    def pv(t, m):
        if m:
            dve.wait_ge(k.s("swa_y_hi"), t + 1)
            dve.tensor_tensor(k.gl[:, t, :], k.ps[:, 2, :], k.gh[:, t, :], ALU.subtract
                              ).then_inc(k.s("swa_y_split"), 1)

    do = {"tile": tile_, "sum": sum_, "rope": rope, "score": score, "turn": turn, "pv": pv}
    for what, i, m in swa_events():
        if what in do:
            do[what](i, m)


MIX_TENSOR = (lru_tensor, ssd_tensor, swa_tensor, hgrn_tensor)
MIX_SCALAR = (lru_scalar, ssd_scalar, swa_scalar, hgrn_scalar)
MIX_VECTOR = (lru_vector, ssd_vector, swa_vector, hgrn_vector)
OUT_IN = ((LRU_T, 1, "lru_y_split", LRU_T), (SSD_T, 1, "ssd_y_split", SSD_T),
          (8, 1, "swa_y_split", 8), (HG_H, 1, "hgrn_y_split", HG_H))



LAYERS = (0, 1, 2, 3)


def program(nc, dram, layers):
    names = set()
    for l in layers:
        names |= {f"up{l}", f"down{l}"} | {f"{MIXER[l]}_{x}" for x in ("in", "out")}
    with ExitStack() as ctx:
        k = Core(nc, ctx, dram, names)
        words = {name: w for name, _, w in JOBS}
        jobs = [name for name, _, _ in JOBS if name in names]
        block = ctx.enter_context(nc.Block())

        @block.sync
        def _(sp):
            sp.dma_start(k.par[:, :], dram["params"]).then_inc(k.s("params_landed"), 16)
            sp.dma_start(k.con[:, :], dram["consts"]).then_inc(k.s("consts_landed"), 16)
            for o in range(DT):
                sp.dma_start(k.x[:, o, :], dram["x"][:, o, :]).then_inc(k.s("x_landed"), 16)
            for job in jobs:
                weights_sync(sp, k, job, words[job])
            sp.wait_ge(k.s("banks_free"), 4 + 2 * (k.pair0[f"down{layers[-1]}"] + DT))
            sp.dma_start(dram["out"], k.x[:, :, :]).then_inc(k.s("out_stored"), 16)
            sp.wait_ge(k.s("out_stored"), 16)

        @block.gpsimd
        def _(pool):
            for job in jobs:
                weights_gpsimd(pool, k, job, words[job])

        @block.tensor
        def _(pe):
            pe.wait_ge(k.s("consts_landed"), 16)
            for n, l in enumerate(layers):
                norm_tensor(pe, k, 2 * n)
                MIX_TENSOR[l](pe, k)
                out_tensor(pe, k, f"{MIXER[l]}_out", *OUT_IN[l])
                norm_tensor(pe, k, 2 * n + 1)
                up_tensor(pe, k, l)
                out_tensor(pe, k, f"down{l}", FF_T // 2, 2, "g_split", FF_T * (l + 1))

        @block.scalar
        def _(act):
            act.wait_ge(k.s("params_landed"), 16)
            act.wait_ge(k.s("x_landed"), 16 * DT)
            residual_scalar(act, k, 0, None)
            norm_scalar(act, k, 0)
            for l in layers:
                MIX_SCALAR[l](act, k)
                residual_scalar(act, k, 2 * l + 1, f"{MIXER[l]}_out")
                norm_scalar(act, k, 2 * l + 1)
                up_scalar(act, k, l)
                if l != layers[-1]:
                    residual_scalar(act, k, 2 * l + 2, f"down{l}")
                    norm_scalar(act, k, 2 * l + 2)

        @block.vector
        def _(dve):
            dve.memset(k.rstd[:, :], 0.0).then_inc(k.s("banks_free"), 4)
            dve.wait_ge(k.s("params_landed"), 16)
            dve.wait_ge(k.s("consts_landed"), 16)
            dve.wait_ge(k.s("x_landed"), 16 * DT)
            residual_vector(dve, k, 0, None)
            for l in layers:
                MIX_VECTOR[l](dve, k)
                residual_vector(dve, k, 2 * l + 1, f"{MIXER[l]}_out")
                up_vector(dve, k, l)
                residual_vector(dve, k, 2 * l + 2 if l != layers[-1] else None, f"down{l}", 2)


MIXER = ("lru", "ssd", "swa", "hgrn")


def panels(w, kt, groups):
    w = w.reshape(kt, P, -1)
    return np.stack([np.ascontiguousarray(w[:, :, g].transpose(1, 0, 2)).reshape(P, -1) for g in groups])


def span(*starts, width=P):
    return np.concatenate([np.arange(a, a + width) for a in starts])


def columns(v):
    return np.ascontiguousarray(np.asarray(v).reshape(-1, P).T)


def ssd_panels(w):
    x, B, C, dt = SSD_T * P, 2 * SSD_T * P, (2 * SSD_T + SSD_G) * P, (2 * SSD_T + 2 * SSD_G) * P
    first = panels(w, DT, [span(dt, dt, dt, width=SSD_DT)])
    first = np.pad(first, ((0, 0), (0, 0), (0, DT * 256 - first.shape[2])))
    groups = []
    for g in range(SSD_G):
        at = SSD_TG * P * g
        groups += [span(B + P * g, C + P * g)]
        groups += [span(x + at, width=2 * P), span(x + at + 2 * P, width=2 * P)]
        groups += [span(at, width=2 * P), span(at + 2 * P, width=2 * P)]
    return np.concatenate([first, panels(w, DT, groups)])


def swa_head_rows():
    return [span(64 * (8 * (t // 4) + t % 4), 64 * (8 * (t // 4) + t % 4 + 4), width=64) for t in range(8)]


def swa_table():
    i = np.arange(P)
    perm = np.zeros((P, P))
    for m in range(P):
        r = m % 64
        if r < ROT:
            perm[m + (8 if r < 8 else -8), m] = 1.0
    key = np.arange(256)
    later = (key > i[:, None]) & (key <= i[:, None] + P)
    masks = [np.where(ok, 0.0, -1e30) for ok in (key <= i[:, None], later, later)]
    freq = (np.float32(ROPE_THETA) ** (-np.arange(0, ROT, 2, dtype=np.float32) / np.float32(ROT))).astype(np.float32)
    angle = freq[:, None] * np.arange(S, dtype=np.float32)
    cos, sin = np.ones((P, S)), np.zeros((P, S))
    for m in range(P):
        r = m % 64
        if r < ROT:
            cos[m] = np.cos(angle[r % 8])
            sin[m] = np.sin(angle[r % 8]) * (-1.0 if r < 8 else 1.0)
    half = i[:, None] // 64 == i // 64
    return np.concatenate([half, perm, *masks, cos, sin], axis=1).astype(np.float32)


def hgrn_masks():
    s, l = np.arange(P)[:, None], np.arange(P)[None]
    m = [(s // (2 * B) == l // (2 * B)) & (s // B % 2 == 0) & (l // B % 2 == 1) for B in LEVELS]
    return np.stack(m, axis=1).astype(np.int32)


def layout(inputs):
    a = {n: np.asarray(v) for n, v in inputs.items()}
    out = {"x": a["x"][0].T.reshape(DT, P, S).transpose(1, 0, 2)}
    for l in range(DEPTH):
        out[f"up{l}"] = panels(a["ffn_w_up"][l], DT, [span(j * P, (FF_T + j) * P) for j in range(FF_T)])
        down = a["ffn_w_down"][l]
        half = FF_T // 2 * P
        parts = [panels(down[h * half:(h + 1) * half], FF_T // 2, [span(o * P) for o in range(DT)])
                 for h in range(2)]
        out[f"down{l}"] = np.stack(parts, 1).reshape(2 * DT, P, -1)
    w = panels(a["lru_w_in"][0], DT, [span(j * P, (LRU_T + j) * P) for j in range(LRU_T)])
    out["lru_in"] = np.concatenate([w, a["lru_w_gate"][0]], axis=2)
    out["lru_out"] = panels(a["lru_w_out"][0], LRU_T, [span(o * P) for o in range(DT)])
    par = {
        "eps": np.full((P, 1), EPS, np.float32),
        "mix_norm": columns(a["mix_norm"]), "ffn_norm": columns(a["ffn_norm"]),
        "ffn_conv_w": columns(a["ffn_conv_w"]), "ffn_conv_b": columns(a["ffn_conv_b"]),
        "lru_conv_w": columns(a["lru_conv_w"]), "lru_conv_b": columns(a["lru_conv_b"]),
        "lru_b_gate": columns(a["lru_b_gate"][0].reshape(LRU_T, 2, P).transpose(1, 0, 2)),
        "lru_lambda": columns(a["lru_lambda"]),
        "ssd_conv_w": columns(a["ssd_conv_w"]), "ssd_conv_b": columns(a["ssd_conv_b"]),
        "ssd_dt_bias": np.tile(a["ssd_dt_bias"][0], 4)[:, None], "ssd_a_log": np.tile(a["ssd_a_log"][0], 4)[:, None],
        "ssd_d": columns(np.repeat(a["ssd_d"][0], 64)), "ssd_norm": columns(a["ssd_norm"]),
        "swa_q_norm": np.tile(a["swa_q_norm"][0], 2)[:, None], "swa_k_norm": np.tile(a["swa_k_norm"][0], 2)[:, None],
        "swa_sinks": np.tile(a["swa_sinks"][0], (P, 1)),
        "hgrn_norm": a["hgrn_norm"][0][:, None],
        "hgrn_lower_bounds": columns(a["hgrn_lower_bounds"]),
    }
    out["params"] = np.concatenate([par[n] for n in PARAMS], axis=1)
    i = np.arange(P)
    const = {"ones": np.ones((P, P)), "ident": np.eye(P)}
    out["swa_table"] = swa_table()
    out["hgrn_masks"] = hgrn_masks()
    q = swa_head_rows()
    groups = [span(D, width=256), span(D + 256, width=256)]
    groups += [np.concatenate(q[2 * n:2 * n + 2]) for n in range(4)]
    out["swa_in"] = panels(a["swa_w_in"][0], DT, groups)
    out["swa_out"] = panels(a["swa_w_out"][0][np.concatenate(q)], DT, [span(o * P) for o in range(DT)])
    groups = []
    for h in range(HG_H):
        groups += [span(h * P, D + h * P), span(2 * D + h * P, 3 * D + h * P)]
    out["hgrn_in"] = panels(a["hgrn_w_in"][0], DT, groups)
    out["hgrn_out"] = panels(a["hgrn_w_out"][0], DT, [span(o * P) for o in range(DT)])
    out["consts"] = np.concatenate([np.asarray(const[n], np.float32) for n in CONSTS], axis=1)
    out["ssd_in"] = ssd_panels(a["ssd_w_in"][0])
    out["ssd_out"] = panels(a["ssd_w_out"][0], SSD_T, [span(o * P) for o in range(DT)])
    out["ssd_table"] = np.concatenate([
        np.tile((i == P - 1)[:, None], (1, P)),
        np.where(i[:, None] <= i, 0.0, -1e30),
        i[:, None] % SSD_DT == np.arange(SSD_DT),
        np.tile(np.arange(S) % P != 0, (P, 1)),
    ], axis=1).astype(np.float32)
    return out



def kernel(**inputs):
    import concourse.bacc as bacc
    from concourse.bass_utils import run_bass_kernel_spmd as run

    nc = bacc.Bacc("TRN2", target_bir_lowering=False, num_devices=1)
    arrays = {n: np.ascontiguousarray(v) for n, v in layout(inputs).items()
              if n not in {x for x, _, _ in JOBS} or any(n in (f"up{l}", f"down{l}") or n.startswith(MIXER[l]) for l in LAYERS)}
    dram = {n: nc.dram_tensor(f"in_{n}", v.shape, mybir.dt.from_np(v.dtype), kind="ExternalInput").ap()
            for n, v in arrays.items()}
    dram["out"] = nc.dram_tensor("out_x", (P, DT, S), F32, kind="ExternalOutput").ap()
    program(nc, dram, LAYERS)
    r = run(nc, [{f"in_{n}": v for n, v in arrays.items()}], core_ids=[0])
    y = r.results[0]["out_x"]
    return np.ascontiguousarray(y.transpose(2, 1, 0).reshape(1, S, D))
```

```python
from contextlib import ExitStack

import numpy as np

import concourse.bass as bass
from concourse import mybir

ALU = mybir.AluOpType
ACT = mybir.ActivationFunctionType
AX = mybir.AxisListType
F32 = mybir.dt.float32
BF16 = mybir.dt.bfloat16
I32 = mybir.dt.int32

P = 128
S = 512
D = 1024
DT = D // P
DEPTH = 4
EPS = 1e-6

FF_T = 2816 // P
LRU_T = 1280 // P
LRU_C = 8.0
SSD_T = 2048 // P
SSD_G = 4
SSD_TG = SSD_T // SSD_G
SSD_R = 8
NC = S // P
SWA_Q = 16
HG_H = 8

RING = 4
PANEL = 2304

JOBS = [("lru_in", LRU_T, 8 * 256 + 256), ("lru_out", DT, LRU_T * P)]
JOBS += [("up0", FF_T, 8 * 256), ("down0", 2 * DT, FF_T // 2 * P)]
JOBS += [("ssd_in", 1 + 5 * SSD_G, 8 * 256), ("ssd_out", DT, SSD_T * P)]
JOBS += [("up1", FF_T, 8 * 256), ("down1", 2 * DT, FF_T // 2 * P)]
JOBS += [("swa_in", 6, 8 * 256), ("swa_out", DT, 8 * P)]
JOBS += [("up2", FF_T, 8 * 256), ("down2", 2 * DT, FF_T // 2 * P)]
JOBS += [("hgrn_in", 2 * HG_H, 8 * 256), ("hgrn_out", DT, 8 * P)]
JOBS += [("up3", FF_T, 8 * 256), ("down3", 2 * DT, FF_T // 2 * P)]

PARAMS = {}


def _columns():
    at = 0
    for name, n in [("eps", 1), ("mix_norm", DEPTH * DT), ("ffn_norm", DEPTH * DT),
                    ("ffn_conv_w", DEPTH * 3 * 2 * FF_T), ("ffn_conv_b", DEPTH * 2 * FF_T),
                    ("lru_conv_w", 4 * LRU_T), ("lru_conv_b", LRU_T), ("lru_b_gate", 2 * LRU_T),
                    ("lru_lambda", LRU_T),
                    ("ssd_conv_w", 4 * 24), ("ssd_conv_b", 24), ("ssd_dt_bias", 1), ("ssd_a_log", 1),
                    ("ssd_d", SSD_T), ("ssd_norm", SSD_T),
                    ("swa_q_norm", 1), ("swa_k_norm", 1), ("swa_sinks", SWA_Q),
                    ("hgrn_norm", 1), ("hgrn_lower_bounds", DEPTH * HG_H)]:
        PARAMS[name] = (at, n)
        at += n
    return at


NPARAM = _columns()

CONSTS = {}


def _constants():
    at = 0
    for name, n in [("mean", P), ("ident", P)]:
        CONSTS[name] = (at, n)
        at += n
    return at


NCONST = _constants()
LEVELS = [1, 2, 4, 8, 16, 32, 64]


def steps(eng, lo, hi, unroll):
    full = (hi - lo) // unroll
    if full > 1:
        with eng.Fori(0, full) as i:
            for u in range(unroll):
                yield i * unroll + (lo + u), (lo + u) % unroll
    else:
        full = 0
    for j in range(lo + full * unroll, hi):
        yield j, j % unroll


class Core:

    def __init__(self, nc, ctx, dram, layers):
        self.nc, self.dram = nc, dram
        self._ctx = ctx
        sb = self.sb
        self.x = sb("x_resid", [P, DT, S])
        self.xh = sb("x_hi", [P, DT, S], BF16)
        self.xl = sb("x_lo", [P, DT, S], BF16)
        self.gh = sb("g_hi", [P, FF_T, S], BF16)
        self.gl = sb("g_lo", [P, FF_T, S], BF16)
        self.w = sb("w_panel", [P, RING, PANEL])
        self.wl = sb("w_lo", [P, RING, PANEL], BF16)
        self.rstd = sb("rstd", [P, S])
        self.factor = sb("inner_factor", [P, S])
        self.sq = sb("x_sq", [P, 2, S])
        self.sqsum = sb("x_sqsum", [P, S])
        self.par = sb("params", [P, NPARAM])
        self.con = sb("consts", [P, NCONST])
        self.arena = sb("arena", [P, 15850])
        self.ps = ctx.enter_context(nc.psum_tensor("psum", [P, 8, S], F32))
        self._sems = {}
        self.panel0, self.pair0, self.count, p, n = {}, {}, {}, 0, 0
        for name, count, _ in JOBS:
            if name not in layers:
                continue
            self.panel0[name], self.pair0[name] = p, n
            self.count[name] = count
            p += count
            n += count if not name.startswith("down") else count // 2

    def sb(self, name, shape, dt=F32):
        return self._ctx.enter_context(self.nc.sbuf_tensor(name, shape, dt))

    def s(self, name):
        if name not in self._sems:
            self._sems[name] = self._ctx.enter_context(self.nc.semaphore(name))
        return self._sems[name]

    def p(self, name, i=0):
        a, n = PARAMS[name]
        assert i < n if isinstance(i, int) else True
        return self.par[:, bass.ds(i + a, 1)]

    def c(self, name, lo=0, hi=None):
        a, n = CONSTS[name]
        return self.con[:, a + lo:a + (n if hi is None else hi)]

    def whi(self, slot, words=PANEL):
        v = self.w[:, slot, 0:words].bitcast(BF16)
        return v.rearrange("p (n two) -> p n two", two=2)[:, :, 1]

    def slot(self, job, u):
        return (self.panel0[job] + u) % RING

    def bank(self, job, u):
        return 2 * ((self.pair0[job] + u) % 2)



def weights_sync(sp, k, job, words):
    p0, n = k.panel0[job], k.count[job]
    lo = 0
    if p0 == 0:
        for j in range(1, RING):
            sp.dma_start(k.w[:, j, 0:words], k.dram[job][j]).then_inc(k.s(f"panel_landed{j}"), 16)
        lo = RING
    for j, u in steps(sp, lo, n, RING):
        slot = k.slot(job, u)
        sp.wait_ge(k.s("panel_used"), j + (p0 - RING + 1))
        sp.dma_start(k.w[:, slot, 0:words],
                     k.dram[job][bass.ds(j, 1), :, :].rearrange("a p w -> p (a w)")
                     ).then_inc(k.s(f"panel_landed{slot}"), 16)


def weights_gpsimd(pool, k, job, words):
    p0, n = k.panel0[job], k.count[job]
    if p0 == 0:
        pool.wait_ge(k.s("panel_landed0"), 16)
        pool.tensor_tensor(k.wl[:, 0, words // 2:words], k.w[:, 0, words // 2:words],
                           k.whi(0, words)[:, words // 2:], ALU.subtract).then_inc(k.s("panel_split"), 1)
    for j, u in steps(pool, int(p0 == 0), n, RING):
        slot = k.slot(job, u)
        pool.wait_ge(k.s(f"panel_landed{slot}"), (j + (p0 - slot)) * (16 // RING) + 16)
        pool.tensor_tensor(k.wl[:, slot, 0:words], k.w[:, slot, 0:words], k.whi(slot, words),
                           ALU.subtract).then_inc(k.s("panel_split"), 1)


def first_lo(dve, k, words):
    dve.wait_ge(k.s("first_landed"), 16)
    dve.tensor_tensor(k.wl[:, 0, 0:words // 2], k.w[:, 0, 0:words // 2], k.whi(0, words // 2),
                      ALU.subtract).then_inc(k.s("first_lo"), 1)


def product(pe, out, wh, wl, ah, al, start, stop):
    pe.matmul(out, wh, ah, start=start, stop=False)
    pe.matmul(out, wh, al, start=False, stop=False)
    return pe.matmul(out, wl, ah, start=False, stop=stop)


def gemm_tile(pe, k, bank, slot, kt, nb, col, hi, lo, k0=0, k1=None, m=P, fresh=None):
    wh, wl = k.whi(slot), k.wl[:, slot, :]
    for q in range(k0, kt if k1 is None else k1):
        if fresh is not None:
            pe.wait_ge(k.s("x_split"), DT * fresh + q + 1)
        a = q * nb + col
        last = product(pe, k.ps[0:m, bank, :], wh[:, a:a + m], wl[:, a:a + m],
                       hi[:, q, :], lo[:, q, :], q == 0, q == kt - 1)
    return last



def gain(k, c, o):
    return k.p("ffn_norm" if c % 2 else "mix_norm", o + DT * (c // 2))


def out_bank(k, job, o):
    return (2 * (k.pair0[job] % 2) + o) % 4


def out_begin(pe, k, job, o):
    pe.wait_ge(k.s("panel_split"), k.panel0[job] + o + 1)
    pe.wait_ge(k.s("banks_free"), 2 * k.pair0[job] + (2 * o - 2 if o >= 4 else 2 if o < 2 else 4))


def out_early(pe, k, job, kt, o, k0, k1):
    if k0 == 0:
        out_begin(pe, k, job, o)
    gemm_tile(pe, k, out_bank(k, job, o), k.slot(job, o), kt, P, 0, k.gh, k.gl, k0, k1)


def out_tensor(pe, k, job, kt, early, early_k, ready):
    pe.wait_ge(k.s(ready), kt)
    for o in range(DT):
        if o >= early:
            out_begin(pe, k, job, o)
        gemm_tile(pe, k, out_bank(k, job, o), k.slot(job, o), kt, P, 0, k.gh, k.gl,
                  early_k if o < early else 0).then_inc(k.s("panel_used"), 1)


def down_tensor(pe, k, l):
    job, half = f"down{l}", FF_T // 2
    p0, n0 = k.panel0[job], k.pair0[job]
    for o, u in steps(pe, 0, DT // 2, 2):
        for h in range(2):
            pe.wait_ge(k.s("g_split"), FF_T * l + half * (h + 1))
            for t in range(2):
                slot, bank = k.slot(job, 2 * h + t), out_bank(k, job, 2 * u + t)
                pe.wait_ge(k.s("panel_split"), o * 4 + (p0 + 2 * h + t + 1))
                if h == 0:
                    pe.wait_ge(k.s("banks_free"), o * 4 + (2 * n0 + 2 + 2 * t))
                wh, wl = k.whi(slot), k.wl[:, slot, :]
                for q in range(half):
                    a, g = q * P, h * half + q
                    mm = product(pe, k.ps[:, bank, :], wh[:, a:a + P], wl[:, a:a + P], k.gh[:, g, :],
                                 k.gl[:, g, :], g == 0, g == FF_T - 1)
                mm.then_inc(k.s("panel_used"), 1)


def residual_scalar(act, k, c, job):
    for o, u in steps(act, 0, DT, 2) if job is not None else ((o, o % 2) for o in range(DT)):
        if job is not None:
            act.wait_ge(k.s("banks_free"), o * 2 + (4 + 2 * k.pair0[job] + 2))
        else:
            act.wait_ge(k.s(f"x{o}_landed"), 16)
            if o >= 2:
                act.wait_ge(k.s("sq_summed"), o)
        act.activation(tile(k.xh, o), tile(k.x, o), ACT.Identity, scale=gain(k, c, o)
                       ).then_inc(k.s("x_hi"), 1)
        act.activation(k.sq[:, u % 2, :], tile(k.x, o), ACT.Square).then_inc(k.s("x_squared"), 1)


def residual_vector(dve, k, c, job, down=False):
    if c is not None:
        dve.memset(k.sqsum[:, :], 0.0).then_inc(k.s("sq_summed"), 1)
    for o, u in steps(dve, 0, DT, 4) if job is not None else ((o, o % 4) for o in range(DT)):
        if job is None:
            dve.wait_ge(k.s(f"x{o}_landed"), 16)
        else:
            dve.wait_ge(k.s("panel_used"), (o * 2 + (k.panel0[job] + (2 if u % 2 else 3)) if down
                                            else o + (k.panel0[job] + 1)))
            dve.tensor_tensor(tile(k.x, o), tile(k.x, o), k.ps[:, out_bank(k, job, u), :], ALU.add
                              ).then_inc(k.s("banks_free"), 2)
        if c is None:
            continue
        dve.wait_ge(k.s("x_hi"), o + (DT * c + 1))
        if job is not None:
            dve.wait_ge(k.s("banks_free"), o * 2 + (4 + 2 * k.pair0[job] + 2))
        dve.scalar_tensor_tensor(tile(k.xl, o), tile(k.x, o), gain(k, c, o), tile(k.xh, o),
                                 ALU.mult, ALU.subtract).then_inc(k.s("x_split"), 1)
        dve.wait_ge(k.s("x_squared"), o + (DT * c + 1))
        dve.wait_ge(k.s("sq_summed"), o + ((DT + 1) * c + 1))
        dve.tensor_tensor(k.sqsum[:, :], k.sqsum[:, :], k.sq[:, u % 2, :], ALU.add
                          ).then_inc(k.s("sq_summed"), 1)


def inverse_root(act, k, out, mean, name, n):
    act.activation(out, mean, ACT.Ln, bias=k.p("eps")).then_inc(k.s(name + "_log"), 1)
    act.wait_ge(k.s(name + "_log"), n)
    act.activation(out, out, ACT.Exp, scale=-0.5).then_inc(k.s(name), 1)


def norm_scalar(act, k, c):
    act.wait_ge(k.s("norm_summed"), c + 1)
    inverse_root(act, k, k.rstd[:, :], k.ps[:, 4, :], "rstd", c + 1)


def norm_vector(dve, k, c):
    dve.wait_ge(k.s("rstd"), c + 1)


def mean_scale(features):
    return float(np.sqrt(D / features))


def norm_tensor(pe, k, c):
    if c == 0:
        pe.wait_ge(k.s("consts_landed"), 16)
    pe.wait_ge(k.s("sq_summed"), (DT + 1) * (c + 1))
    pe.matmul(k.ps[:, 4, :], k.c("mean"), k.sqsum[:, :], start=True, stop=True
              ).then_inc(k.s("norm_summed"), 1)


def tile(t, o):
    return t[:, bass.ds(o, 1), :].rearrange("p a s -> p (a s)")



class FfnBuffers:
    def __init__(self, k):
        a = Arena(k)
        self.raw = a.take(2, 2, S + 2)
        self.conv = a.take(2, 2, S)


class Chain:

    def __init__(self, eng, k, name):
        self.eng, self.k, self.name, self.n = eng, k, name, 0

    def __call__(self, ins):
        self.n += 1
        ins.then_inc(self.k.s(self.name), 1)
        self.eng.wait_ge(self.k.s(self.name), self.n)


class Arena:
    def __init__(self, k, at=0):
        self.k, self.at = k, at

    def take(self, *shape, dt=F32):
        n = int(np.prod(shape))
        words = n if dt != BF16 else (n + 1) // 2
        v = self.k.arena[:, self.at:self.at + words]
        self.at += words
        assert self.at <= self.k.arena.shape[1], self.at
        if dt != F32:
            v = v.bitcast(dt)
        if len(shape) == 1:
            return v
        names = "abcd"[:len(shape)]
        return v.rearrange("p (%s) -> p %s" % (" ".join(names), " ".join(names)),
                           **{n: s for n, s in zip(names, shape)})


def up_tensor(pe, k, l):
    job = f"up{l}"
    p0, n0 = k.panel0[job], k.pair0[job]

    def pair(j, u, first):
        slot, bank = k.slot(job, u), k.bank(job, u)
        pe.wait_ge(k.s("panel_split"), j + (p0 + 1))
        pe.wait_ge(k.s("banks_free"), j * 2 + (2 * n0 + 2))
        gemm_tile(pe, k, bank, slot, DT, 256, 0, k.xh, k.xl, fresh=2 * l + 1 if first else None)
        if first:
            norm_tensor(pe, k, 2 * l + 1)
        gemm_tile(pe, k, bank + 1, slot, DT, 256, P, k.xh, k.xl).then_inc(k.s("panel_used"), 1)

    pair(0, 0, True)
    pair(1, 1, False)
    for j, u in steps(pe, 2, FF_T, RING):
        pair(j, u, False)


def up_scalar(act, k, l):
    b = FfnBuffers(k)
    n0 = k.pair0[f"up{l}"]
    for j, u in steps(act, 0, FF_T, 2):
        for half in (1, 0):
            act.wait_ge(k.s("banks_free"), j * 2 + (4 + 2 * n0 + 2 - half))
            act.activation(b.conv[:, u, half, :], b.raw[:, u, half, 2:], ACT.Identity,
                           bias=k.p("ffn_conv_b", j + (l * 2 * FF_T + half * FF_T)),
                           scale=k.p("ffn_conv_w", j + ((l * 3 + 2) * 2 * FF_T + half * FF_T))
                           ).then_inc(k.s("ffn_biased"), 1)
        act.wait_ge(k.s("ffn_tapped"), j * 4 + (4 * FF_T * l + 3))
        act.activation(b.conv[:, u, 1, :], b.conv[:, u, 1, :], ACT.Silu).then_inc(k.s("ffn_silu"), 1)
        act.wait_ge(k.s("ffn_gated"), j + (FF_T * l + 1))
        act.activation(tile(k.gh, j), b.conv[:, u, 0, :], ACT.Copy).then_inc(k.s("ffn_hi"), 1)


def up_vector(dve, k, l):
    b = FfnBuffers(k)
    job = f"up{l}"
    p0 = k.panel0[job]
    dve.memset(b.raw[:, :, :, 0:2], 0.0).then_inc(k.s("ffn_padded"), 1)
    dve.wait_ge(k.s("ffn_padded"), l + 1)
    norm_vector(dve, k, 2 * l + 1)
    for j, u in steps(dve, 0, FF_T, 2):
        bank = k.bank(job, u)
        dve.wait_ge(k.s("panel_used"), j + (p0 + 1))
        for half in (1, 0):
            dve.tensor_tensor(b.raw[:, u, half, 2:], k.ps[:, bank + half, :], k.rstd[:, :], ALU.mult
                              ).then_inc(k.s("banks_free"), 1)
        for tap in (1, 0):
            for half in (1, 0):
                if tap == 1:
                    dve.wait_ge(k.s("ffn_biased"), j * 2 + (2 * FF_T * l + 2 - half))
                else:
                    dve.wait_ge(k.s("ffn_tapped"), j * 4 + (4 * FF_T * l + 2 - half))
                dve.scalar_tensor_tensor(
                    b.conv[:, u, half, :], b.raw[:, u, half, tap:tap + S],
                    k.p("ffn_conv_w", j + ((l * 3 + tap) * 2 * FF_T + half * FF_T)),
                    b.conv[:, u, half, :], ALU.mult, ALU.add).then_inc(k.s("ffn_tapped"), 1)
        dve.wait_ge(k.s("ffn_tapped"), j * 4 + (4 * FF_T * l + 4))
        dve.wait_ge(k.s("ffn_silu"), j + (FF_T * l + 1))
        dve.tensor_tensor(b.conv[:, u, 0, :], b.conv[:, u, 0, :], b.conv[:, u, 1, :], ALU.mult
                          ).then_inc(k.s("ffn_gated"), 1)
        dve.wait_ge(k.s("ffn_hi"), j + (FF_T * l + 1))
        dve.tensor_tensor(tile(k.gl, j), b.conv[:, u, 0, :], tile(k.gh, j), ALU.subtract
                          ).then_inc(k.s("g_split"), 1)



def softplus_scalar(act, k, name, n_abs, e):
    act.wait_ge(k.s(name), 2)
    act.activation(e, n_abs, ACT.Exp, scale=-1.0).then_inc(k.s(name + "_exp"), 1)


def softplus_vector(dve, k, name, x, size, e, z, out):
    chained = Chain(dve, k, name)
    chained(dve.tensor_scalar(out, x, 0.0, None, ALU.max))
    chained(dve.scalar_tensor_tensor(size, x, -1.0, x, ALU.mult, ALU.max))
    dve.wait_ge(k.s(name + "_exp"), 1)
    chained(dve.tensor_scalar(z, e, 2.0, None, ALU.add))
    chained(dve.reciprocal(z, z))
    chained(dve.tensor_tensor(z, e, z, ALU.mult))
    chained(dve.tensor_tensor(e, z, z, ALU.mult))
    chained(dve.tensor_scalar(size, e, 1.0 / 17, None, ALU.mult))
    for odd in (15, 13, 11, 9, 7, 5, 3):
        chained(dve.scalar_tensor_tensor(size, size, 1.0 / odd, e, ALU.add, ALU.mult))
    chained(dve.scalar_tensor_tensor(size, size, 1.0, z, ALU.add, ALU.mult))
    chained(dve.scalar_tensor_tensor(out, size, 2.0, out, ALU.mult, ALU.add))



class LruBuffers:
    def __init__(self, k):
        a = Arena(k)
        self.gate = a.take(2, S)
        self.inner = a.take(2, S)
        self.raw = a.take(2, S + 3)
        self.conv = a.take(2, S)
        self.conv_hi = a.take(2, S, dt=BF16)
        self.conv_lo = a.take(2, S, dt=BF16)
        self.tanh_r, self.tanh_i, self.a, self.th, self.s, self.wu, self.h = (a.take(S) for _ in range(7))
        self.half_rate = a.take(LRU_T)
        self.neg_half_rate = a.take(LRU_T)
        self.half_bias = a.take(2 * LRU_T)
        self.nlam, self.t0, self.t1, self.t2, self.t3 = (a.take(LRU_T) for _ in range(5))


GELU_A = float(np.sqrt(2.0 / np.pi))
GELU_B = GELU_A * 0.044715


def lru_tensor(pe, k):
    b = LruBuffers(k)
    job, T = "lru_in", LRU_T
    p0, n0 = k.panel0[job], k.pair0[job]

    def project(j, u):
        slot, bank = k.slot(job, u), k.bank(job, u)
        if isinstance(j, int) and j == 0:
            pe.wait_ge(k.s("first_lo"), 1)
            pe.wait_ge(k.s("banks_free"), 2)
            gemm_tile(pe, k, bank, slot, DT, 256, 0, k.xh, k.xl, 0, DT // 2, fresh=0)
            pe.wait_ge(k.s("panel_split"), 1)
            gemm_tile(pe, k, bank, slot, DT, 256, 0, k.xh, k.xl, DT // 2, DT, fresh=0)
            norm_tensor(pe, k, 0)
        else:
            pe.wait_ge(k.s("panel_split"), j + (p0 + 1))
            pe.wait_ge(k.s("banks_free"), j * 2 + (2 * n0 + 2))
            gemm_tile(pe, k, bank, slot, DT, 256, 0, k.xh, k.xl)
        gemm_tile(pe, k, bank + 1, slot, DT, 256, P, k.xh, k.xl).then_inc(k.s("lru_projected"), 1)

    def gates(j, u, first):
        slot = k.slot(job, u)
        pe.wait_ge(k.s("lru_conv_split"), j + 1)
        if not first:
            pe.wait_ge(k.s("lru_gates_read"), j * 2)
        for half in range(2):
            a = DT * 256 + half * P
            product(pe, k.ps[:, 5 + half, :], k.whi(slot)[:, a:a + P], k.wl[:, slot, a:a + P],
                    b.conv_hi[:, u % 2, :], b.conv_lo[:, u % 2, :], True, True
                    ).then_inc(k.s("panel_used" if half else "lru_r_done"), 1)

    project(0, 0)
    project(1, 1)
    gates(0, 0, True)
    for j, u in steps(pe, 2, T, RING):
        project(j, u)
        gates(j - 1, (u - 1) % RING, False)
    early_k = OUT_IN[0][2]
    pe.wait_ge(k.s("lru_y_split"), early_k)
    out_early(pe, k, "lru_out", T, 0, 0, early_k)
    gates(T - 1, (T - 1) % RING, False)
    out_early(pe, k, "lru_out", T, 1, 0, early_k)


def lru_scalar(act, k):
    b = LruBuffers(k)
    n0, p0 = k.pair0["lru_in"], k.panel0["lru_in"]
    softplus_scalar(act, k, "lru_softplus", b.t0, b.t1)

    def decay(j):
        act.wait_ge(k.s("lru_r_done"), j + 1)
        act.activation(b.tanh_r, k.ps[:, 5, :], ACT.Tanh, bias=b.half_bias[:, bass.ds(j, 1)], scale=0.5
                       ).then_inc(k.s("lru_gates_read"), 1)
        act.wait_ge(k.s("panel_used"), j + (p0 + 1))
        act.activation(b.tanh_i, k.ps[:, 6, :], ACT.Tanh, bias=b.half_bias[:, bass.ds(j + LRU_T, 1)],
                       scale=0.5).then_inc(k.s("lru_gates_read"), 1)
        act.wait_ge(k.s("lru_gates_read"), j * 2 + 1)
        rate, neg = b.half_rate[:, bass.ds(j, 1)], b.neg_half_rate[:, bass.ds(j, 1)]
        act.activation(b.a, b.tanh_r, ACT.Exp, bias=rate, scale=rate).then_inc(k.s("lru_decay"), 1)
        act.activation(b.th, b.tanh_r, ACT.Tanh, bias=neg, scale=neg).then_inc(k.s("lru_decay"), 1)

    def unit(j, u, conv, rec):
        if conv:
            act.wait_ge(k.s("banks_free"), j * 2 + (4 + 2 * n0 + 1))
            act.activation(b.inner[:, u, :], b.gate[:, u, :], ACT.Square).then_inc(k.s("lru_gate_sq"), 1)
            act.wait_ge(k.s("banks_free"), j * 2 + (4 + 2 * n0 + 2))
            act.activation(b.conv[:, u, :], b.raw[:, u, 3:], ACT.Identity, bias=k.p("lru_conv_b", j),
                           scale=k.p("lru_conv_w", j + 3 * LRU_T)).then_inc(k.s("lru_biased"), 1)
        if rec:
            decay(j - 1)
        if conv:
            act.wait_ge(k.s("lru_inner"), j * 2 + 2)
            act.activation(b.inner[:, u, :], b.inner[:, u, :], ACT.Tanh).then_inc(k.s("lru_gate_tanh"), 1)
            act.wait_ge(k.s("lru_tapped"), j * 3 + 3)
            act.activation(b.conv_hi[:, u, :], b.conv[:, u, :], ACT.Copy).then_inc(k.s("lru_conv_hi"), 1)
        if rec:
            r = j - 1
            act.wait_ge(k.s("lru_s"), r * 2 + 2)
            act.activation(b.s, b.s, ACT.Sqrt).then_inc(k.s("lru_root"), 1)
            act.wait_ge(k.s("lru_y"), r * 3 + 3)
            act.activation(tile(k.gh, r), b.h, ACT.Copy).then_inc(k.s("lru_y_hi"), 1)

    act.wait_ge(k.s("lru_constants"), 3)
    unit(0, 0, True, False)
    for j, u in steps(act, 1, LRU_T, 2):
        unit(j, u, True, True)
    unit(LRU_T, LRU_T % 2, False, True)


def lru_vector(dve, k):
    b = LruBuffers(k)
    job = "lru_in"
    dve.tensor_scalar(b.nlam, k.par[:, PARAMS["lru_lambda"][0]:PARAMS["lru_lambda"][0] + LRU_T], -1.0, None,
                      ALU.mult).then_inc(k.s("lru_nlam"), 1)
    dve.wait_ge(k.s("lru_nlam"), 1)
    softplus_vector(dve, k, "lru_softplus", b.nlam, b.t0, b.t1, b.t2, b.t3)
    dve.tensor_scalar(b.half_rate, b.t3, -LRU_C / 2, None, ALU.mult).then_inc(k.s("lru_constants"), 1)
    dve.tensor_scalar(b.neg_half_rate, b.t3, LRU_C / 2, None, ALU.mult).then_inc(k.s("lru_constants"), 1)
    bias0 = PARAMS["lru_b_gate"][0]
    dve.tensor_scalar(b.half_bias, k.par[:, bias0:bias0 + 2 * LRU_T], 0.5, None, ALU.mult
                      ).then_inc(k.s("lru_constants"), 1)
    dve.memset(b.raw[:, :, 0:3], 0.0).then_inc(k.s("lru_padded"), 1)
    dve.wait_ge(k.s("lru_padded"), 1)
    norm_vector(dve, k, 0)

    def unit(j, u, conv, rec):
        r, v = j - 1, 1 - u
        if conv:
            bank = k.bank(job, u)
            dve.wait_ge(k.s("lru_projected"), j + 1)
            dve.tensor_tensor(b.gate[:, u, :], k.ps[:, bank, :], k.rstd[:, :], ALU.mult
                              ).then_inc(k.s("banks_free"), 1)
            dve.tensor_tensor(b.raw[:, u, 3:], k.ps[:, bank + 1, :], k.rstd[:, :], ALU.mult
                              ).then_inc(k.s("banks_free"), 1)
            dve.wait_ge(k.s("lru_gate_sq"), j + 1)
            dve.tensor_scalar(b.inner[:, u, :], b.inner[:, u, :], GELU_B, GELU_A, ALU.mult, ALU.add
                              ).then_inc(k.s("lru_inner"), 1)
            dve.wait_ge(k.s("lru_inner"), j * 2 + 1)
            dve.tensor_tensor(b.inner[:, u, :], b.inner[:, u, :], b.gate[:, u, :], ALU.mult
                              ).then_inc(k.s("lru_inner"), 1)
            dve.wait_ge(k.s("lru_biased"), j + 1)
            for n, tap in enumerate((2, 1, 0)):
                if n:
                    dve.wait_ge(k.s("lru_tapped"), j * 3 + n)
                dve.scalar_tensor_tensor(b.conv[:, u, :], b.raw[:, u, tap:tap + S],
                                         k.p("lru_conv_w", j + tap * LRU_T), b.conv[:, u, :],
                                         ALU.mult, ALU.add).then_inc(k.s("lru_tapped"), 1)
        if rec:
            dve.wait_ge(k.s("lru_decay"), r * 2 + 1)
            dve.tensor_tensor(b.s, b.a, b.a, ALU.mult).then_inc(k.s("lru_s"), 1)
            dve.wait_ge(k.s("lru_decay"), r * 2 + 2)
            dve.wait_ge(k.s("lru_s"), r * 2 + 1)
            dve.scalar_tensor_tensor(b.s, b.s, 1.0, b.th, ALU.add, ALU.mult).then_inc(k.s("lru_s"), 1)
            dve.scalar_tensor_tensor(b.wu, b.tanh_i, 1.0, b.conv[:, v, :], ALU.add, ALU.mult
                                     ).then_inc(k.s("lru_gated"), 1)
        if conv:
            dve.wait_ge(k.s("lru_tapped"), j * 3 + 3)
            dve.wait_ge(k.s("lru_conv_hi"), j + 1)
            dve.tensor_tensor(b.conv_lo[:, u, :], b.conv[:, u, :], b.conv_hi[:, u, :], ALU.subtract
                              ).then_inc(k.s("lru_conv_split"), 1)
        if rec:
            dve.wait_ge(k.s("lru_gated"), r + 1)
            dve.wait_ge(k.s("lru_root"), r + 1)
            dve.scalar_tensor_tensor(b.wu, b.wu, 0.5, b.s, ALU.mult, ALU.mult).then_inc(k.s("lru_y"), 1)
            dve.wait_ge(k.s("lru_y"), r * 3 + 1)
            dve.tensor_tensor_scan(b.h, b.a, b.wu, 0.0, ALU.mult, ALU.add).then_inc(k.s("lru_y"), 1)
        if conv:
            dve.wait_ge(k.s("lru_gate_tanh"), j + 1)
            dve.scalar_tensor_tensor(b.gate[:, u, :], b.inner[:, u, :], 1.0, b.gate[:, u, :],
                                     ALU.add, ALU.mult).then_inc(k.s("lru_gelu"), 1)
        if rec:
            dve.wait_ge(k.s("lru_y"), r * 3 + 2)
            dve.wait_ge(k.s("lru_gelu"), r + 1)
            dve.scalar_tensor_tensor(b.h, b.gate[:, v, :], 0.5, b.h, ALU.mult, ALU.mult
                                     ).then_inc(k.s("lru_y"), 1)
            dve.wait_ge(k.s("lru_y"), r * 3 + 3)
            dve.wait_ge(k.s("lru_y_hi"), r + 1)
            dve.tensor_tensor(tile(k.gl, r), b.h, tile(k.gh, r), ALU.subtract
                              ).then_inc(k.s("lru_y_split"), 1)

    unit(0, 0, True, False)
    for j, u in steps(dve, 1, LRU_T, 2):
        unit(j, u, True, True)
    unit(LRU_T, LRU_T % 2, False, True)





SSD_DT = 32
SSD_ROWS = 3 * SSD_DT


class SsdBuffers:
    def __init__(self, k):
        a = Arena(k)
        self.x = a.take(2, SSD_TG, S)
        self.bc = a.take(2, 2, S)
        self.z = a.take(SSD_TG, S)
        self.xdt = a.take(NC, S)
        self.xw = a.take(2, S)
        self.raw = a.take(2, S + 3)
        self.prev = a.take(NC - 1, S)
        self.cs_t, self.dt_t, self.end_w, self.dec = (a.take(NC, SSD_DT) for _ in range(4))
        self.pick = a.take(SSD_R, P, dt=BF16)
        self.pick_pair = a.take(SSD_R * 64, dt=BF16)
        self.cs3 = a.take(S, dt=BF16)
        self.ident, self.mask = a.take(P, dt=BF16), a.take(P, dt=BF16)
        self.table = a.take(P + P + SSD_DT)
        self.last_row, self.mask32 = self.table[:, 0:P], self.table[:, P:2 * P]
        self.pick32 = self.table[:, 2 * P:2 * P + SSD_DT]
        t = Arena(k, SSD_TG * S)
        self.dtx, self.size, self.e, self.q = (t.take(S) for _ in range(4))
        t = Arena(k, 2 * SSD_TG * S + 2 * S)
        self.dt, self.start = t.take(S), t.take(S)
        gh = k.gh[:, SSD_T:, :].bitcast(F32).rearrange("p a s -> p (a s)")
        gl = k.gl[:, SSD_T:, :].bitcast(F32).rearrange("p a s -> p (a s)")
        self.m = gh[:, 0:2 * S].rearrange("p (a s) -> p a s", a=2)
        self.cb = gh[:, 2 * S:3 * S]
        self.ecs = gl[:, 0:384]
        self.off = gl[:, 384:768]
        self.b_t = gl[:, 768:1152]
        self.ncs3 = gl[:, 1152:1408].bitcast(BF16)
        self.pick3 = gl[:, 1408:1408 + SSD_DT // 2].bitcast(BF16)
        self.ea = gl[0:SSD_ROWS, 1424:1425]


def heads_of(t, c, g):
    return t[:, c, SSD_R * g:SSD_R * (g + 1)].unsqueeze(2).to_broadcast([P, SSD_R, 64])


def by_head(t):
    return t.rearrange("p (h d) -> p h d", d=64)


SSD_EARLY, SSD_EARLY_K = 4, (SSD_G - 1) * SSD_TG


def ssd_events():
    ev = [("dt", 0, 0)]
    last = None
    for g in range(SSD_G):
        for i in range(10):
            if g > 0 and 2 * i < SSD_R:
                ev += [("tile", g, (i, 0, 2)), ("seg", g - 1, 2 * i), ("tile", g, (i, 2, 4)),
                       ("seg", g - 1, 2 * i + 1), ("tile", g, (i, 4, DT))]
            else:
                ev.append(("tile", g, (i, 0, DT)))
            if last is not None:
                ev.append(("conv", *last))
            last = (g, i)
            if g > 0 and 2 * i < SSD_R:
                ev += [("out", g - 1, 2 * i), ("out", g - 1, 2 * i + 1)]
            if i == 4 and g > 0:
                ev.append(("norm", g - 1, 0))
            if i in (5, 6) and g == 0:
                ev.append(("decays", 0, i - 5))
            if i == 7:
                ev.append(("turn", g, 0))
                ev += [("finish", g - 1, 0)] if g else []
            if i >= 8:
                ev.append(("states", g, i - 8))
    ev.append(("conv", *last))
    g = SSD_G - 1
    for r in range(0, SSD_R, 2):
        ev += [("seg", g, r), ("early", g, r), ("seg", g, r + 1), ("early", g, r + 1)]
        ev += [("out", g, r), ("out", g, r + 1)]
    ev += [("early", g, SSD_R + n) for n in range(4)]
    ev += [("norm", g, 0), ("finish", g, 0)]
    return ev + [("early", g, SSD_R + 4 + n) for n in range(4)]


def ssd_tensor(pe, k):
    b = SsdBuffers(k)
    job = "ssd_in"
    p0, n0 = k.panel0[job], k.pair0[job]
    chunk = [slice(c * P, (c + 1) * P) for c in range(NC)]

    def dt(g, i):
        pe.wait_ge(k.s("panel_split"), p0 + 1)
        pe.wait_ge(k.s("banks_free"), 2 * n0 + 2)
        gemm_tile(pe, k, k.bank(job, 0), k.slot(job, 0), DT, SSD_ROWS, 0, k.xh, k.xl, m=SSD_ROWS,
                  fresh=2).then_inc(k.s("panel_used"), 1)
        norm_tensor(pe, k, 2)

    def tile_(g, part):
        i, k0, k1 = part
        n = 1 + 5 * g + i // 2
        if k0 == 0:
            if i % 2 == 0:
                pe.wait_ge(k.s("panel_split"), p0 + n + 1)
            pe.wait_ge(k.s("banks_free"), 2 * (n0 + n) + i % 2 + 1)
        mm = gemm_tile(pe, k, ssd_bank(k, g, i), k.slot(job, n), DT, 256, P * (i % 2), k.xh, k.xl, k0, k1)
        if k1 == DT:
            mm.then_inc(k.s("panel_used" if i % 2 else "ssd_tile"), 1)

    def early(g, n):
        if n == 0:
            pe.wait_ge(k.s("ssd_y_split"), SSD_EARLY_K)
        o, k0 = divmod(3 * n, SSD_EARLY_K)
        out_early(pe, k, "ssd_out", SSD_T, o, k0, k0 + 3)

    def decays(g, part):
        if part:
            pe.wait_ge(k.s("ssd_dt_t"), 2)
            pe.matmul(k.ps[:, 6, 0:P], b.last_row, b.cs_t.rearrange("p c h -> p (c h)"), start=True, stop=True
                      ).then_inc(k.s("ssd_ends"), 1)
            return
        pe.wait_ge(k.s("ssd_cs"), 1)
        for c in range(NC):
            pe.transpose(k.ps[:, 5, c * SSD_DT:(c + 1) * SSD_DT], b.dtx[0:SSD_DT, chunk[c]],
                         k.c("ident")[0:SSD_DT, 0:SSD_DT])
            mm = pe.transpose(k.ps[:, 5, (NC + c) * SSD_DT:(NC + c + 1) * SSD_DT], b.dt[0:SSD_DT, chunk[c]],
                              k.c("ident")[0:SSD_DT, 0:SSD_DT])
        mm.then_inc(k.s("ssd_turned_dt"), 1)

    def turn(g, _):
        if g == 0:
            pe.wait_ge(k.s("rstd_log"), 3)
            pe.wait_ge(k.s("ssd_decays"), 2)
        pe.wait_ge(k.s("ssd_silu"), 6 * g + 6)
        for c in range(NC):
            if c >= 2:
                pe.wait_ge(k.s("ssd_xdt"), NC * g + c - 1)
            for t in range(SSD_TG):
                mm = pe.transpose(k.ps[:, 5 + c % 2, t * P:(t + 1) * P], b.x[:, g % 2, t, chunk[c]],
                                  k.c("ident"))
            mm.then_inc(k.s("ssd_turned_x"), 1)
        if g:
            pe.wait_ge(k.s("ssd_rstd_log"), g)
            pe.wait_ge(k.s("ssd_y"), SSD_TG * g)
        for c in range(NC - 1):
            mm = pe.transpose(k.ps[:, 7, chunk[c]], b.bc[:, g % 2, 0, chunk[c]], k.c("ident"))
        mm.then_inc(k.s("ssd_turned_b"), 1)
        for c in range(NC):
            mm = pe.matmul(k.ps[:, 4, chunk[c]], b.bc[:, g % 2, 0, chunk[c]], b.bc[:, g % 2, 1, chunk[c]],
                           start=True, stop=True)
        mm.then_inc(k.s("ssd_cb_done"), 1)

    def states(g, part):
        for c in ((0, 1), (2,))[part]:
            pe.wait_ge(k.s("ssd_xw"), 3 * g + c + 1)
            if c == 0:
                pe.wait_ge(k.s("ssd_b_t"), g + 1)
                pe.wait_ge(k.s("ssd_xdt"), NC * (g + 1))
            if c == 2:
                pe.wait_ge(k.s("ssd_prev"), 5 * g + 1)
            pe.matmul(k.ps[:, 5 + c % 2, :], b.b_t[:, chunk[c]], b.xw[:, c % 2, :],
                      start=True, stop=True).then_inc(k.s("ssd_state"), 1)

    def seg(g, r):
        h = SSD_R * g + r
        if r < 2:
            pe.wait_ge(k.s("ssd_prev"), 5 * (g + 1))
            pe.wait_ge(k.s("ssd_pick"), 2 * (g + 1))
            pe.wait_ge(k.s("ssd_cb"), g + 1)
            pe.wait_ge(k.s("ssd_b_t"), g + 1)
        if r % 2 == 0:
            if h:
                pe.wait_ge(k.s("ssd_off"), h // 2)
            pe.matmul(k.ps[:, 7, 0:384], b.pick_pair[0:SSD_ROWS, 64 * r:64 * (r + 2)], b.cs3[0:SSD_ROWS, P:],
                      start=True, stop=True).then_inc(k.s("ssd_cs_spread"), 1)
        if h >= 2:
            pe.wait_ge(k.s("ssd_seg_exp"), h - 1)
        pick = b.pick[0:SSD_ROWS, r, :]
        bank = 5 + r % 2
        pe.matmul(k.ps[:, bank, :], pick, b.cs3[0:SSD_ROWS, :], start=True, stop=False)
        for c in range(NC):
            pe.matmul(k.ps[:, bank, chunk[c]], b.ncs3[0:SSD_ROWS, chunk[c]], b.pick[0:SSD_ROWS, r, :],
                      start=False, stop=False)
        for c in range(NC):
            mm = pe.matmul(k.ps[:, bank, chunk[c]], b.ident, b.mask, start=False, stop=c == NC - 1)
        mm.then_inc(k.s("ssd_seg"), 1)

    def out(g, r):
        h, rows = SSD_R * g + r, slice(64 * (r % 2), 64 * (r % 2) + 64)
        if r % 2 == 0:
            pe.wait_ge(k.s("ssd_ecs"), h // 2 + 1)
            for c in range(1, NC):
                mm = pe.matmul(k.ps[:, 7, chunk[c - 1]], b.prev[:, c - 1, 64 * r:64 * (r + 2)],
                               b.bc[:, g % 2, 1, chunk[c]], start=True, stop=True)
            mm.then_inc(k.s("ssd_carried"), 1)
            if h:
                pe.wait_ge(k.s("ssd_y"), h // 2)
        pe.wait_ge(k.s("ssd_m"), h + 1)
        if r == 0:
            pe.wait_ge(k.s("ssd_cb"), g + 1)
        cols = slice(64 * r, 64 * r + 64)
        for c in range(NC):
            mm = pe.matmul(k.ps[rows, 4, chunk[c]], b.xdt[:, c, cols], b.m[:, r % 2, chunk[c]],
                           start=True, stop=True)
        mm.then_inc(k.s("ssd_out"), 1)

    def norm(g, _):
        pe.wait_ge(k.s("ssd_sqsum"), SSD_TG * (g + 1))
        pe.wait_ge(k.s("ssd_off"), SSD_TG * (g + 1))
        pe.matmul(k.ps[:, 7, :], k.c("mean"), k.sqsum[:, :], start=True, stop=True
                  ).then_inc(k.s("ssd_norm_sum"), 1)

    do = {"dt": dt, "tile": tile_, "turn": turn, "states": states, "seg": seg, "out": out, "norm": norm,
          "decays": decays, "early": early}
    for what, g, i in ssd_events():
        if what in do:
            do[what](g, i)


def ssd_bank(k, g, i):
    return 2 * ((k.pair0["ssd_in"] + 1 + 5 * g + i // 2) % 2) + i % 2


def ssd_channel(g, i):
    return (SSD_T + g, SSD_T + SSD_G + g)[i] if i < 2 else SSD_TG * g + i - 2


def ssd_place(b, g, i):
    return b.bc[:, g % 2, i, :] if i < 2 else b.x[:, g % 2, i - 2, :]


def ssd_scalar(act, k):
    b = SsdBuffers(k)
    n0 = k.pair0["ssd_in"]
    act.dma_start(b.table, k.dram["ssd_table"][:, 0:2 * P + SSD_DT]).then_inc(k.s("ssd_table"), 16)
    act.dma_start(b.start, k.dram["ssd_table"][:, 2 * P + SSD_DT:]).then_inc(k.s("ssd_table"), 16)

    def dt(g, i):
        act.activation(b.ea, k.p("ssd_a_log")[0:SSD_ROWS], ACT.Exp).then_inc(k.s("ssd_ea"), 1)
        softplus_scalar(act, k, "ssd_softplus", b.size[0:SSD_ROWS], b.e[0:SSD_ROWS])

    def decays(g, part):
        if part == 0:
            return
        act.wait_ge(k.s("ssd_end_diff"), 1)
        ends = k.ps[:, 6, 0:P].rearrange("p (c h) -> p c h", h=SSD_DT)
        act.activation(b.dec, ends, ACT.Exp).then_inc(k.s("ssd_decays"), 1)
        act.activation(b.end_w, b.end_w, ACT.Exp).then_inc(k.s("ssd_decays"), 1)

    def conv(g, i):
        n = n0 + 1 + 5 * g + i // 2
        act.wait_ge(k.s("banks_free"), 4 + 2 * n + i % 2 + 1)
        if i < 6:
            ci = 6 * g + i
            ch = ssd_channel(g, i)
            place = ssd_place(b, g, i)
            act.activation(place, b.raw[:, i % 2, 3:], ACT.Identity, bias=k.p("ssd_conv_b", ch),
                           scale=k.p("ssd_conv_w", 3 * 24 + ch)).then_inc(k.s("ssd_biased"), 1)
            act.wait_ge(k.s("ssd_tapped"), 3 * ci + 3)
            act.activation(place, place, ACT.Silu).then_inc(k.s("ssd_silu"), 1)
        else:
            act.activation(b.z[:, i - 6, :], b.z[:, i - 6, :], ACT.Silu).then_inc(k.s("ssd_z"), 1)

    def turn(g, _):
        act.wait_ge(k.s("ssd_turned_b"), g + 1)
        act.activation(b.b_t, k.ps[:, 7, 0:384], ACT.Copy
                       ).then_inc(k.s("ssd_b_t"), 1)
        act.wait_ge(k.s("ssd_cb_done"), g + 1)
        act.activation(b.cb, k.ps[:, 4, :], ACT.Copy).then_inc(k.s("ssd_cb"), 1)

    def seg(g, r):
        h = SSD_R * g + r
        if r % 2 == 0:
            act.wait_ge(k.s("ssd_cs_spread"), h // 2 + 1)
            if h:
                act.wait_ge(k.s("ssd_off"), h // 2)
            act.activation(b.ecs, k.ps[:, 7, 0:384], ACT.Exp).then_inc(k.s("ssd_ecs"), 1)
        act.wait_ge(k.s("ssd_seg"), h + 1)
        if h >= 2:
            act.wait_ge(k.s("ssd_out"), h - 1)
        act.activation(b.m[:, r % 2, :], k.ps[:, 5 + r % 2, :], ACT.Exp).then_inc(k.s("ssd_seg_exp"), 1)

    def out(g, r):
        if r % 2:
            t = SSD_TG * g + r // 2
            act.wait_ge(k.s("ssd_gated"), t + 1)
            if t >= 2:
                act.wait_ge(k.s("ssd_sqsum"), t - 1)
            act.activation(k.sq[:, t % 2, :], b.x[:, g % 2, r // 2, :], ACT.Square,
                           scale=mean_scale(SSD_TG * P)).then_inc(k.s("ssd_sq"), 1)

    def norm(g, _):
        act.wait_ge(k.s("ssd_norm_sum"), g + 1)
        inverse_root(act, k, k.factor[:, :], k.ps[:, 7, :], "ssd_rstd", g + 1)

    def finish(g, _):
        for t in range(SSD_TG):
            act.wait_ge(k.s("ssd_normed"), SSD_TG * g + t + 1)
            act.activation(k.gh[:, SSD_TG * g + t, :], b.x[:, g % 2, t, :], ACT.Copy
                           ).then_inc(k.s("ssd_y_hi"), 1)

    do = {"dt": dt, "conv": conv, "decays": decays, "turn": turn, "seg": seg, "out": out, "norm": norm,
          "finish": finish}
    for what, g, i in ssd_events():
        if what in do:
            do[what](g, i)


def ssd_vector(dve, k):
    b = SsdBuffers(k)
    job = "ssd_in"
    p0 = k.panel0[job]
    R = slice(0, SSD_ROWS)
    dve.memset(b.raw[:, :, 0:3], 0.0).then_inc(k.s("ssd_padded"), 1)
    dve.wait_ge(k.s("ssd_padded"), 1)
    norm_vector(dve, k, 2)

    def dt(g, i):
        dve.wait_ge(k.s("ssd_table"), 32)
        dve.tensor_copy(b.ident, k.c("ident")).then_inc(k.s("ssd_tables"), 1)
        dve.tensor_copy(b.mask, b.mask32).then_inc(k.s("ssd_tables"), 1)
        dve.tensor_copy(b.pick3, b.pick32).then_inc(k.s("ssd_tables"), 1)
        dve.wait_ge(k.s("panel_used"), p0 + 1)
        dve.tensor_tensor(b.dtx[R], k.ps[R, k.bank(job, 0), :], k.rstd[R], ALU.mult
                          ).then_inc(k.s("banks_free"), 2)
        dve.wait_ge(k.s("banks_free"), 4 + 2 * k.pair0[job] + 2)
        dve.tensor_scalar(b.dtx[R], b.dtx[R], k.p("ssd_dt_bias")[R], None, ALU.add
                          ).then_inc(k.s("ssd_dt_raw"), 1)
        dve.wait_ge(k.s("ssd_dt_raw"), 1)
        softplus_vector(dve, k, "ssd_softplus", b.dtx[R], b.size[R], b.e[R], b.q[R], b.dt[R])
        dve.wait_ge(k.s("ssd_ea"), 1)
        chain = Chain(dve, k, "ssd_chain")
        chain(dve.tensor_scalar(b.size[R], b.dt[R], b.ea, -1.0, ALU.mult, ALU.mult))
        chain(dve.tensor_tensor_scan(b.dtx[R], b.start[R], b.size[R], 0.0, ALU.mult, ALU.add))
        hi, mid = b.e[R].bitcast(BF16)[:, 0:S], b.e[R].bitcast(BF16)[:, S:2 * S]
        chain(dve.tensor_copy(hi, b.dtx[R]))
        chain(dve.tensor_tensor(b.q[R], b.dtx[R], hi, ALU.subtract))
        chain(dve.tensor_copy(mid, b.q[R]))
        chain(dve.tensor_copy(b.cs3[0:32], hi[0:32]))
        chain(dve.tensor_copy(b.cs3[32:64], mid[32:64]))
        chain(dve.tensor_tensor(b.cs3[64:96], b.q[64:96], mid[64:96], ALU.subtract))
        dve.tensor_scalar(b.ncs3[R], b.cs3[R], -1.0, None, ALU.mult).then_inc(k.s("ssd_cs"), 1)

    def decays(g, part):
        if part:
            dve.wait_ge(k.s("ssd_dt_t"), 2)
            dve.wait_ge(k.s("ssd_ends"), 1)
            dve.tensor_tensor(b.end_w.rearrange("p c h -> p (c h)"), k.ps[:, 6, 0:P],
                              b.cs_t.rearrange("p c h -> p (c h)"), ALU.subtract).then_inc(k.s("ssd_end_diff"), 1)
            return
        dve.wait_ge(k.s("ssd_turned_dt"), 1)
        dve.tensor_copy(b.cs_t.rearrange("p c h -> p (c h)"), k.ps[:, 5, 0:P]).then_inc(k.s("ssd_dt_t"), 1)
        dve.tensor_copy(b.dt_t.rearrange("p c h -> p (c h)"), k.ps[:, 5, P:2 * P]).then_inc(k.s("ssd_dt_t"), 1)

    def conv(g, i):
        if i % 2:
            dve.wait_ge(k.s("panel_used"), p0 + 1 + 5 * g + i // 2 + 1)
        else:
            dve.wait_ge(k.s("ssd_tile"), 5 * g + i // 2 + 1)
        place = b.raw[:, i % 2, 3:] if i < 6 else b.z[:, i - 6, :]
        if i < 6 and 6 * g + i >= 2:
            dve.wait_ge(k.s("ssd_tapped"), 3 * (6 * g + i - 1))
        if i >= 6 and g:
            dve.wait_ge(k.s("ssd_gated"), SSD_TG * g)
        dve.tensor_tensor(place, k.ps[:, ssd_bank(k, g, i), :], k.rstd[:, :], ALU.mult
                          ).then_inc(k.s("banks_free"), 1)
        if i >= 6:
            return
        ci, ch, place = 6 * g + i, ssd_channel(g, i), ssd_place(b, g, i)
        dve.wait_ge(k.s("ssd_biased"), ci + 1)
        for n, tap in enumerate((2, 1, 0)):
            if n:
                dve.wait_ge(k.s("ssd_tapped"), 3 * ci + n)
            dve.scalar_tensor_tensor(place, b.raw[:, i % 2, tap:tap + S], k.p("ssd_conv_w", tap * 24 + ch),
                                     place, ALU.mult, ALU.add).then_inc(k.s("ssd_tapped"), 1)

    def turn(g, _):
        if g == 0:
            dve.wait_ge(k.s("ssd_decays"), 2)
        if g:
            dve.wait_ge(k.s("ssd_xw"), 3 * g)
        for c in range(NC):
            dve.wait_ge(k.s("ssd_turned_x"), NC * g + c + 1)
            dve.tensor_tensor(by_head(b.xdt[:, c, :]), by_head(k.ps[:, 5 + c % 2, :]), heads_of(b.dt_t, c, g),
                              ALU.mult).then_inc(k.s("ssd_xdt"), 1)
        weigh(g, 0)
        weigh(g, 1)

    def weigh(g, c):
        dve.wait_ge(k.s("ssd_xdt"), NC * g + c + 1)
        dve.tensor_tensor(by_head(b.xw[:, c % 2, :]), by_head(b.xdt[:, c, :]), heads_of(b.end_w, c, g),
                          ALU.mult).then_inc(k.s("ssd_xw"), 1)

    def states(g, part):
        def decay(c):
            dve.wait_ge(k.s("ssd_prev"), 5 * g + 2 * c - 1)
            dve.tensor_tensor(by_head(b.prev[:, c, :]), by_head(b.prev[:, c - 1, :]), heads_of(b.dec, c, g),
                              ALU.mult).then_inc(k.s("ssd_prev"), 1)

        def carry(c):
            dve.wait_ge(k.s("ssd_prev"), 5 * g + 2 * c)
            dve.wait_ge(k.s("ssd_state"), 3 * g + c + 1)
            dve.tensor_tensor(b.prev[:, c, :], b.prev[:, c, :], k.ps[:, 5 + c % 2, :], ALU.add
                              ).then_inc(k.s("ssd_prev"), 1)

        if part == 0:
            dve.wait_ge(k.s("ssd_state"), 3 * g + 1)
            if g:
                dve.wait_ge(k.s("ssd_prev"), 5 * g)
            dve.tensor_copy(b.prev[:, 0, :], k.ps[:, 5, :]).then_inc(k.s("ssd_prev"), 1)
            weigh(g, 2)
            decay(1)
            carry(1)
            decay(2)
            dve.wait_ge(k.s("ssd_tables"), 3)
            dve.tensor_copy(b.pick_pair[R].rearrange("p (h d) -> p h d", d=64), b.pick3[R, SSD_R * g:SSD_R * (g + 1)]
                            .unsqueeze(2).to_broadcast([SSD_ROWS, SSD_R, 64])).then_inc(k.s("ssd_pick"), 1)
            dve.tensor_copy(b.pick[R], b.pick3[R, SSD_R * g:SSD_R * (g + 1)].unsqueeze(2)
                            .to_broadcast([SSD_ROWS, SSD_R, P])).then_inc(k.s("ssd_pick"), 1)
            return
        carry(2)

    def seg(g, r):
        h = SSD_R * g + r
        dve.wait_ge(k.s("ssd_seg_exp"), h + 1)
        if r == 0:
            dve.wait_ge(k.s("ssd_cb"), g + 1)
        dve.tensor_tensor(b.m[:, r % 2, :], b.m[:, r % 2, :], b.cb, ALU.mult).then_inc(k.s("ssd_m"), 1)

    def out(g, r):
        if r % 2 == 0:
            return
        t = r // 2
        n = SSD_TG * g + t
        place = b.x[:, g % 2, t, :]
        dve.wait_ge(k.s("ssd_carried"), n + 1)
        if n:
            dve.wait_ge(k.s("ssd_joined"), n)
        dve.tensor_tensor(b.off, k.ps[:, 7, 0:384], b.ecs, ALU.mult).then_inc(k.s("ssd_off"), 1)
        dve.wait_ge(k.s("ssd_out"), SSD_R * g + r + 1)
        dve.scalar_tensor_tensor(place, place, k.p("ssd_d", n), k.ps[:, 4, :], ALU.mult, ALU.add
                                 ).then_inc(k.s("ssd_y"), 1)
        dve.wait_ge(k.s("ssd_y"), n + 1)
        dve.wait_ge(k.s("ssd_off"), n + 1)
        dve.tensor_tensor(place[:, P:], place[:, P:], b.off, ALU.add).then_inc(k.s("ssd_joined"), 1)
        dve.wait_ge(k.s("ssd_joined"), n + 1)
        dve.wait_ge(k.s("ssd_z"), SSD_TG * (g + 1))
        dve.tensor_tensor(place, place, b.z[:, t, :], ALU.mult).then_inc(k.s("ssd_gated"), 1)
        dve.wait_ge(k.s("ssd_sq"), n + 1)
        if t == 0:
            if n:
                dve.wait_ge(k.s("ssd_sqsum"), n)
            dve.tensor_copy(k.sqsum[:, :], k.sq[:, n % 2, :]).then_inc(k.s("ssd_sqsum"), 1)
        else:
            dve.wait_ge(k.s("ssd_sqsum"), n)
            dve.tensor_tensor(k.sqsum[:, :], k.sqsum[:, :], k.sq[:, n % 2, :], ALU.add
                              ).then_inc(k.s("ssd_sqsum"), 1)

    def finish(g, _):
        dve.wait_ge(k.s("ssd_rstd"), g + 1)
        dve.wait_ge(k.s("ssd_gated"), SSD_TG * (g + 1))
        for t in range(SSD_TG):
            n = SSD_TG * g + t
            place = b.x[:, g % 2, t, :]
            dve.scalar_tensor_tensor(place, place, k.p("ssd_norm", n), k.factor[:, :], ALU.mult, ALU.mult
                                     ).then_inc(k.s("ssd_normed"), 1)
        for t in range(SSD_TG):
            n = SSD_TG * g + t
            dve.wait_ge(k.s("ssd_normed"), n + 1)
            dve.wait_ge(k.s("ssd_y_hi"), n + 1)
            dve.tensor_tensor(k.gl[:, n, :], b.x[:, g % 2, t, :], k.gh[:, n, :], ALU.subtract
                              ).then_inc(k.s("ssd_y_split"), 1)

    do = {"dt": dt, "conv": conv, "decays": decays, "turn": turn, "states": states, "seg": seg, "out": out,
          "finish": finish}
    for what, g, i in ssd_events():
        if what in do:
            do[what](g, i)



HG_HALVES = 8
HG_LEVEL_AT = 5
HG_TAIL_AT = HG_LEVEL_AT + 8
HG_TAIL = 6


class HgrnBuffers:
    def __init__(self, k):
        a = Arena(k)
        self.q, self.ks, self.qp = a.take(2, S), a.take(2, S), a.take(2, S)
        self.f = a.take(S)
        self.pd = [self.f] + [a.take(S >> n) for n in range(1, 8)]
        self.attn, self.i, self.g = a.take(2, S), a.take(2, S), a.take(2, S)
        self.i_t = a.take(NC, P)
        self.k_end = a.take(NC - 1, P)
        self.state = a.take(NC - 1, P)
        self.y = a.take(S)
        self.masks = a.take(len(LEVELS), P // 2, dt=I32)
        self.lb, self.one_lb, self.top = (a.take(HG_H) for _ in range(3))
        self.e = a.take(DEPTH, HG_H)


HG_EARLY_K = HG_H - 1
HG_EARLY = [(HG_H * HG_HALVES + n, n // 3, n % 3 * 2, n % 3 * 2 + 2) for n in range(9)]
HG_EARLY += [(HG_H * HG_HALVES + 10, 3, a, a + 2) for a in (0, 2, 4)]
HG_EARLY += [(HG_H * HG_HALVES + 10, o, 6, HG_EARLY_K) for o in range(4)]


def hgrn_events():
    ev = []
    for slot in range((HG_H - 1) * HG_HALVES + HG_TAIL_AT + HG_TAIL):
        h, half = divmod(slot, HG_HALVES)
        if h < HG_H:
            ev.append(("half", h, half))
        ev += [("early", i, 0) for i, part in enumerate(HG_EARLY) if part[0] == slot]
        h, level = divmod(slot - HG_LEVEL_AT, HG_HALVES)
        if 0 <= h < HG_H:
            ev.append(("level", h, level))
        h, t = divmod(slot - HG_TAIL_AT, HG_HALVES)
        if 0 <= h < HG_H and t < HG_TAIL:
            ev.append(("tail", h, t))
    return ev


def in_halves(t, B):
    return t.rearrange("p (n two b) -> p n two b", two=2, b=B)


def hgrn_tensor(pe, k):
    b = HgrnBuffers(k)
    job = "hgrn_in"
    p0, n0 = k.panel0[job], k.pair0[job]
    chunk = [slice(c * P, (c + 1) * P) for c in range(NC)]

    def half(h, i):
        n, second, part = 2 * h + i // 4, i // 2 % 2, i % 2
        if i % 4 == 0:
            pe.wait_ge(k.s("panel_split"), p0 + n + 1)
            pe.wait_ge(k.s("banks_free"), 2 * (n0 + n) + 2)
        slot = k.slot(job, n)
        wh, wl = k.whi(slot), k.wl[:, slot, :]
        for q in range(4 * part, 4 * part + 4):
            if h == 0 and i < 2:
                pe.wait_ge(k.s("x_split"), DT * 6 + q + 1)
            a = q * 256 + P * second
            mm = product(pe, k.ps[:, k.bank(job, n) + second, :], wh[:, a:a + P], wl[:, a:a + P],
                         k.xh[:, q, :], k.xl[:, q, :], q == 0, q == DT - 1)
        if part:
            mm.then_inc(k.s("panel_used" if second else "hgrn_tile"), 1)
        if h == 0 and i == 1:
            norm_tensor(pe, k, 6)

    def early(i, _):
        _, o, k0, k1 = HG_EARLY[i]
        pe.wait_ge(k.s("hgrn_y_split"), k1)
        out_early(pe, k, "hgrn_out", HG_H, o, k0, k1)

    def level(h, n):
        if n == 0:
            pe.wait_ge(k.s("hgrn_gates"), 3 * h + 3)
        elif n >= 2:
            pe.wait_ge(k.s("hgrn_update"), 21 * h + 3 * (n - 1))
        done = 8 * h + n
        if done >= 2:
            pe.wait_ge(k.s("hgrn_attn"), done - 1)
        for c in range(NC):
            if n:
                out = k.ps[:, 5 + n % 2, c * P // 2:(c + 1) * P // 2]
                rhs = in_halves(b.qp[:, h % 2, chunk[c]], LEVELS[n - 1])[:, :, 1, :]
            else:
                out, rhs = k.ps[:, 5, chunk[c]], b.q[:, h % 2, chunk[c]]
            mm = pe.matmul(out, b.ks[:, h % 2, chunk[c]], rhs, start=True, stop=True)
        mm.then_inc(k.s("hgrn_level"), 1)

    def tail(h, t):
        if t == 0:
            pe.wait_ge(k.s("banks_free"), 4 + 2 * (n0 + 2 * h + 1) + 1)
            if h:
                pe.wait_ge(k.s("hgrn_rstd_log"), h)
            else:
                pe.wait_ge(k.s("rstd_log"), 7)
            for c in range(NC):
                mm = pe.transpose(k.ps[:, 4, chunk[c]], b.i[:, h % 2, chunk[c]], k.c("ident"))
            mm.then_inc(k.s("hgrn_turned_i"), 1)
        elif t == 1:
            pe.wait_ge(k.s("hgrn_i_t"), h + 1)
            pe.wait_ge(k.s("hgrn_update"), 21 * (h + 1))
            for c in range(NC - 1):
                mm = pe.transpose(k.ps[:, 4, chunk[c]], b.ks[:, h % 2, chunk[c]], k.c("ident"))
            mm.then_inc(k.s("hgrn_turned_k"), 1)
        elif t == 2:
            pe.wait_ge(k.s("hgrn_k_end"), h + 1)
            for c in range(NC - 1):
                mm = pe.matmul(k.ps[:, 4, chunk[c]], b.k_end[:, c, :], b.i_t[:, c, :], start=True, stop=True)
            mm.then_inc(k.s("hgrn_kv"), 1)
        elif t == 3:
            pe.wait_ge(k.s("hgrn_state"), 3 * (h + 1))
            pe.wait_ge(k.s("hgrn_attn"), 8 * (h + 1))
            if h:
                pe.wait_ge(k.s("hgrn_y"), 2 * h)
            for c in range(NC):
                mm = pe.matmul(k.ps[:, 7, chunk[c]], b.i_t[:, c, :], b.attn[:, h % 2, chunk[c]],
                               start=True, stop=c == 0)
                if c:
                    mm = pe.matmul(k.ps[:, 7, chunk[c]], b.state[:, c - 1, :], b.qp[:, h % 2, chunk[c]],
                                   start=False, stop=True)
            mm.then_inc(k.s("hgrn_o"), 1)
        elif t == 4:
            pe.wait_ge(k.s("hgrn_sq"), h + 1)
            pe.matmul(k.ps[:, 4, :], k.c("mean"), k.sq[:, h % 2, :], start=True, stop=True
                      ).then_inc(k.s("hgrn_sum"), 1)

    do = {"half": half, "level": level, "tail": tail, "early": early}
    for what, h, i in hgrn_events():
        do[what](h, i)


def hgrn_scalar(act, k):
    b = HgrnBuffers(k)
    n0 = k.pair0["hgrn_in"]
    act.dma_start(b.masks, k.dram["hgrn_masks"]).then_inc(k.s("hgrn_masks"), 16)
    act.wait_ge(k.s("hgrn_lb"), 4)
    act.activation(b.e, b.e, ACT.Exp).then_inc(k.s("hgrn_lb_exp"), 1)

    def half(h, i):
        freed = 4 + 2 * (n0 + 2 * h)
        if i == 3:
            act.wait_ge(k.s("banks_free"), freed + 2)
            act.activation(b.f, b.f, ACT.Sigmoid).then_inc(k.s("hgrn_sigmoid"), 1)
        elif i == 7:
            act.wait_ge(k.s("banks_free"), freed + 4)
            act.activation(b.g[:, h % 2, :], b.g[:, h % 2, :], ACT.Silu).then_inc(k.s("hgrn_silu"), 1)

    def tail(h, t):
        if t == 0:
            act.wait_ge(k.s("hgrn_turned_i"), h + 1)
            act.activation(b.i_t.rearrange("p c v -> p (c v)"), k.ps[:, 4, :], ACT.Copy
                           ).then_inc(k.s("hgrn_i_t"), 1)
        elif t == 1:
            act.wait_ge(k.s("hgrn_turned_k"), h + 1)
            act.activation(b.k_end.rearrange("p c v -> p (c v)"), k.ps[:, 4, 0:384], ACT.Copy
                           ).then_inc(k.s("hgrn_k_end"), 1)
        elif t == 3:
            act.wait_ge(k.s("hgrn_o"), h + 1)
            act.activation(k.sq[:, h % 2, :], k.ps[:, 7, :], ACT.Square, scale=mean_scale(P)).then_inc(k.s("hgrn_sq"), 1)
        elif t == 4:
            act.wait_ge(k.s("hgrn_sum"), h + 1)
            if h:
                act.wait_ge(k.s("hgrn_y"), 2 * h)
            inverse_root(act, k, k.factor[:, :], k.ps[:, 4, :], "hgrn_rstd", h + 1)
        elif t == 5:
            act.wait_ge(k.s("hgrn_y"), 2 * h + 2)
            act.activation(k.gh[:, h, :], b.y, ACT.Copy).then_inc(k.s("hgrn_y_hi"), 1)

    do = {"half": half, "tail": tail}
    for what, h, i in hgrn_events():
        if what in do:
            do[what](h, i)


def hgrn_vector(dve, k):
    b = HgrnBuffers(k)
    job = "hgrn_in"
    p0 = k.panel0[job]
    low0, n = PARAMS["hgrn_lower_bounds"]
    low = k.par[:, low0:low0 + n].rearrange("p (l h) -> p l h", l=DEPTH)
    chain = Chain(dve, k, "hgrn_lb")
    chain(dve.tensor_tensor(b.top, low[:, 0], low[:, 1], ALU.max))
    chain(dve.tensor_tensor(b.top, b.top, low[:, 2], ALU.max))
    chain(dve.tensor_tensor(b.top, b.top, low[:, 3], ALU.max))
    chain(dve.tensor_tensor(b.e, low, b.top.unsqueeze(1).to_broadcast([P, DEPTH, HG_H]), ALU.subtract))
    dve.wait_ge(k.s("hgrn_lb_exp"), 1)
    chain(dve.tensor_tensor(b.lb, b.e[:, 1], b.e[:, 2], ALU.add))
    chain(dve.tensor_tensor(b.lb, b.lb, b.e[:, 3], ALU.add))
    chain(dve.tensor_tensor(b.top, b.lb, b.e[:, 0], ALU.add))
    chain(dve.reciprocal(b.top, b.top))
    chain(dve.tensor_tensor(b.lb, b.lb, b.top, ALU.mult))
    chain(dve.tensor_scalar(b.one_lb, b.lb, -1.0, 1.0, ALU.mult, ALU.add))
    norm_vector(dve, k, 6)
    dve.wait_ge(k.s("hgrn_masks"), 16)

    def half(h, i):
        if i % 2 == 0:
            return
        n, which = 2 * h + i // 4, i // 2
        bank = k.bank(job, n) + which % 2
        dve.wait_ge(k.s("panel_used" if which % 2 else "hgrn_tile"), (p0 if which % 2 else 0) + n + 1)
        if which == 0:
            dve.scalar_tensor_tensor(b.q[:, h % 2, :], k.ps[:, bank, :], float(P) ** -0.5, k.rstd[:, :],
                                     ALU.mult, ALU.mult).then_inc(k.s("banks_free"), 1)
            return
        if which == 1 and h:
            dve.wait_ge(k.s("hgrn_update"), 21 * (h - 1) + 3)
        place = (b.q[:, 0, :], b.f, b.i[:, h % 2, :], b.g[:, h % 2, :])[which]
        dve.tensor_tensor(place, k.ps[:, bank, :], k.rstd[:, :], ALU.mult).then_inc(k.s("banks_free"), 1)
        if which == 1:
            dve.wait_ge(k.s("hgrn_sigmoid"), h + 1)
            dve.tensor_scalar(b.f, b.f, b.one_lb[:, h:h + 1], b.lb[:, h:h + 1], ALU.mult, ALU.add
                              ).then_inc(k.s("hgrn_gates"), 1)
            dve.wait_ge(k.s("hgrn_gates"), 3 * h + 1)
            dve.tensor_scalar(b.ks[:, h % 2, :], b.f, -1.0, 1.0, ALU.mult, ALU.add
                              ).then_inc(k.s("hgrn_gates"), 1)
            dve.tensor_tensor(b.qp[:, h % 2, :], b.q[:, h % 2, :], b.f, ALU.mult
                              ).then_inc(k.s("hgrn_gates"), 1)

    def level(h, n):
        if n:
            B = LEVELS[n - 1]
            blocks = S // (2 * B)
            pd = b.pd[n - 1].rearrange("p (n two) -> p n two", two=2)
            first, second = pd[:, :, 0], pd[:, :, 1]
            wide = [P, blocks, B]
            qp = in_halves(b.qp[:, h % 2, :], B)[:, :, 1, :]
            ks = in_halves(b.ks[:, h % 2, :], B)[:, :, 0, :]
            dve.wait_ge(k.s("hgrn_level"), 8 * h + n + 1)
            if n > 1:
                dve.wait_ge(k.s("hgrn_update"), 21 * h + 3 * (n - 1))
            else:
                dve.wait_ge(k.s("hgrn_gates"), 3 * h + 3)
            dve.tensor_tensor(b.pd[n], first, second, ALU.mult).then_inc(k.s("hgrn_update"), 1)
            dve.tensor_tensor(qp, qp, first.unsqueeze(2).to_broadcast(wide), ALU.mult
                              ).then_inc(k.s("hgrn_update"), 1)
            dve.tensor_tensor(ks, ks, second.unsqueeze(2).to_broadcast(wide), ALU.mult
                              ).then_inc(k.s("hgrn_update"), 1)
            dve.wait_ge(k.s("hgrn_attn"), 8 * h + n)
        else:
            dve.wait_ge(k.s("hgrn_level"), 8 * h + 1)
        attn = b.attn[:, h % 2, :].rearrange("p (c l) -> p c l", c=NC)
        if n:
            attn = attn.rearrange("p c (n two b) -> p c n two b", two=2, b=B)[:, :, :, 1, :]
            ps = k.ps[:, 5 + n % 2, 0:S // 2].rearrange("p (c n b) -> p c n b", c=NC, b=B)
            mask = b.masks[:, n - 1, :].rearrange("p (n b) -> p n b", b=B).unsqueeze(1)
            dve.copy_predicated(attn, mask.to_broadcast([P, NC, P // 2 // B, B]), ps
                                ).then_inc(k.s("hgrn_attn"), 1)
        else:
            ps = k.ps[:, 5, :].rearrange("p (c l) -> p c l", c=NC)
            ident = k.c("ident").unsqueeze(1).to_broadcast([P, NC, P])
            dve.tensor_tensor(attn, ps, ident, ALU.mult).then_inc(k.s("hgrn_attn"), 1)

    def tail(h, t):
        if t == 2:
            dve.wait_ge(k.s("hgrn_kv"), h + 1)
            if h:
                dve.wait_ge(k.s("hgrn_state"), 3 * h)
            dve.tensor_copy(b.state[:, 0, :], k.ps[:, 4, 0:P]).then_inc(k.s("hgrn_state"), 1)
            for c in (1, 2):
                dve.wait_ge(k.s("hgrn_state"), 3 * h + c)
                dve.scalar_tensor_tensor(b.state[:, c, :], b.state[:, c - 1, :], b.pd[7][:, c:c + 1],
                                         k.ps[:, 4, c * P:(c + 1) * P], ALU.mult, ALU.add
                                         ).then_inc(k.s("hgrn_state"), 1)
        elif t == 5:
            dve.wait_ge(k.s("hgrn_rstd"), h + 1)
            if h:
                dve.wait_ge(k.s("hgrn_y_split"), h)
            dve.scalar_tensor_tensor(b.y, k.ps[:, 7, :], k.p("hgrn_norm"), k.factor[:, :], ALU.mult, ALU.mult
                                     ).then_inc(k.s("hgrn_y"), 1)
            dve.wait_ge(k.s("hgrn_y"), 2 * h + 1)
            dve.wait_ge(k.s("hgrn_silu"), h + 1)
            dve.tensor_tensor(b.y, b.y, b.g[:, h % 2, :], ALU.mult).then_inc(k.s("hgrn_y"), 1)
            dve.wait_ge(k.s("hgrn_y_hi"), h + 1)
            dve.tensor_tensor(k.gl[:, h, :], b.y, k.gh[:, h, :], ALU.subtract
                              ).then_inc(k.s("hgrn_y_split"), 1)

    do = {"half": half, "level": level, "tail": tail}
    for what, h, i in hgrn_events():
        if what in do:
            do[what](h, i)



SWA_TILES = 12
ROT = 16
ROPE_THETA = 500000.0
SWA_TABLE = P + P + 3 * 256 + 2 * S


class SwaBuffers:
    def __init__(self, k):
        a = Arena(k)
        self.table = a.take(SWA_TABLE)
        t, at = self.table, 0
        self.half_mean, self.perm = t[:, 0:P], t[:, P:2 * P]
        self.mask = t[:, 2 * P:2 * P + 768]
        self.cos, self.sin = t[:, 1024:1024 + S], t[:, 1024 + S:1024 + 2 * S]
        self.raw = a.take(2, S)
        self.kt = a.take(2, S)
        self.vt = a.take(NC, 256)
        self.q = a.take(2, S)
        self.s = a.take(2, 2, 2, 256)
        self.pt = a.take(2, 2, 4 * P)
        self.xc, self.xs = a.take(S), a.take(S)
        self.mx, self.neg, self.sum, self.esink, self.inv = (a.take(2, 2, 2) for _ in range(5))


SWA_SCORE_AT = 12
SWA_EARLY = [(24, 0, 0, 2), (25, 0, 2, 4), (25, 1, 0, 2), (26, 1, 2, 4), (27, 0, 4, 5), (27, 1, 4, 5),
             (28, 0, 5, 6), (28, 1, 5, 6), (30, 0, 6, 7), (30, 1, 6, 7)]


def swa_events():
    ev = []
    for slot in range(SWA_SCORE_AT + 16 + 3):
        u = slot - SWA_SCORE_AT
        if 0 <= u - 1 < 16:
            ev.append(("scale", (u - 1) // 2, (u - 1) % 2))
        i, second = divmod(slot - 2, 2)
        if 0 <= i < SWA_TILES and second and i not in (2, 3):
            ev.append(("factor", i, 0))
        if slot < 2 * SWA_TILES:
            ev.append(("tile", slot // 2, slot % 2))
        ev += [("early", i, 0) for i, part in enumerate(SWA_EARLY) if part[0] == slot]
        if 0 <= u - 2 < 16:
            ev.append(("pv", (u - 2) // 2, u % 2))
        if 0 <= u < 16:
            ev.append(("score", u // 2, u % 2))
        if 0 <= u - 1 < 16:
            ev.append(("turn", (u - 1) // 2, (u - 1) % 2))
        if 0 <= i < SWA_TILES:
            if i in (2, 3):
                ev += [] if second else [("turn_v", i, 0)]
            else:
                ev.append(("rope" if second else "sum", i, 0))
    return ev


def normed_index(i):
    return i if i < 2 else i - 2


def swa_tensor(pe, k):
    b = SwaBuffers(k)
    job = "swa_in"
    p0, n0 = k.panel0[job], k.pair0[job]

    def tile_(i, part):
        n = i // 2
        if i % 2 == 0 and part == 0:
            pe.wait_ge(k.s("panel_split"), p0 + n + 1)
        if part == 0:
            pe.wait_ge(k.s("banks_free"), 2 * n0 + max(i, 1) + 3)
        half = DT // 2
        mm = gemm_tile(pe, k, 2 + i % 2, k.slot(job, n), DT, 256, P * (i % 2), k.xh, k.xl,
                       half * part, half * (part + 1), fresh=None if i else 4)
        if part:
            mm.then_inc(k.s("panel_used" if i % 2 else "swa_tile"), 1)
        if i == 0 and part:
            norm_tensor(pe, k, 4)

    def early(i, _):
        _, o, k0, k1 = SWA_EARLY[i]
        pe.wait_ge(k.s("swa_y_split"), k1)
        if i == 0:
            pe.wait_ge(k.s("banks_free"), 4 + 2 * n0 + SWA_TILES)
        out_early(pe, k, "swa_out", 8, o, k0, k1)

    def sum_(i, _):
        m = normed_index(i)
        pe.wait_ge(k.s("swa_sq"), m + 1)
        if m == 0:
            pe.wait_ge(k.s("swa_table"), 16)
        else:
            pe.wait_ge(k.s("swa_rotated"), 3 * m)
        pe.matmul(k.ps[:, 1, :], b.half_mean, k.sq[:, i % 2, :], start=True, stop=True
                  ).then_inc(k.s("swa_half_mean"), 1)

    def rope(i, _):
        m = normed_index(i)
        pe.wait_ge(k.s("swa_normed"), m + 1)
        pe.matmul(k.ps[:, 1, :], b.perm, b.raw[:, i % 2, :], start=True, stop=True
                  ).then_inc(k.s("swa_partner"), 1)

    def turn_v(i, _):
        pe.wait_ge(k.s("banks_free"), 4 + 2 * n0 + i + 1)
        if i == 3:
            pe.wait_ge(k.s("swa_v"), 1)
        for c in range(NC):
            mm = pe.transpose(k.ps[:, 7, c * P:(c + 1) * P], b.raw[:, i % 2, c * P:(c + 1) * P], k.c("ident"))
        mm.then_inc(k.s("swa_turned_v"), 1)

    def score(t, m):
        un = 2 * t + m
        pe.wait_ge(k.s("swa_rotated"), 3 * (2 + t) + 3)
        if un:
            pe.wait_ge(k.s("swa_masked"), 2 * un)
        for a in range(2):
            rows = slice(64 * a, 64 * a + 64)
            for blk in range(2):
                n = 2 * m + blk
                key = max(n - 1, 0) * P
                mm = pe.matmul(k.ps[:, 5 + a, blk * 256:(blk + 1) * 256], b.q[rows, t % 2, n * P:(n + 1) * P],
                               b.kt[rows, t // 4, key:key + 256], start=True, stop=True)
        mm.then_inc(k.s("swa_scored"), 1)

    def turn(t, m):
        un = 2 * t + m
        pe.wait_ge(k.s("swa_p"), 4 * (un + 1))
        if un:
            pe.wait_ge(k.s("swa_pt0"), un)
            pe.wait_ge(k.s("swa_pt1"), un)
        else:
            pe.wait_ge(k.s("swa_v"), 2)
            pe.wait_ge(k.s("rstd_log"), 5)
        for a in range(2):
            for blk in range(2):
                for kh in range(2):
                    at = (2 * blk + kh) * P
                    mm = pe.transpose(k.ps[:, (7, 4)[a], at:at + P], b.s[:, m, a, blk, kh * P:(kh + 1) * P],
                                      k.c("ident"))
            mm.then_inc(k.s(f"swa_turned{a}"), 1)

    def pv(t, m):
        un = 2 * t + m
        if m == 0 and t:
            pe.wait_ge(k.s("swa_y_split"), t)
        for a in range(2):
            pe.wait_ge(k.s(f"swa_pt{a}"), un + 1)
            head = 2 * (t // 4) + a
            for blk in range(2):
                n = 2 * m + blk
                for kh in range(2):
                    chunk = max(n - 1, 0) + kh
                    at = (2 * blk + kh) * P
                    mm = pe.matmul(k.ps[64 * a:64 * a + 64, 0, n * P:(n + 1) * P],
                                   b.vt[:, chunk, 64 * head:64 * head + 64], b.pt[:, m, a, at:at + P],
                                   start=kh == 0, stop=kh == 1)
        mm.then_inc(k.s("swa_pv"), 1)

    do = {"tile": tile_, "sum": sum_, "rope": rope, "turn_v": turn_v, "score": score, "turn": turn, "pv": pv,
          "early": early}
    for what, i, m in swa_events():
        if what in do:
            do[what](i, m)


def swa_scalar(act, k):
    b = SwaBuffers(k)
    n0 = k.pair0["swa_in"]
    act.dma_start(b.table, k.dram["swa_table"]).then_inc(k.s("swa_table"), 16)

    def tile_(i, part):
        if i in (2, 3) or not part:
            return
        act.wait_ge(k.s("banks_free"), 4 + 2 * n0 + i + 1)
        act.activation(k.sq[:, i % 2, :], b.raw[:, i % 2, :], ACT.Square).then_inc(k.s("swa_sq"), 1)

    def sum_(i, _):
        m = normed_index(i)
        act.wait_ge(k.s("swa_half_mean"), m + 1)
        if m:
            act.wait_ge(k.s("swa_normed"), m)
        inverse_root(act, k, k.factor[:, :], k.ps[:, 1, :], "swa_rstd", m + 1)

    def turn_v(i, _):
        act.wait_ge(k.s("swa_turned_v"), i - 1)
        v = b.vt[:, :, P * (i - 2):P * (i - 1)]
        act.activation(v, k.ps[:, 7, :].rearrange("p (c d) -> p c d", c=NC), ACT.Copy
                       ).then_inc(k.s("swa_v"), 1)

    def score(t, m):
        un = 2 * t + m
        act.wait_ge(k.s("swa_max"), 4 * (un + 1))
        for a in range(2):
            for blk in range(2):
                row = b.s[:, m, a, blk, :]
                act.activation(row, row, ACT.Exp, bias=b.neg[:, m, a, blk:blk + 1],
                               accum_out=b.sum[:, m, a, blk:blk + 1]).then_inc(k.s("swa_exp"), 1)
        act.activation(b.esink[:, m], b.esink[:, m], ACT.Exp).then_inc(k.s("swa_exp"), 1)

    def scale(t, m):
        un = 2 * t + m
        act.wait_ge(k.s("swa_inv"), 2 * (un + 1))
        for a in range(2):
            for blk in range(2):
                row = b.s[:, m, a, blk, :]
                act.activation(row, row, ACT.Copy, scale=b.inv[:, m, a, blk:blk + 1]
                               ).then_inc(k.s("swa_p"), 1)

    def turn(t, m):
        un = 2 * t + m
        act.wait_ge(k.s("swa_turned0"), un + 1)
        act.activation(b.pt[:, m, 0, :], k.ps[:, 7, :], ACT.Copy).then_inc(k.s("swa_pt0"), 1)

    def pv(t, m):
        if m:
            act.wait_ge(k.s("swa_pv"), 2 * t + 2)
            act.activation(k.gh[:, t, :], k.ps[:, 0, :], ACT.Copy).then_inc(k.s("swa_y_hi"), 1)

    do = {"tile": tile_, "sum": sum_, "turn_v": turn_v, "score": score, "scale": scale, "turn": turn, "pv": pv}
    for what, i, m in swa_events():
        if what in do:
            do[what](i, m)


def swa_vector(dve, k):
    b = SwaBuffers(k)
    job = "swa_in"
    p0, n0 = k.panel0[job], k.pair0[job]
    sink0 = PARAMS["swa_sinks"][0]
    norm_vector(dve, k, 4)
    dve.wait_ge(k.s("swa_table"), 16)

    def tile_(i, part):
        if not part:
            return
        dve.wait_ge(k.s("panel_used" if i % 2 else "swa_tile"), (p0 if i % 2 else 0) + i // 2 + 1)
        if i in (4, 5):
            dve.wait_ge(k.s("swa_turned_v"), i - 3)
        elif i >= 2:
            dve.wait_ge(k.s("swa_rotated"), 3 * normed_index(i - 2) + 3)
        dve.tensor_tensor(b.raw[:, i % 2, :], k.ps[:, 2 + i % 2, :], k.rstd[:, :], ALU.mult
                          ).then_inc(k.s("banks_free"), 1)

    def factor(i, _):
        m = normed_index(i)
        dve.wait_ge(k.s("swa_rstd"), m + 1)
        x = b.raw[:, i % 2, :]
        dve.scalar_tensor_tensor(x, x, k.p("swa_k_norm" if i < 2 else "swa_q_norm"), k.factor[:, :],
                                 ALU.mult, ALU.mult).then_inc(k.s("swa_normed"), 1)

    def rope(i, _):
        m = normed_index(i)
        dve.wait_ge(k.s("swa_normed"), m + 1)
        if m:
            dve.wait_ge(k.s("swa_rotated"), 3 * m)
        dve.tensor_tensor(b.xc, b.raw[:, i % 2, :], b.cos, ALU.mult).then_inc(k.s("swa_rotated"), 1)
        dve.wait_ge(k.s("swa_partner"), m + 1)
        dve.tensor_tensor(b.xs, k.ps[:, 1, :], b.sin, ALU.mult).then_inc(k.s("swa_rotated"), 1)
        dve.wait_ge(k.s("swa_rotated"), 3 * m + 2)
        place = b.kt[:, i, :] if i < 2 else b.q[:, i % 2, :]
        dve.tensor_tensor(place, b.xc, b.xs, ALU.add).then_inc(k.s("swa_rotated"), 1)

    def score(t, m):
        un = 2 * t + m
        dve.wait_ge(k.s("swa_scored"), un + 1)
        if un >= 2:
            dve.wait_ge(k.s("swa_turned1"), un - 1)
        for a in range(2):
            dve.scalar_tensor_tensor(b.s[:, m, a].rearrange("p b k -> p (b k)"), k.ps[:, 5 + a, :], 0.125,
                                     b.mask[:, 256 * m:256 * m + 512], ALU.mult, ALU.add
                                     ).then_inc(k.s("swa_masked"), 1)
        chain = 4 * un
        dve.wait_ge(k.s("swa_masked"), 2 * un + 2)
        dve.tensor_reduce(b.mx[:, m], b.s[:, m], AX.X, ALU.max).then_inc(k.s("swa_max"), 1)
        at = sink0 + 8 * (t // 4) + t % 4
        sinks = k.par[:, at:at + 5:4].unsqueeze(2).to_broadcast([P, 2, 2])
        dve.wait_ge(k.s("swa_max"), chain + 1)
        dve.tensor_tensor(b.mx[:, m], b.mx[:, m], sinks, ALU.max).then_inc(k.s("swa_max"), 1)
        dve.wait_ge(k.s("swa_max"), chain + 2)
        dve.tensor_scalar(b.neg[:, m], b.mx[:, m], -1.0, None, ALU.mult).then_inc(k.s("swa_max"), 1)
        dve.tensor_tensor(b.esink[:, m], sinks, b.mx[:, m], ALU.subtract).then_inc(k.s("swa_max"), 1)

    def scale(t, m):
        un = 2 * t + m
        dve.wait_ge(k.s("swa_exp"), 5 * (un + 1))
        dve.tensor_tensor(b.sum[:, m], b.sum[:, m], b.esink[:, m], ALU.add).then_inc(k.s("swa_inv"), 1)
        dve.wait_ge(k.s("swa_inv"), 2 * un + 1)
        dve.reciprocal(b.inv[:, m], b.sum[:, m]).then_inc(k.s("swa_inv"), 1)

    def turn(t, m):
        un = 2 * t + m
        dve.wait_ge(k.s("swa_turned1"), un + 1)
        dve.tensor_copy(b.pt[:, m, 1, :], k.ps[:, 4, :]).then_inc(k.s("swa_pt1"), 1)

    def pv(t, m):
        if m:
            dve.wait_ge(k.s("swa_y_hi"), t + 1)
            dve.tensor_tensor(k.gl[:, t, :], k.ps[:, 0, :], k.gh[:, t, :], ALU.subtract
                              ).then_inc(k.s("swa_y_split"), 1)

    do = {"tile": tile_, "factor": factor, "rope": rope, "score": score, "scale": scale, "turn": turn,
          "pv": pv}
    for what, i, m in swa_events():
        if what in do:
            do[what](i, m)


MIX_TENSOR = (lru_tensor, ssd_tensor, swa_tensor, hgrn_tensor)
MIX_SCALAR = (lru_scalar, ssd_scalar, swa_scalar, hgrn_scalar)
MIX_VECTOR = (lru_vector, ssd_vector, swa_vector, hgrn_vector)
OUT_IN = ((LRU_T, 2, 7, "lru_y_split"), (SSD_T, SSD_EARLY, SSD_EARLY_K, "ssd_y_split"),
          (8, 2, 7, "swa_y_split"), (HG_H, 4, HG_EARLY_K, "hgrn_y_split"))



LAYERS = (0, 1, 2, 3)


def program(nc, dram, layers):
    names = set()
    for l in layers:
        names |= {f"up{l}", f"down{l}"} | {f"{MIXER[l]}_{x}" for x in ("in", "out")}
    with ExitStack() as ctx:
        k = Core(nc, ctx, dram, names)
        words = {name: w for name, _, w in JOBS}
        jobs = [name for name, _, _ in JOBS if name in names]
        block = ctx.enter_context(nc.Block())

        @block.sync
        def _(sp):
            n, half = PARAMS["ffn_norm"][0], words[jobs[0]] // 2
            sp.dma_start(k.par[:, 0:n], dram["params"][:, 0:n]).then_inc(k.s("gains_landed"), 16)
            sp.dma_start(k.w[:, 0, 0:half], dram[jobs[0]][0][:, 0:half]).then_inc(k.s("first_landed"), 16)
            for o in range(2):
                sp.dma_start(k.x[:, o, :], dram["x"][:, o, :]).then_inc(k.s(f"x{o}_landed"), 16)
            sp.dma_start(k.w[:, 0, half:2 * half], dram[jobs[0]][0][:, half:]).then_inc(k.s("panel_landed0"), 16)
            for o in range(2, DT):
                sp.dma_start(k.x[:, o, :], dram["x"][:, o, :]).then_inc(k.s(f"x{o}_landed"), 16)
            sp.dma_start(k.par[:, n:], dram["params"][:, n:]).then_inc(k.s("params_landed"), 16)
            sp.dma_start(k.con[:, :], dram["consts"]).then_inc(k.s("consts_landed"), 16)
            for job in jobs:
                weights_sync(sp, k, job, words[job])
            for o in range(DT):
                sp.wait_ge(k.s("banks_free"), 4 + 2 * (k.pair0[f"down{layers[-1]}"] + o + 1))
                sp.dma_start(dram["out"][:, o, :], k.x[:, o, :]).then_inc(k.s("out_stored"), 16)
            sp.wait_ge(k.s("out_stored"), 16 * DT)

        @block.gpsimd
        def _(pool):
            for job in jobs:
                weights_gpsimd(pool, k, job, words[job])

        @block.tensor
        def _(pe):
            for l in layers:
                MIX_TENSOR[l](pe, k)
                out_tensor(pe, k, f"{MIXER[l]}_out", *OUT_IN[l])
                up_tensor(pe, k, l)
                down_tensor(pe, k, l)

        @block.scalar
        def _(act):
            act.wait_ge(k.s("gains_landed"), 16)
            residual_scalar(act, k, 0, None)
            norm_scalar(act, k, 0)
            act.wait_ge(k.s("params_landed"), 16)
            for l in layers:
                MIX_SCALAR[l](act, k)
                residual_scalar(act, k, 2 * l + 1, f"{MIXER[l]}_out")
                norm_scalar(act, k, 2 * l + 1)
                up_scalar(act, k, l)
                if l != layers[-1]:
                    residual_scalar(act, k, 2 * l + 2, f"down{l}")
                    norm_scalar(act, k, 2 * l + 2)

        @block.vector
        def _(dve):
            dve.memset(k.rstd[:, :], 0.0).then_inc(k.s("banks_free"), 4)
            first_lo(dve, k, words[jobs[0]])
            dve.wait_ge(k.s("gains_landed"), 16)
            residual_vector(dve, k, 0, None)
            dve.wait_ge(k.s("consts_landed"), 16)
            dve.wait_ge(k.s("params_landed"), 16)
            for l in layers:
                MIX_VECTOR[l](dve, k)
                residual_vector(dve, k, 2 * l + 1, f"{MIXER[l]}_out")
                up_vector(dve, k, l)
                residual_vector(dve, k, 2 * l + 2 if l != layers[-1] else None, f"down{l}", True)


MIXER = ("lru", "ssd", "swa", "hgrn")


def panels(w, kt, groups):
    w = w.reshape(kt, P, -1)
    return np.stack([np.ascontiguousarray(w[:, :, g].transpose(1, 0, 2)).reshape(P, -1) for g in groups])


def span(*starts, width=P):
    return np.concatenate([np.arange(a, a + width) for a in starts])


def columns(v):
    return np.ascontiguousarray(np.asarray(v).reshape(-1, P).T)


def ssd_panels(w):
    x, B, C, dt = SSD_T * P, 2 * SSD_T * P, (2 * SSD_T + SSD_G) * P, (2 * SSD_T + 2 * SSD_G) * P
    first = panels(w, DT, [span(dt, dt, dt, width=SSD_DT)])
    first = np.pad(first, ((0, 0), (0, 0), (0, DT * 256 - first.shape[2])))
    groups = []
    for g in range(SSD_G):
        at = SSD_TG * P * g
        groups += [span(B + P * g, C + P * g)]
        groups += [span(x + at, width=2 * P), span(x + at + 2 * P, width=2 * P)]
        groups += [span(at, width=2 * P), span(at + 2 * P, width=2 * P)]
    return np.concatenate([first, panels(w, DT, groups)])


def swa_head_rows():
    return [span(64 * (8 * (t // 4) + t % 4), 64 * (8 * (t // 4) + t % 4 + 4), width=64) for t in range(8)]


def swa_table():
    i = np.arange(P)
    perm = np.zeros((P, P))
    for m in range(P):
        r = m % 64
        if r < ROT:
            perm[m + (8 if r < 8 else -8), m] = 1.0
    key = np.arange(256)
    later = (key > i[:, None]) & (key <= i[:, None] + P)
    masks = [np.where(ok, 0.0, -1e30) for ok in (key <= i[:, None], later, later)]
    freq = (np.float32(ROPE_THETA) ** (-np.arange(0, ROT, 2, dtype=np.float32) / np.float32(ROT))).astype(np.float32)
    angle = freq[:, None] * np.arange(S, dtype=np.float32)
    cos, sin = np.ones((P, S)), np.zeros((P, S))
    for m in range(P):
        r = m % 64
        if r < ROT:
            cos[m] = np.cos(angle[r % 8])
            sin[m] = np.sin(angle[r % 8]) * (-1.0 if r < 8 else 1.0)
    half = (i[:, None] // 64 == i // 64) / 64
    return np.concatenate([half, perm, *masks, cos, sin], axis=1).astype(np.float32)


def hgrn_masks():
    s, n = np.arange(P)[:, None], np.arange(P // 2)[None]
    m = [(s // (2 * B) == n // B) & (s // B % 2 == 0) for B in LEVELS]
    return np.stack(m, axis=1).astype(np.int32)


def layout(inputs):
    a = {n: np.asarray(v) for n, v in inputs.items()}
    out = {"x": a["x"][0].T.reshape(DT, P, S).transpose(1, 0, 2)}
    for l in range(DEPTH):
        out[f"up{l}"] = panels(a["ffn_w_up"][l], DT, [span(j * P, (FF_T + j) * P) for j in range(FF_T)])
        down = a["ffn_w_down"][l]
        half = FF_T // 2 * P
        parts = [panels(down[h * half:(h + 1) * half], FF_T // 2, [span(o * P) for o in range(DT)])
                 for h in range(2)]
        out[f"down{l}"] = np.stack(parts).reshape(2, DT // 2, 2, P, -1).transpose(1, 0, 2, 3, 4).reshape(2 * DT, P, -1)
    w = panels(a["lru_w_in"][0], DT, [span(j * P, (LRU_T + j) * P) for j in range(LRU_T)])
    out["lru_in"] = np.concatenate([w, a["lru_w_gate"][0]], axis=2)
    out["lru_out"] = panels(a["lru_w_out"][0], LRU_T, [span(o * P) for o in range(DT)])
    par = {
        "eps": np.full((P, 1), EPS, np.float32),
        "mix_norm": columns(a["mix_norm"]), "ffn_norm": columns(a["ffn_norm"]),
        "ffn_conv_w": columns(a["ffn_conv_w"]), "ffn_conv_b": columns(a["ffn_conv_b"]),
        "lru_conv_w": columns(a["lru_conv_w"]), "lru_conv_b": columns(a["lru_conv_b"]),
        "lru_b_gate": columns(a["lru_b_gate"][0].reshape(LRU_T, 2, P).transpose(1, 0, 2)),
        "lru_lambda": columns(a["lru_lambda"]),
        "ssd_conv_w": columns(a["ssd_conv_w"]), "ssd_conv_b": columns(a["ssd_conv_b"]),
        "ssd_dt_bias": np.tile(a["ssd_dt_bias"][0], 4)[:, None], "ssd_a_log": np.tile(a["ssd_a_log"][0], 4)[:, None],
        "ssd_d": columns(np.repeat(a["ssd_d"][0], 64)), "ssd_norm": columns(a["ssd_norm"]),
        "swa_q_norm": np.tile(a["swa_q_norm"][0], 2)[:, None], "swa_k_norm": np.tile(a["swa_k_norm"][0], 2)[:, None],
        "swa_sinks": np.tile(a["swa_sinks"][0], (P, 1)),
        "hgrn_norm": a["hgrn_norm"][0][:, None],
        "hgrn_lower_bounds": columns(a["hgrn_lower_bounds"]),
    }
    out["params"] = np.concatenate([par[n] for n in PARAMS], axis=1)
    i = np.arange(P)
    const = {"mean": np.full((P, P), 1 / D), "ident": np.eye(P)}
    out["swa_table"] = swa_table()
    out["hgrn_masks"] = hgrn_masks()
    q = swa_head_rows()
    groups = [span(D, width=256), span(D + 256, width=256)]
    groups += [np.concatenate(q[2 * n:2 * n + 2]) for n in range(4)]
    out["swa_in"] = panels(a["swa_w_in"][0], DT, groups)
    out["swa_out"] = panels(a["swa_w_out"][0][np.concatenate(q)], DT, [span(o * P) for o in range(DT)])
    groups = []
    for h in range(HG_H):
        groups += [span(h * P, D + h * P), span(2 * D + h * P, 3 * D + h * P)]
    out["hgrn_in"] = panels(a["hgrn_w_in"][0], DT, groups)
    out["hgrn_out"] = panels(a["hgrn_w_out"][0], DT, [span(o * P) for o in range(DT)])
    out["consts"] = np.concatenate([np.asarray(const[n], np.float32) for n in CONSTS], axis=1)
    out["ssd_in"] = ssd_panels(a["ssd_w_in"][0])
    out["ssd_out"] = panels(a["ssd_w_out"][0], SSD_T, [span(o * P) for o in range(DT)])
    out["ssd_table"] = np.concatenate([
        np.tile((i == P - 1)[:, None], (1, P)),
        np.where(i[:, None] <= i, 0.0, -1e30),
        i[:, None] % SSD_DT == np.arange(SSD_DT),
        np.tile(np.arange(S) % P != 0, (P, 1)),
    ], axis=1).astype(np.float32)
    return out



def kernel(**inputs):
    import concourse.bacc as bacc
    from concourse.bass_utils import run_bass_kernel_spmd as run

    nc = bacc.Bacc("TRN2", target_bir_lowering=False, num_devices=1)
    arrays = {n: np.ascontiguousarray(v) for n, v in layout(inputs).items()
              if n not in {x for x, _, _ in JOBS} or any(n in (f"up{l}", f"down{l}") or n.startswith(MIXER[l]) for l in LAYERS)}
    dram = {n: nc.dram_tensor(f"in_{n}", v.shape, mybir.dt.from_np(v.dtype), kind="ExternalInput").ap()
            for n, v in arrays.items()}
    dram["out"] = nc.dram_tensor("out_x", (P, DT, S), F32, kind="ExternalOutput").ap()
    program(nc, dram, LAYERS)
    r = run(nc, [{f"in_{n}": v for n, v in arrays.items()}], core_ids=[0])
    y = r.results[0]["out_x"]
    return np.ascontiguousarray(y.transpose(2, 1, 0).reshape(1, S, D))
```
